# Optimizing a Trainium2 kernel written in Bass

```python
import jax
import jax.numpy as jnp
from jax import lax
import numpy as np
import jax, jax.numpy as jnp

D_MODEL = 1024
BATCH = 1
SEQ = 512
DEPTH = 2

GRID_W = 64
CTX_LEN = 256
N_EVEN = (DEPTH + 1) // 2
N_ODD = DEPTH // 2
EPS = 1e-6
ROPE_BASE = 10000.0
CHUNK = 128
Q_BLOCK = 128

RET_HEADS = 8
RET_DK = 64
RET_DV = 64
RET_WIDTH = RET_HEADS * RET_DV
SSD_HEADS = 8
SSD_HEADDIM = 64
SSD_INNER = SSD_HEADS * SSD_HEADDIM
SSD_GROUPS = 2
SSD_STATE = 128
SSD_CONV = 5
CONV_CH = SSD_INNER + 2 * SSD_GROUPS * SSD_STATE
IN0_SPLITS = [RET_WIDTH, 2 * RET_WIDTH, 3 * RET_WIDTH, 4 * RET_WIDTH, 4 * RET_WIDTH + SSD_INNER, 4 * RET_WIDTH + SSD_INNER + CONV_CH]
IN0_WIDTH = 4 * RET_WIDTH + SSD_INNER + CONV_CH + 2 * SSD_HEADS
MIX0_WIDTH = RET_WIDTH + SSD_INNER
MLA_HEADS = 16
QK_NOPE = 64
QK_ROPE = 32
V_HEAD = 64
KV_RANK = 256
Q_RANK = 768
IN1_WIDTH = Q_RANK + KV_RANK + QK_ROPE
MLA_WIDTH = MLA_HEADS * V_HEAD
_FF_CEIL = -(-8 * D_MODEL // 3)
D_FF = -(-_FF_CEIL // 256) * 256


def rms_norm(x, w=None):
    xf = x.astype(jnp.float32)
    y = xf * lax.rsqrt(jnp.mean(xf * xf, axis=-1, keepdims=True) + EPS)
    if w is not None:
        y = y * w.astype(jnp.float32)
    return y.astype(x.dtype)

def adaln_params(cond, w_ada, b_ada):
    m = jax.nn.silu(cond) @ w_ada + b_ada
    return jnp.split(m[:, None, :], 6, axis=-1)

def modulate(h, shift, scale):
    return h * (1 + scale) + shift

def axial_rope_tables(n_tok, rot_dim):
    rows = n_tok // GRID_W
    row = jnp.repeat(jnp.arange(rows), GRID_W).astype(jnp.float32)
    col = jnp.tile(jnp.arange(GRID_W), rows).astype(jnp.float32)
    n_freq = rot_dim // 4
    inv_freq = ROPE_BASE ** (-jnp.arange(n_freq, dtype=jnp.float32) / n_freq)
    ang = jnp.concatenate([row[:, None] * inv_freq, col[:, None] * inv_freq], axis=-1)
    return jnp.cos(ang), jnp.sin(ang)

def apply_rope(x, cos, sin):
    half = x.shape[-1] // 2
    x1 = x[..., :half].astype(jnp.float32)
    x2 = x[..., half:].astype(jnp.float32)
    c = cos[:, None, :]
    s = sin[:, None, :]
    return jnp.concatenate([x1 * c - x2 * s, x1 * s + x2 * c], axis=-1).astype(x.dtype)

def bhld(t):
    return jnp.transpose(t, (0, 2, 1, 3))

def depthwise_conv_centred(x, w, b):
    k = w.shape[0]
    y = lax.conv_general_dilated(x, w[:, None, :].astype(x.dtype), window_strides=(1,), padding=[(k // 2, k // 2)],
                                 dimension_numbers=('NWC', 'WIO', 'NWC'), feature_group_count=x.shape[-1])
    return y + b

def chunked_decay_scan(q, k, v, log_a, s0):
    b, h, l, dk = q.shape
    dv = v.shape[-1]
    n = l // CHUNK
    qc = q.astype(jnp.float32).reshape(b, h, n, CHUNK, dk)
    kc = k.astype(jnp.float32).reshape(b, h, n, CHUNK, dk)
    vc = v.astype(jnp.float32).reshape(b, h, n, CHUNK, dv)
    cum = jnp.cumsum(log_a.astype(jnp.float32).reshape(b, h, n, CHUNK), axis=-1)
    idx = jnp.arange(CHUNK)
    lower = idx[:, None] >= idx[None, :]
    decay = jnp.exp(jnp.where(lower, cum[..., :, None] - cum[..., None, :], -jnp.inf))
    scores = jnp.einsum('bhnid,bhnjd->bhnij', qc, kc) * decay
    y_intra = jnp.einsum('bhnij,bhnjv->bhniv', scores, vc)
    to_end = jnp.exp(cum[..., -1:] - cum)
    kv_chunk = jnp.einsum('bhnjd,bhnj,bhnjv->bhndv', kc, to_end, vc)
    total = jnp.exp(cum[..., -1])

    def step(s, inp):
        kv_n, tot_n = inp
        return tot_n[..., None, None] * s + kv_n, s

    s_final, s_before = lax.scan(step, s0, (jnp.moveaxis(kv_chunk, 2, 0), jnp.moveaxis(total, 2, 0)))
    s_before = jnp.moveaxis(s_before, 0, 2)
    y_inter = jnp.einsum('bhnid,bhni,bhndv->bhniv', qc, jnp.exp(cum), s_before)
    return (y_intra + y_inter).reshape(b, h, l, dv), s_final

def bidir_prefix_scan(ctx_in, lat_in):
    qc, kc, vfc, vbc, lafc, labc = ctx_in
    ql, kl, vfl, vbl, lafl, labl = lat_in
    b, h, _, dk = qc.shape
    dv = vfc.shape[-1]
    s0 = jnp.zeros((b, h, dk, dv), jnp.float32)
    flip = lambda t: jnp.flip(t, axis=2)
    yc_f, sc_f = chunked_decay_scan(qc, kc, vfc, lafc, s0)
    yc_b, sc_b = chunked_decay_scan(flip(qc), flip(kc), flip(vbc), flip(labc), s0)
    yl_f, _ = chunked_decay_scan(ql, kl, vfl, lafl, sc_f)
    yl_b, _ = chunked_decay_scan(flip(ql), flip(kl), flip(vbl), flip(labl), sc_b)

    def merge(q, k, vb, yf, yb):
        diag = jnp.einsum('bhld,bhld->bhl', q.astype(jnp.float32), k.astype(jnp.float32))[..., None] * vb.astype(jnp.float32)
        return (yf + flip(yb) - diag).astype(vb.dtype)

    return merge(qc, kc, vbc, yc_f, yc_b), merge(ql, kl, vbl, yl_f, yl_b)

def ret_ssd_project(h, w_in, conv_w, conv_b, dt_bias, a_log, decay_logit, rope):
    b, l, _ = h.shape
    q, k, v, g, z, xbc, dt_raw = jnp.split(h @ w_in, IN0_SPLITS, axis=-1)
    q = q.reshape(b, l, RET_HEADS, RET_DK)
    k = k.reshape(b, l, RET_HEADS, RET_DK) * (RET_DK ** -0.5)
    if rope is not None:
        q = apply_rope(q, *rope)
        k = apply_rope(k, *rope)
    v = v.reshape(b, l, RET_HEADS, RET_DV)
    ret_la = jax.nn.log_sigmoid(decay_logit.astype(jnp.float32))
    la_r = [jnp.broadcast_to(ret_la[d][None, :, None], (b, RET_HEADS, l)) for d in range(2)]
    ret_in = (bhld(q), bhld(k), bhld(v), bhld(v), la_r[0], la_r[1])
    xbc = jax.nn.silu(depthwise_conv_centred(xbc, conv_w, conv_b))
    xs, bm, cm = jnp.split(xbc, [SSD_INNER, SSD_INNER + SSD_GROUPS * SSD_STATE], axis=-1)
    xs = xs.reshape(b, l, SSD_HEADS, SSD_HEADDIM)
    rep = SSD_HEADS // SSD_GROUPS
    bm = jnp.repeat(bm.reshape(b, l, SSD_GROUPS, SSD_STATE), rep, axis=2)
    cm = jnp.repeat(cm.reshape(b, l, SSD_GROUPS, SSD_STATE), rep, axis=2)
    dt = jax.nn.softplus(dt_raw.astype(jnp.float32).reshape(b, l, 2, SSD_HEADS) + dt_bias.astype(jnp.float32))
    log_a = dt * (-jnp.exp(a_log.astype(jnp.float32)))
    v_f = xs * dt[:, :, 0, :, None].astype(xs.dtype)
    v_b = xs * dt[:, :, 1, :, None].astype(xs.dtype)
    ssd_in = (bhld(cm), bhld(bm), bhld(v_f), bhld(v_b),
              jnp.transpose(log_a[:, :, 0], (0, 2, 1)), jnp.transpose(log_a[:, :, 1], (0, 2, 1)))
    return ret_in, ssd_in, g, z, xs

def retention_ssd_mixer(a_ctx, a_lat, w_in, conv_w, conv_b, dt_bias, a_log, d_skip, ssd_norm_w,
                        decay_logit, gn_w, w_out, rope, need_ctx):
    pc = ret_ssd_project(a_ctx, w_in, conv_w, conv_b, dt_bias, a_log, decay_logit, None)
    pl = ret_ssd_project(a_lat, w_in, conv_w, conv_b, dt_bias, a_log, decay_logit, rope)
    ret_c, ret_l = bidir_prefix_scan(pc[0], pl[0])
    ssd_c, ssd_l = bidir_prefix_scan(pc[1], pl[1])

    def finish(proj, y_ret, y_ssd):
        _, _, g, z, xs = proj
        b, l = g.shape[:2]
        yr = bhld(y_ret).astype(jnp.float32)
        mu = jnp.mean(yr, axis=-1, keepdims=True)
        var = jnp.mean(jnp.square(yr - mu), axis=-1, keepdims=True)
        yr = ((yr - mu) * lax.rsqrt(var + EPS)).reshape(b, l, RET_WIDTH) * gn_w.astype(jnp.float32)
        yr = yr.astype(g.dtype) * jax.nn.silu(g)
        ys = bhld(y_ssd) + d_skip[:, None] * xs
        ys = rms_norm(ys.reshape(b, l, SSD_INNER) * jax.nn.silu(z), ssd_norm_w)
        return jnp.concatenate([yr, ys], axis=-1) @ w_out

    out_l = finish(pl, ret_l, ssd_l)
    out_c = finish(pc, ret_c, ssd_c) if need_ctx else None
    return out_c, out_l

def mla_project(h, w_in, q_norm_w, w_uq, kv_norm_w, w_ukv, rope):
    b, l, _ = h.shape
    c_q, c_kv, k_pe = jnp.split(h @ w_in, [Q_RANK, Q_RANK + KV_RANK], axis=-1)
    q = (rms_norm(c_q, q_norm_w) @ w_uq).reshape(b, l, MLA_HEADS, QK_NOPE + QK_ROPE)
    q_nope, q_pe = jnp.split(q, [QK_NOPE], axis=-1)
    kv = (rms_norm(c_kv, kv_norm_w) @ w_ukv).reshape(b, l, MLA_HEADS, QK_NOPE + V_HEAD)
    k_nope, v = jnp.split(kv, [QK_NOPE], axis=-1)
    k_pe = k_pe[:, :, None, :]
    if rope is not None:
        q_pe = apply_rope(q_pe, *rope)
        k_pe = apply_rope(k_pe, *rope)
    q = jnp.concatenate([q_nope, q_pe], axis=-1)
    k = jnp.concatenate([k_nope, jnp.broadcast_to(k_pe, (b, l, MLA_HEADS, QK_ROPE))], axis=-1)
    return q, k, v

def softmax_attention(q, k, v):
    s = jnp.einsum('bqhd,bkhd->bhqk', q, k).astype(jnp.float32) * ((QK_NOPE + QK_ROPE) ** -0.5)
    p = jax.nn.softmax(s, axis=-1)
    return jnp.einsum('bhqk,bkhd->bqhd', p.astype(v.dtype), v)

def mla_mixer(a_ctx, a_lat, w_in, q_norm_w, w_uq, kv_norm_w, w_ukv, w_out, rope, need_ctx):
    q_c, k_c, v_c = mla_project(a_ctx, w_in, q_norm_w, w_uq, kv_norm_w, w_ukv, None)
    q_l, k_l, v_l = mla_project(a_lat, w_in, q_norm_w, w_uq, kv_norm_w, w_ukv, rope)
    k_all = jnp.concatenate([k_c, k_l], axis=1)
    v_all = jnp.concatenate([v_c, v_l], axis=1)
    b, l = a_lat.shape[:2]
    nb = l // Q_BLOCK
    q_blocks = jnp.moveaxis(q_l.reshape(b, nb, Q_BLOCK, MLA_HEADS, QK_NOPE + QK_ROPE), 1, 0)
    o_l = lax.map(lambda qb: softmax_attention(qb, k_all, v_all), q_blocks)
    out_l = jnp.moveaxis(o_l, 0, 1).reshape(b, l, MLA_WIDTH) @ w_out
    out_c = None
    if need_ctx:
        out_c = softmax_attention(q_c, k_c, v_c).reshape(b, a_ctx.shape[1], MLA_WIDTH) @ w_out
    return out_c, out_l

def swiglu(h, w_gate, w_up, w_down):
    return (jax.nn.silu(h @ w_gate) * (h @ w_up)) @ w_down

def first_inputs(seed: int = 0) -> dict:
    key = jax.random.key(seed)
    ks = iter(jax.random.split(key, 40))
    f32 = jnp.float32

    def normal(shape, scale=1.0):
        return scale * jax.random.normal(next(ks), shape, f32)

    def dense(shape):
        return normal(shape, shape[-2] ** -0.5)

    def gain(shape):
        return 1.0 + normal(shape, 0.02)

    gammas = 1.0 - 2.0 ** (-5.0 - np.arange(RET_HEADS))
    base_logit = jnp.asarray(np.log(gammas / (1.0 - gammas)), dtype=f32)
    dt0 = jnp.exp(jax.random.uniform(next(ks), (N_EVEN, 2, SSD_HEADS), f32, np.log(1e-3), np.log(1e-1)))
    return {
        'x': normal((BATCH, SEQ, D_MODEL)),
        'c': normal((BATCH, D_MODEL)),
        'ctx': normal((BATCH, CTX_LEN, D_MODEL)),
        'c_ctx': normal((D_MODEL,)),
        'w_ada': dense((DEPTH, D_MODEL, 6 * D_MODEL)),
        'b_ada': normal((DEPTH, 6 * D_MODEL), 0.02),
        'w_ffn_gate': dense((DEPTH, D_MODEL, D_FF)),
        'w_ffn_up': dense((DEPTH, D_MODEL, D_FF)),
        'w_ffn_down': dense((DEPTH, D_FF, D_MODEL)),
        'ret_ssd_w_in': dense((N_EVEN, D_MODEL, IN0_WIDTH)),
        'ssd_conv_w': dense((N_EVEN, SSD_CONV, CONV_CH)),
        'ssd_conv_b': normal((N_EVEN, CONV_CH), 0.02),
        'ssd_dt_bias': dt0 + jnp.log(-jnp.expm1(-dt0)),
        'ssd_a_log': jnp.log(jax.random.uniform(next(ks), (N_EVEN, 2, SSD_HEADS), f32, 1.0, 16.0)),
        'ssd_d': gain((N_EVEN, SSD_HEADS)),
        'ssd_norm_w': gain((N_EVEN, SSD_INNER)),
        'ret_decay_logit': base_logit + normal((N_EVEN, 2, RET_HEADS), 0.1),
        'ret_gn_w': gain((N_EVEN, RET_WIDTH)),
        'ret_ssd_w_out': dense((N_EVEN, MIX0_WIDTH, D_MODEL)),
        'mla_w_in': dense((N_ODD, D_MODEL, IN1_WIDTH)),
        'mla_q_norm_w': gain((N_ODD, Q_RANK)),
        'mla_w_uq': dense((N_ODD, Q_RANK, MLA_HEADS * (QK_NOPE + QK_ROPE))),
        'mla_kv_norm_w': gain((N_ODD, KV_RANK)),
        'mla_w_ukv': dense((N_ODD, KV_RANK, MLA_HEADS * (QK_NOPE + V_HEAD))),
        'mla_w_out': dense((N_ODD, MLA_WIDTH, D_MODEL)),
        'final_norm_w': gain((D_MODEL,)),
    }

def first_block(x, c, ctx, c_ctx, w_ada, b_ada, w_ffn_gate, w_ffn_up, w_ffn_down,
              ret_ssd_w_in, ssd_conv_w, ssd_conv_b, ssd_dt_bias, ssd_a_log, ssd_d, ssd_norm_w,
              ret_decay_logit, ret_gn_w, ret_ssd_w_out,
              mla_w_in, mla_q_norm_w, mla_w_uq, mla_kv_norm_w, mla_w_ukv, mla_w_out, final_norm_w):
    lat_len = x.shape[1]
    rope_ret = axial_rope_tables(lat_len, RET_DK)
    rope_mla = axial_rope_tables(lat_len, QK_ROPE)
    h_ctx, h_lat = ctx, x
    for i in range(DEPTH):
        last = i == DEPTH - 1
        j = i // 2
        m_lat = adaln_params(c, w_ada[i], b_ada[i])
        m_ctx = adaln_params(c_ctx[None], w_ada[i], b_ada[i])
        a_ctx = modulate(rms_norm(h_ctx), m_ctx[0], m_ctx[1])
        a_lat = modulate(rms_norm(h_lat), m_lat[0], m_lat[1])
        if i % 2 == 0:
            o_ctx, o_lat = retention_ssd_mixer(a_ctx, a_lat, ret_ssd_w_in[j], ssd_conv_w[j], ssd_conv_b[j],
                                               ssd_dt_bias[j], ssd_a_log[j], ssd_d[j], ssd_norm_w[j],
                                               ret_decay_logit[j], ret_gn_w[j], ret_ssd_w_out[j], rope_ret, not last)
        else:
            o_ctx, o_lat = mla_mixer(a_ctx, a_lat, mla_w_in[j], mla_q_norm_w[j], mla_w_uq[j], mla_kv_norm_w[j],
                                     mla_w_ukv[j], mla_w_out[j], rope_mla, not last)
        h_lat = h_lat + m_lat[2] * o_lat
        h_lat = h_lat + m_lat[5] * swiglu(modulate(rms_norm(h_lat), m_lat[3], m_lat[4]),
                                          w_ffn_gate[i], w_ffn_up[i], w_ffn_down[i])
        if not last:
            h_ctx = h_ctx + m_ctx[2] * o_ctx
            h_ctx = h_ctx + m_ctx[5] * swiglu(modulate(rms_norm(h_ctx), m_ctx[3], m_ctx[4]),
                                              w_ffn_gate[i], w_ffn_up[i], w_ffn_down[i])
    return rms_norm(h_lat, final_norm_w)


DEPTH_2 = 1

D_RWKV = 512
D_CONV = 512
RWKV_HEAD = 64
RWKV_HEADS = D_RWKV // RWKV_HEAD
CONV_WIDTH = 3
LORA_W = 64
LORA_A = 64
LORA_G = 128
N_EXPERTS = 16
EC_CAPACITY = 2
D_EXPERT = 1024
NORM_EPS = 1e-6
GN_EPS = 64e-5
RWKV_COLS = 3 * D_RWKV + LORA_W + LORA_A + LORA_G
CONV_COLS = 3 * D_CONV
D_IN = RWKV_COLS + CONV_COLS


def rmsnorm(x, g):
    xf = x.astype(jnp.float32)
    y = xf * lax.rsqrt(jnp.mean(xf * xf, axis=-1, keepdims=True) + NORM_EPS)
    return (y * g.astype(jnp.float32)).astype(x.dtype)

def modulate_2(h, shift, scale):
    return h * (1 + scale) + shift

def grid_shift(p, rows):
    b, t, ch = p.shape
    q = p.reshape(b, rows, GRID_W, ch // 4, 4)
    zc = jnp.zeros_like(q[:, :, :1, :, 0])
    zr = jnp.zeros_like(q[:, :1, :, :, 0])
    left = jnp.concatenate([zc, q[:, :, :-1, :, 0]], axis=2)
    right = jnp.concatenate([q[:, :, 1:, :, 1], zc], axis=2)
    up = jnp.concatenate([zr, q[:, :-1, :, :, 2]], axis=1)
    down = jnp.concatenate([q[:, 1:, :, :, 3], zr], axis=1)
    return jnp.stack([left, right, up, down], axis=-1).reshape(b, t, ch)

def seq_shift(p):
    b, t, ch = p.shape
    q = p.reshape(b, t, ch // 2, 2)
    z = jnp.zeros_like(q[:, :1, :, 0])
    prev = jnp.concatenate([z, q[:, :-1, :, 0]], axis=1)
    nxt = jnp.concatenate([q[:, 1:, :, 1], z], axis=1)
    return jnp.stack([prev, nxt], axis=-1).reshape(b, t, ch)

def split_rwkv(p, mu, shifted):
    p = p + mu * (shifted - p)
    o = 3 * D_RWKV
    return jnp.split(p, [D_RWKV, 2 * D_RWKV, o, o + LORA_W, o + LORA_W + LORA_A], axis=-1)

def wkv_scan(s0, r, w, k, v, a, b, reverse):
    def step(s, inp):
        r_t, w_t, k_t, v_t, a_t, b_t = inp
        sa = jnp.einsum('bhvk,bhk->bhv', s, a_t)
        s = s * w_t[:, :, None, :] + sa[..., :, None] * b_t[:, :, None, :] + v_t[..., :, None] * k_t[:, :, None, :]
        return s, jnp.einsum('bhvk,bhk->bhv', s, r_t)
    xs = tuple(jnp.moveaxis(z, 1, 0) for z in (r, w, k, v, a, b))
    s, y = lax.scan(step, s0, xs, reverse=reverse)
    return jnp.moveaxis(y, 0, 1), s

def rwkv_bidir(xr, xk, xv, xw, xa, w0, w_up, a0, a_up, k_k, k_a, s0_f, s0_b):
    bsz, t = xr.shape[0], xr.shape[1]
    f32 = jnp.float32
    heads = lambda z: z.astype(f32).reshape(bsz, t, RWKV_HEADS, RWKV_HEAD)
    per_head = lambda z: z.astype(f32).reshape(RWKV_HEADS, RWKV_HEAD)
    r, k, v = heads(xr), heads(xk), heads(xv)
    kk = k * per_head(k_k)
    kk = kk / jnp.maximum(jnp.sqrt(jnp.sum(kk * kk, axis=-1, keepdims=True)), 1e-12)
    tw = jnp.tanh(xw.astype(f32))
    xa = xa.astype(f32)
    k_a_h = per_head(k_a)
    y_sum, k_sum, states = 0.0, 0.0, []
    for d, (rev, s0) in enumerate(((False, s0_f), (True, s0_b))):
        wl = -jax.nn.softplus(-(w0[d].astype(f32) + tw @ w_up[d].astype(f32))) - 0.5
        decay = jnp.exp(-jnp.exp(heads(wl)))
        a = heads(jax.nn.sigmoid(a0[d].astype(f32) + xa @ a_up[d].astype(f32)))
        kd = k * (1 + (a - 1) * k_a_h)
        y, s = wkv_scan(s0, r, decay, kd, v, -kk, kk * a, rev)
        y_sum = y_sum + y
        k_sum = k_sum + kd
        states.append(s)
    return y_sum, states[0], states[1], r, k_sum, v

def rwkv_out(y, r, k_sum, v, xg, g_up, r_k, gn_g, gn_b):
    bsz, t = y.shape[0], y.shape[1]
    f32 = jnp.float32
    mu = jnp.mean(y, axis=-1, keepdims=True)
    var = jnp.mean(jnp.square(y - mu), axis=-1, keepdims=True)
    yn = ((y - mu) * lax.rsqrt(var + GN_EPS)).reshape(bsz, t, D_RWKV) * gn_g.astype(f32) + gn_b.astype(f32)
    bonus = (jnp.sum(r * k_sum * r_k.astype(f32), axis=-1, keepdims=True) * v).reshape(bsz, t, D_RWKV)
    g = jax.nn.sigmoid(xg.astype(f32)) @ g_up.astype(f32)
    return (yn + bonus) * g

def dwconv3(u, w):
    return lax.conv_general_dilated(u, w[:, None, :].astype(u.dtype), window_strides=(1,), padding=((1, 1),),
                                    dimension_numbers=('NWC', 'WIO', 'NWC'), feature_group_count=u.shape[-1])

def short_conv(p, conv_w):
    b_gate, c_gate, u = jnp.split(p, 3, axis=-1)
    return b_gate * dwconv3(c_gate * u, conv_w)

def expert_choice_ffn(h, router_w, w_gate, w_up, w_down):
    bsz, t, d = h.shape
    cap = EC_CAPACITY * t // N_EXPERTS
    aff = jax.nn.softmax((h @ router_w).astype(jnp.float32), axis=-1)
    vals, idx = lax.top_k(jnp.swapaxes(aff, 1, 2), cap)
    xs = jax.vmap(lambda hb, ib: hb[ib])(h, idx)
    hid = jax.nn.silu(jnp.einsum('becd,edf->becf', xs, w_gate)) * jnp.einsum('becd,edf->becf', xs, w_up)
    out = jnp.einsum('becf,efd->becd', hid, w_down) * vals[..., None].astype(h.dtype)
    return jax.vmap(lambda ob, ib: jnp.zeros((t, d), h.dtype).at[ib.reshape(-1)].add(ob.reshape(-1, d)))(out, idx)

def second_inputs(seed: int = 0) -> dict:
    key = jax.random.key(seed)
    ks = jax.random.split(key, 28)
    L = DEPTH_2
    nrm = lambda k, shape, scale: jax.random.normal(k, shape, jnp.float32) * scale
    return {
        'x': nrm(ks[0], (BATCH, SEQ, D_MODEL), 1.0),
        'c': nrm(ks[1], (BATCH, D_MODEL), 1.0),
        'ctx': nrm(ks[2], (BATCH, CTX_LEN, D_MODEL), 1.0),
        'c_ctx': nrm(ks[3], (D_MODEL,), 1.0),
        'ada_w': nrm(ks[4], (L, D_MODEL, 6 * D_MODEL), 0.5 * D_MODEL ** -0.5),
        'ada_b': nrm(ks[5], (L, 6 * D_MODEL), 0.02),
        'norm1_g': 1.0 + nrm(ks[6], (L, D_MODEL), 0.02),
        'norm2_g': 1.0 + nrm(ks[7], (L, D_MODEL), 0.02),
        'w_in': nrm(ks[8], (L, D_MODEL, D_IN), D_MODEL ** -0.5),
        'shift_mu': jax.random.uniform(ks[9], (L, RWKV_COLS), jnp.float32),
        'w0': jax.random.uniform(ks[10], (L, 2, D_RWKV), jnp.float32, minval=-6.0, maxval=1.0),
        'w_lora_up': nrm(ks[11], (L, 2, LORA_W, D_RWKV), 0.1 * LORA_W ** -0.5),
        'a0': nrm(ks[12], (L, 2, D_RWKV), 0.5),
        'a_lora_up': nrm(ks[13], (L, 2, LORA_A, D_RWKV), LORA_A ** -0.5),
        'k_k': 0.85 + nrm(ks[14], (L, D_RWKV), 0.05),
        'k_a': 1.0 + nrm(ks[15], (L, D_RWKV), 0.05),
        'r_k': nrm(ks[16], (L, RWKV_HEADS, RWKV_HEAD), 0.1),
        'g_lora_up': nrm(ks[17], (L, LORA_G, D_RWKV), LORA_G ** -0.5),
        'gn_g': 1.0 + nrm(ks[18], (L, D_RWKV), 0.02),
        'gn_b': nrm(ks[19], (L, D_RWKV), 0.02),
        'conv_w': nrm(ks[20], (L, CONV_WIDTH, D_CONV), CONV_WIDTH ** -0.5),
        'w_out': nrm(ks[21], (L, D_RWKV + D_CONV, D_MODEL), (D_RWKV + D_CONV) ** -0.5),
        'router_w': nrm(ks[22], (L, D_MODEL, N_EXPERTS), D_MODEL ** -0.5),
        'exp_w_gate': nrm(ks[23], (L, N_EXPERTS, D_MODEL, D_EXPERT), D_MODEL ** -0.5),
        'exp_w_up': nrm(ks[24], (L, N_EXPERTS, D_MODEL, D_EXPERT), D_MODEL ** -0.5),
        'exp_w_down': nrm(ks[25], (L, N_EXPERTS, D_EXPERT, D_MODEL), D_EXPERT ** -0.5),
        'final_g': 1.0 + nrm(ks[26], (D_MODEL,), 0.02),
    }

def second_block(x, c, ctx, c_ctx, ada_w, ada_b, norm1_g, norm2_g, w_in, shift_mu, w0, w_lora_up, a0, a_lora_up,
              k_k, k_a, r_k, g_lora_up, gn_g, gn_b, conv_w, w_out, router_w, exp_w_gate, exp_w_up, exp_w_down,
              final_g):
    bsz, t, _ = x.shape
    rows = t // GRID_W
    s_zero = jnp.zeros((bsz, RWKV_HEADS, RWKV_HEAD, RWKV_HEAD), jnp.float32)
    for l in range(DEPTH_2):
        last = l == DEPTH_2 - 1
        mod = jax.nn.silu(c) @ ada_w[l] + ada_b[l]
        mod_c = jax.nn.silu(c_ctx) @ ada_w[l] + ada_b[l]
        sh1, sc1, g1, sh2, sc2, g2 = jnp.split(mod[:, None, :], 6, axis=-1)
        csh1, csc1, cg1, csh2, csc2, cg2 = jnp.split(mod_c, 6, axis=-1)

        pc = modulate_2(rmsnorm(ctx, norm1_g[l]), csh1, csc1) @ w_in[l]
        px = modulate_2(rmsnorm(x, norm1_g[l]), sh1, sc1) @ w_in[l]
        pc_rw, pc_cv = pc[..., :RWKV_COLS], pc[..., RWKV_COLS:]
        px_rw, px_cv = px[..., :RWKV_COLS], px[..., RWKV_COLS:]

        cr, ck, cv, cw, ca, cgl = split_rwkv(pc_rw, shift_mu[l], seq_shift(pc_rw))
        xr, xk, xv, xw, xa, xgl = split_rwkv(px_rw, shift_mu[l], grid_shift(px_rw, rows))

        yc, sf, sb, rc, kc, vc = rwkv_bidir(cr, ck, cv, cw, ca, w0[l], w_lora_up[l], a0[l], a_lora_up[l],
                                            k_k[l], k_a[l], s_zero, s_zero)
        yx, _, _, rx, kx, vx = rwkv_bidir(xr, xk, xv, xw, xa, w0[l], w_lora_up[l], a0[l], a_lora_up[l],
                                          k_k[l], k_a[l], sf, sb)
        a_x = rwkv_out(yx, rx, kx, vx, xgl, g_lora_up[l], r_k[l], gn_g[l], gn_b[l]).astype(x.dtype)
        b_x = short_conv(px_cv, conv_w[l])
        x = x + g1 * (jnp.concatenate([a_x, b_x], axis=-1) @ w_out[l])
        if not last:
            a_c = rwkv_out(yc, rc, kc, vc, cgl, g_lora_up[l], r_k[l], gn_g[l], gn_b[l]).astype(ctx.dtype)
            b_c = short_conv(pc_cv, conv_w[l])
            ctx = ctx + cg1 * (jnp.concatenate([a_c, b_c], axis=-1) @ w_out[l])

        hx = modulate_2(rmsnorm(x, norm2_g[l]), sh2, sc2)
        x = x + g2 * expert_choice_ffn(hx, router_w[l], exp_w_gate[l], exp_w_up[l], exp_w_down[l])
        if not last:
            hc = modulate_2(rmsnorm(ctx, norm2_g[l]), csh2, csc2)
            ctx = ctx + cg2 * expert_choice_ffn(hc, router_w[l], exp_w_gate[l], exp_w_up[l], exp_w_down[l])
    return rmsnorm(x, final_g)


def setup_inputs(seed=0):
    out = dict(first_inputs(seed))
    for name, value in second_inputs(seed + 1).items():
        if name != "x":
            out[name + "_2"] = value
    return out


def reference(
    x, c, ctx, c_ctx, w_ada, b_ada, w_ffn_gate, w_ffn_up, w_ffn_down, ret_ssd_w_in, ssd_conv_w,
    ssd_conv_b, ssd_dt_bias, ssd_a_log, ssd_d, ssd_norm_w, ret_decay_logit, ret_gn_w,
    ret_ssd_w_out, mla_w_in, mla_q_norm_w, mla_w_uq, mla_kv_norm_w, mla_w_ukv, mla_w_out,
    final_norm_w, c_2, ctx_2, c_ctx_2, ada_w_2, ada_b_2, norm1_g_2, norm2_g_2, w_in_2,
    shift_mu_2, w0_2, w_lora_up_2, a0_2, a_lora_up_2, k_k_2, k_a_2, r_k_2, g_lora_up_2, gn_g_2,
    gn_b_2, conv_w_2, w_out_2, router_w_2, exp_w_gate_2, exp_w_up_2, exp_w_down_2, final_g_2,
):
    x = first_block(
        x, c, ctx, c_ctx, w_ada, b_ada, w_ffn_gate, w_ffn_up, w_ffn_down, ret_ssd_w_in,
        ssd_conv_w, ssd_conv_b, ssd_dt_bias, ssd_a_log, ssd_d, ssd_norm_w, ret_decay_logit,
        ret_gn_w, ret_ssd_w_out, mla_w_in, mla_q_norm_w, mla_w_uq, mla_kv_norm_w, mla_w_ukv,
        mla_w_out, final_norm_w,
    )
    return second_block(
        x, c_2, ctx_2, c_ctx_2, ada_w_2, ada_b_2, norm1_g_2, norm2_g_2, w_in_2, shift_mu_2,
        w0_2, w_lora_up_2, a0_2, a_lora_up_2, k_k_2, k_a_2, r_k_2, g_lora_up_2, gn_g_2, gn_b_2,
        conv_w_2, w_out_2, router_w_2, exp_w_gate_2, exp_w_up_2, exp_w_down_2, final_g_2,
    )


_drawn_inputs = setup_inputs


def setup_inputs(seed=0):
    import zlib

    import numpy as np

    out = dict(_drawn_inputs(seed))
    spreads = {}
    factors = {'ssd_conv_b': 4.94,
     'ssd_d': 8.0,
     'ssd_norm_w': 5.782,
     'ret_gn_w': 6.499,
     'mla_q_norm_w': 8.0,
     'mla_kv_norm_w': 8.0,
     'c_ctx_2': 12.06,
     'norm1_g_2': 5.057,
     'norm2_g_2': 27.133,
     'w_lora_up_2': 64.0,
     'k_k_2': 25.08,
     'k_a_2': 2.848,
     'gn_g_2': 64.0,
     'gn_b_2': 64.0,
     'final_g_2': 7.574,
     'ctx_2': 4.219}
    for name, (base, spread) in spreads.items():
        noise = np.random.default_rng([zlib.crc32(name.encode()), seed]).standard_normal(out[name].shape)
        drawn = base * np.exp(spread * noise) if base else spread * noise
        out[name] = jnp.asarray(drawn.astype(out[name].dtype))
    for name, factor in factors.items():
        out[name] = (out[name] * factor).astype(out[name].dtype)
    return out
```

```python
from contextlib import ExitStack

import numpy as np

import concourse.bass as bass
from concourse import mybir

F32 = mybir.dt.float32
ALU = mybir.AluOpType
ACT = mybir.ActivationFunctionType
AX = mybir.AxisListType

P = 128
D = 1024
KD = D // P
NC_, NL = 256, 512
T = NC_ + NL
TT = T // P
CTX, LAT, ALL = slice(0, NC_), slice(NC_, T), slice(0, T)
GRID_W = 64
EPS = 1e-6
GN_EPS = 64e-5
HEADS0 = 8
D_FF = 2816
KF = D_FF // P
XPAD = 2 + NC_ + 4 + NL + 2
CTX_AT, LAT_AT = 2, NC_ + 6
MLA_HEADS, NOPE, ROPE, VH = 16, 64, 32, 64
CHUNK = 64
N_STEPS = T // CHUNK
EXPERTS, CAP = 16, 64
RING, SLOT = 4, 2048


def columns(v):
    return np.ascontiguousarray(v, dtype=np.float32).reshape(-1, P).T


def spread(v):
    return np.broadcast_to(np.asarray(v).reshape(1, -1), (P, np.asarray(v).size))


def lay_params(x):
    at, cols, n = {}, [], 0
    pairs = {"cond1": ("c", "c_ctx"), "cond2": ("c_2", "c_ctx_2")}
    items = [(k, np.stack([columns(x[a].reshape(-1)), columns(x[b].reshape(-1))], -1).reshape(P, -1))
             for k, (a, b) in pairs.items()]
    items += [("b_ada0", columns(x["b_ada"][0])), ("b_ada1", columns(x["b_ada"][1])),
              ("b_ada2", columns(x["ada_b_2"][0]))]
    items += [("conv_w", np.concatenate([columns(x["ssd_conv_w"][0, j]) for j in range(5)], 1)),
              ("conv_b", columns(x["ssd_conv_b"][0])),
              ("ssd_norm", columns(x["ssd_norm_w"][0])), ("gn0", columns(x["ret_gn_w"][0])),
              ("ssd_d", columns(np.repeat(x["ssd_d"][0], 64))),
              ("dt_bias", spread(x["ssd_dt_bias"][0])), ("a_log", spread(x["ssd_a_log"][0])),
              ("decay_logit", spread(x["ret_decay_logit"][0])),
              ("q_norm", columns(x["mla_q_norm_w"][0])), ("kv_norm", columns(x["mla_kv_norm_w"][0])),
              ("final_norm", columns(x["final_norm_w"])),
              ("norm1_g", columns(x["norm1_g_2"][0])), ("norm2_g", columns(x["norm2_g_2"][0])),
              ("shift_mu", columns(x["shift_mu_2"][0])),
              ("w0", np.concatenate([columns(x["w0_2"][0, d]) for d in range(2)], 1)),
              ("a0", np.concatenate([columns(x["a0_2"][0, d]) for d in range(2)], 1)),
              ("k_k", columns(x["k_k_2"][0])), ("k_a", columns(x["k_a_2"][0])),
              ("r_k", columns(x["r_k_2"][0].reshape(-1))),
              ("gn_g", columns(x["gn_g_2"][0])), ("gn_b", columns(x["gn_b_2"][0])),
              ("conv3", np.concatenate([columns(x["conv_w_2"][0, j]) for j in range(3)], 1)),
              ("final_g", columns(x["final_g_2"]))]
    for name, a in items:
        at[name] = (n, a.shape[1])
        cols.append(a)
        n += a.shape[1]
    return np.ascontiguousarray(np.concatenate(cols, 1), dtype=np.float32), at


def constants():
    p = np.arange(P)[:, None]
    f = np.arange(P)[None, :]
    out = {}
    out["ident"] = (p == f)
    out["ones"] = np.ones((P, P))
    out["blk64"] = (p // 64 == f // 64)
    out["upto"] = (p <= f)
    out["before"] = (p < f)
    half = 32
    sw = np.zeros((P, P))
    for m in range(P):
        base, r = m // 64 * 64, m % 64
        if r < half:
            sw[base + r + half, m] = -1.0
        else:
            sw[base + r - half, m] = 1.0
    out["swap0"] = sw
    sw = np.zeros((P, 64))
    for b in (0, 32, 64, 96):
        for m in range(32):
            if m < 16:
                sw[b + m + 16, m] = -1.0
            else:
                sw[b + m - 16, m] = 1.0
    out["swap1"] = sw
    row = np.repeat(np.arange(NL // GRID_W), GRID_W).astype(np.float32)
    col = np.tile(np.arange(GRID_W), NL // GRID_W).astype(np.float32)
    for name, rot in (("0", 64), ("1", 32)):
        nf = rot // 4
        inv = (np.float32(10000.0) ** (-np.arange(nf, dtype=np.float32) / nf)).astype(np.float32)
        ang = np.concatenate([row[:, None] * inv, col[:, None] * inv], -1).astype(np.float32)
        which = np.arange(P) % (rot // 2)
        out["cos" + name] = np.cos(ang).T[which]
        out["sin" + name] = np.sin(ang).T[which]
    d1 = np.arange(896)[None, :] - 384 - p
    out["ahead"] = np.maximum(d1, 0)
    out["behind"] = np.maximum(-d1, 0)
    d2 = np.arange(640)[None, :] - 128 - p
    out["gap_f"] = d2 + NC_
    out["gap_b"] = NL - d2
    out["lower"] = (f >= p)
    out["upper"] = (f < p)
    for r in range(16):
        out[f"row{r}"] = np.broadcast_to(p == r, (P, P))
    q = p % 64
    g = np.arange(64)[None, :]
    fwd = [q < g, q <= g]
    bwd = [q > g, q >= g]
    out["pairs"] = np.concatenate([np.concatenate(fwd, 1), np.concatenate(bwd, 1)], 1)
    levels = []
    for size in (1, 2, 4, 8, 16, 32):
        same = (q // (2 * size) == g // (2 * size))
        low = same & (q // size % 2 == 0) & (g // size % 2 == 1)
        up = same & (q // size % 2 == 1) & (g // size % 2 == 0)
        levels += [low, up]
    out["levels"] = np.concatenate(levels, 1)
    out["eye64"] = (q == g)
    out["iota64"] = np.broadcast_to(g, (P, 64))
    out["restart"] = np.broadcast_to((np.arange(256)[None, :] % 64 != 0), (P, 256))
    out["restart_b"] = np.broadcast_to((np.arange(256)[None, :] % 64 != 63), (P, 256))
    out["mod4"] = (p % 4 == np.arange(4)[None, :])
    out["mod2"] = (p % 2 == np.arange(2)[None, :])
    small = np.zeros((P, 8))
    small[:, 0], small[:, 1], small[:, 2], small[:, 3] = EPS, GN_EPS, 1.0, 0.0
    small[:, 4], small[:, 5] = 1e-24, 10 * np.log(2.0)
    out["small"] = small
    at, cols, n = {}, [], 0
    for k, a in out.items():
        at[k] = (n, a.shape[1])
        cols.append(a.astype(np.float32))
        n += a.shape[1]
    return np.ascontiguousarray(np.concatenate(cols, 1), dtype=np.float32), at


class Stage:

    def __init__(self, prog, name):
        self.prog, self.name, self.kept, self.sems = prog, name, ExitStack(), []

    def __enter__(self):
        return self

    def sem(self, name):
        s = self.kept.enter_context(self.prog.nc.semaphore(f"{self.name}_{name}"))
        self.sems.append(s)
        return s

    def begin(self, pool):
        if self.prog.last_stage:
            for s in self.prog.last_stage.sems:
                pool.sem_clear(s)

    def __exit__(self, *_):
        if self.prog.last_stage:
            self.prog.last_stage.kept.close()
        self.prog.last_stage = self


class Chain:

    def __init__(self, engine, sem):
        self.engine, self.sem, self.n = engine, sem, 0

    def done(self, ins):
        self.n += 1
        ins.then_inc(self.sem, 1)
        return self.n

    def settle(self):
        self.engine.wait_ge(self.sem, self.n)

    def link(self, ins):
        self.done(ins)
        self.settle()


class Weights:

    def __init__(self):
        self.entries, self.before, self.freed, self.landed = [], [0], [], []
        self.issued, self.slot_count = 0, [0] * RING

    def add(self, parts, uses, also=0):
        n = len(self.entries)
        self.entries.append(parts)
        self.before.append(self.before[-1] + uses)
        self.freed.append(self.before[-1] + also)
        self.slot_count[n % RING] += 16 * len(parts)
        self.landed.append(self.slot_count[n % RING])

    def add_block(self, src, kt, cols, uses, also=0):
        self.add([(src, kt, cols, 0)], uses, also)

    def slot(self, n, kt=8, cols=256, at=0):
        return self.ring[:, n % RING, at:at + kt * cols].rearrange("p (k n) -> p k n", k=kt)

    def arrived(self, pe, n, more=0):
        pe.wait_ge(self.landed_sems[n % RING], self.landed[n] + more)

    def feed(self, sp, end):
        while self.issued < min(end + RING, len(self.entries)):
            n = self.issued
            if n >= RING:
                sp.wait_ge(self.product_done, self.freed[n - RING])
            for src, kt, cols, at in self.entries[n]:
                sp.dma_start(self.slot(n, kt, cols, at), src).then_inc(self.landed_sems[n % RING], 16)
            self.issued += 1


class Prog:
    def __init__(self, nc):
        self.nc, self.last_stage = nc, None
        self.w = Weights()


def k_major(ap, c0, c1, k0=0, k1=None):
    k1 = ap.shape[0] // P if k1 is None else k1
    return ap[k0 * P:k1 * P, c0:c1].rearrange("(k p) n -> p k n", p=P)


def plan_weights(g, A):
    w, first = g.w, {}

    def ada(name, ap):
        first[name] = len(w.entries)
        for e in range(24):
            w.add_block(k_major(ap, 256 * e, 256 * e + 256), 8, 256, 1)

    def ffn(name, l):
        first[name + "_up"] = len(w.entries)
        for e in range(11):
            w.add_block(k_major(A["w_ffn_gate"][l], 256 * e, 256 * e + 256), 8, 256, 0, 2)
            w.add_block(k_major(A["w_ffn_up"][l], 256 * e, 256 * e + 256), 8, 256, 2)
        first[name + "_down"] = len(w.entries)
        for m in range(8):
            for half in range(2):
                w.add_block(k_major(A["w_ffn_down"][l], P * m, P * m + P, 11 * half, 11 * half + 11), 11, P, half, 1 - half)

    def plain(name, ap, widths, uses):
        first[name] = len(w.entries)
        c = 0
        for width, u in zip(widths, uses):
            w.add_block(k_major(ap, c, c + width), ap.shape[0] // P, width, u)
            c += width

    ada("ada0", A["w_ada"][0])
    plain("in0", A["ret_ssd_w_in"][0], [256] * 14 + [16], [2] * 4 + [6, 6] + [2] * 8 + [6])
    plain("out0", A["ret_ssd_w_out"][0], [256] * 4, [2] * 4)
    ffn("ffn0", 0)
    ada("ada1", A["w_ada"][1])
    plain("in1", A["mla_w_in"][0], [256] * 4 + [32], [2] * 4 + [1])
    first["heads"] = len(w.entries)
    for h in range(MLA_HEADS):
        w.add([(k_major(A["mla_w_uq"][0], 96 * h, 96 * h + 96), 6, 96, 0),
               (k_major(A["mla_w_ukv"][0], 128 * h, 128 * h + 128), 2, 128, 576)], 1)
    plain("out1", A["mla_w_out"][0], [256] * 4, [2] * 4)
    ffn("ffn1", 1)
    ada("ada2", A["ada_w_2"][0])
    plain("in2", A["w_in_2"][0], [256] * 13, [2] * 13)
    plain("out2", A["w_out_2"][0], [256] * 4, [2] * 4)
    first["experts"] = len(w.entries)
    for e in range(EXPERTS):
        for half in range(2):
            for name in ("exp_w_gate_2", "exp_w_up_2"):
                for c in range(2):
                    lo = 512 * half + 256 * c
                    w.add_block(k_major(A[name][0, e], lo, lo + 256), 8, 256, 1)
        for c in range(4):
            w.add_block(k_major(A["exp_w_down_2"][0, e], 256 * c, 256 * c + 256), 8, 256, 1)
    return first


def vector_memory(g, A):
    nc, keep = g.nc, g.keep

    def sb(name, shape):
        return keep.enter_context(nc.sbuf_tensor(name, shape, F32))

    g.h = sb("h", [P, KD, T])
    g.params = sb("params", [P, A["params"].shape[1]])
    g.basic = sb("basic", [P, 2 * P + 8])
    g.ident, g.ones = g.basic[:, 0:P], g.basic[:, P:2 * P]
    g.eps, g.gn_eps = g.basic[:, 2 * P:2 * P + 1], g.basic[:, 2 * P + 1:2 * P + 2]
    g.one, g.tiny = g.basic[:, 2 * P + 2:2 * P + 3], g.basic[:, 2 * P + 4:2 * P + 5]
    g.zero = g.basic[:, 2 * P + 3:2 * P + 4]
    g.mod = sb("mod", [P, 6 * KD, 2])
    g.cond = sb("cond", [P, 2, KD, 2])
    g.w.ring = sb("weight_ring", [P, RING, SLOT])
    g.ps = keep.enter_context(nc.psum_tensor("ps", [P, 8, 512], F32))
    g.w.product_done = keep.enter_context(nc.semaphore("product_done"))
    g.w.landed_sems = [keep.enter_context(nc.semaphore(f"weights_landed{i}")) for i in range(RING)]
    g.out_stored = keep.enter_context(nc.semaphore("out_stored"))


def col(g, name, i=0, n=None):
    at, width = g.at[name]
    return g.params[:, at + i:at + (width if n is None else i + n)]


def load_const(g, eng, tile, name, sem, count=None):
    at, width = g.cat[name]
    eng.dma_start(tile, g.A["consts"][:, at:at + width]).then_inc(sem, 16)


def stage_start(g, A):
    with Stage(g, "start") as st:
        params_in, tokens_in = st.sem("params_in"), st.sem("tokens_in")
        with g.nc.Block() as block:
            @block.sync
            def _(sp):
                sp.dma_start(g.params[:, :], A["params"]).then_inc(params_in, 16)
                for name, lo, hi in (("ident", 0, P), ("ones", P, 2 * P), ("small", 2 * P, 2 * P + 8)):
                    load_const(g, sp, g.basic[:, lo:hi], name, params_in)
                sp.dma_start(g.h[:, :, LAT], A["xT"].rearrange("(k p) t -> p k t", p=P)).then_inc(tokens_in, 16)
                sp.dma_start(g.h[:, :, CTX], A["ctxT"].rearrange("(k p) t -> p k t", p=P)).then_inc(tokens_in, 16)
                g.w.feed(sp, 0)
                sp.wait_ge(tokens_in, 32)

            @block.scalar
            def _(act):
                act.wait_ge(params_in, 64)
                for b, name in enumerate(("cond1", "cond2")):
                    nc_out = g.cond[:, b].rearrange("p k w -> p (k w)")
                    act.activation(nc_out, col(g, name), ACT.Silu)


def stage_ada(g, name, bias, cond, gains=(None, None)):
    w, n0 = g.w, g.first[name]
    base = w.before[n0]
    TURN = 8
    with Stage(g, name) as st, ExitStack() as mem:
        rows = mem.enter_context(g.nc.sbuf_tensor(f"{name}_rows", [2, 256 * TURN], F32))
        mod_step, rows_ready, turned = st.sem("mod_step"), st.sem("rows_ready"), st.sem("turned")
        with g.nc.Block() as block:
            @block.sync
            def _(sp):
                w.feed(sp, n0 + 24)

            @block.tensor
            def _(pe):
                with pe.Fori(0, 24 // TURN) as i:
                    for e in range(TURN):
                        w.arrived(pe, n0 + e, i * (16 * TURN // RING))
                        for k in range(KD):
                            mm = pe.matmul(g.ps[0:2, e // 2, 256 * (e % 2):256 * (e % 2) + 256], g.cond[:, cond, k, :],
                                           w.slot(n0 + e)[:, k, :], start=(k == 0), stop=(k == KD - 1))
                        mm.then_inc(w.product_done, 1)
                    pe.wait_ge(rows_ready, i * 4 + 4)
                    for q in range(2 * TURN):
                        mm = pe.matmul(g.ps[:, 7, bass.ds(i * (4 * TURN) + 2 * q, 2)], rows[:, P * q:P * q + P], g.ident[0:2, 0:2],
                                       start=True, stop=True)
                    mm.then_inc(turned, 1)

            @block.scalar
            def _(act):
                with act.Fori(0, 24 // TURN) as i:
                    for b in range(4):
                        act.wait_ge(w.product_done, i * TURN + (base + 2 * b + 2))
                        act.activation(rows[:, 512 * b:512 * b + 512], g.ps[0:2, b, :], ACT.Copy).then_inc(rows_ready, 1)
                    act.wait_ge(turned, i + 1)

            @block.vector
            def _(dve):
                step = Chain(dve, mod_step)
                dve.wait_ge(turned, 24 // TURN)
                b = col(g, bias).unsqueeze(2).to_broadcast([P, 48, 2])
                step.link(dve.tensor_tensor(g.mod[:, :, :], g.ps[:, 7, 0:96].rearrange("p (m w) -> p m w", w=2), b, ALU.add))
                for j, gain in zip((1, 4), gains):
                    part = g.mod[:, j * KD:j * KD + KD, :]
                    step.done(dve.tensor_scalar(part, part, 1.0, None, ALU.add))
                step.settle()
                for j, gain in zip((1, 4), gains):
                    if gain is not None:
                        part = g.mod[:, j * KD:j * KD + KD, :]
                        step.done(dve.tensor_tensor(part, part, col(g, gain).unsqueeze(2).to_broadcast([P, KD, 2]), ALU.mult))

            @block.gpsimd
            def _(pool):
                st.begin(pool)


def norm_parts(g, j, both):
    parts = [(LAT, lambda k: g.mod[:, (j + 1) * KD + k, 0:1], lambda k: g.mod[:, j * KD + k, 0:1])]
    if both:
        parts.append((CTX, lambda k: g.mod[:, (j + 1) * KD + k, 1:2], lambda k: g.mod[:, j * KD + k, 1:2]))
    return parts


def stage_norm(g, name, src, dst, nk, parts, store=None):
    lo, hi = min(t.start for t, _, _ in parts), max(t.stop for t, _, _ in parts)
    shifted = parts[0][2] is not None
    with Stage(g, name) as st, ExitStack() as mem:
        sq = mem.enter_context(g.nc.sbuf_tensor(f"{name}_sq", [P, 2, T], F32))
        rs = mem.enter_context(g.nc.sbuf_tensor(f"{name}_rs", [P, T], F32))
        squared, summed = st.sem("squared"), st.sem("summed")
        root_step, scaled, ready = st.sem("root_step"), st.sem("scaled"), st.sem("ready")
        with g.nc.Block() as block:
            @block.scalar
            def _(act):
                for k in range(nk):
                    if k >= 2:
                        act.wait_ge(summed, k - 1)
                    act.activation(sq[:, k % 2, lo:hi], src[:, k, lo:hi], ACT.Square).then_inc(squared, 1)
                act.wait_ge(summed, nk)
                step = Chain(act, root_step)
                for b, (toks, _, _) in enumerate(parts):
                    n = toks.stop - toks.start
                    step.done(act.activation(rs[:, toks], g.ps[:, b, 0:n], ACT.Ln, bias=g.eps, scale=1.0 / (nk * P)))
                step.settle()
                step.done(act.activation(rs[:, lo:hi], rs[:, lo:hi], ACT.Exp, scale=-0.5))
                if shifted:
                    for k in range(nk):
                        for b, (toks, _, shift) in enumerate(parts):
                            act.wait_ge(scaled, len(parts) * k + b + 1)
                            act.activation(dst[:, k, toks], dst[:, k, toks], ACT.Identity, bias=shift(k)).then_inc(ready, 1)

            @block.tensor
            def _(pe):
                for k in range(nk):
                    pe.wait_ge(squared, k + 1)
                    for b, (toks, _, _) in enumerate(parts):
                        mm = pe.matmul(g.ps[:, b, 0:toks.stop - toks.start], g.ones, sq[:, k % 2, toks],
                                       start=(k == 0), stop=(k == nk - 1))
                    mm.then_inc(summed, 1)

            @block.vector
            def _(dve):
                dve.wait_ge(root_step, len(parts) + 1)
                for k in range(nk):
                    for toks, gain, _ in parts:
                        dve.scalar_tensor_tensor(dst[:, k, toks], src[:, k, toks], gain(k), rs[:, toks],
                                                 ALU.mult, ALU.mult).then_inc(scaled, 1)

            @block.gpsimd
            def _(pool):
                st.begin(pool)

            @block.sync
            def _(sp):
                if store is not None:
                    for k in range(nk):
                        sp.wait_ge(scaled, k + 1)
                        sp.dma_start(store[k * P:k * P + P, :], dst[:, k, parts[0][0]]).then_inc(g.out_stored, 16)
                    sp.wait_ge(g.out_stored, 16 * nk)


def stage_project(g, name, groups, end, extra=None):
    w = g.w
    base = w.before[groups[0][0]]
    turn = {"act": [0], "dve": [0]}
    for gr in groups:
        for e in turn:
            turn[e].append(turn[e][-1] + (gr[3] == e))
    with Stage(g, name) as st:
        read = {"act": st.sem("act_read"), "dve": st.sem("dve_read")}
        with g.nc.Block() as block:
            @block.sync
            def _(sp):
                w.feed(sp, end)

            @block.tensor
            def _(pe):
                last = None
                for j, (n, kt, outs, _, _) in enumerate(groups):
                    if n != last:
                        w.arrived(pe, n)
                        last = n
                    if j >= 4:
                        who = groups[j - 4][3]
                        pe.wait_ge(read[who], turn[who][j - 3])
                    for out, lhsT, rhs in outs(2 * (j % 4)):
                        for k in range(kt):
                            mm = pe.matmul(out, lhsT(k), rhs(k), start=(k == 0), stop=(k == kt - 1))
                    mm.then_inc(w.product_done, 1)

            def take(engine, who):
                for j, gr in enumerate(groups):
                    if gr[3] == who:
                        engine.wait_ge(w.product_done, base + j + 1)
                        gr[4](engine, 2 * (j % 4)).then_inc(read[who], 1)

            @block.scalar
            def _(act):
                take(act, "act")

            @block.vector
            def _(dve):
                take(dve, "dve")

            @block.gpsimd
            def _(pool):
                st.begin(pool)


def feature_group(g, n, kt, c0, src, both, who, evacuate, m=P, width=256):
    def outs(b):
        def lhsT(k):
            return g.w.slot(n, kt, width)[:, k, c0:c0 + m]
        made = [(g.ps[0:m, b, 0:NL], lhsT, lambda k: src[:, k, LAT])]
        if both:
            made.append((g.ps[0:m, b + 1, 0:NC_], lhsT, lambda k: src[:, k, CTX]))
        return made
    return (n, kt, outs, who, evacuate)


def token_group(g, n, kt, c0, width, slot_width, src, tile, who, evacuate):
    def outs(b):
        return [(g.ps[:, b, 0:width], lambda k: src[:, k, P * tile:P * tile + P],
                 lambda k: g.w.slot(n, kt, slot_width)[:, k, c0:c0 + width])]
    return (n, kt, outs, who, evacuate)


def copy_act(g, dst, both, func=ACT.Copy, scale=1.0, m=P):
    def go(act, b):
        for bank, toks in ((b, LAT), (b + 1, CTX))[:2 if both else 1]:
            ins = act.activation(dst(toks), g.ps[0:m, bank, 0:toks.stop - toks.start], func, scale=scale)
        return ins
    return go


def copy_dve(g, dst, both, scale=1.0, m=P):
    def go(dve, b):
        for bank, toks in ((b, LAT), (b + 1, CTX))[:2 if both else 1]:
            ins = dve.tensor_scalar(dst(toks), g.ps[0:m, bank, 0:toks.stop - toks.start], scale, None, ALU.mult)
        return ins
    return go


def add_gated(g, j, m, both):
    def go(dve, b):
        for bank, toks, wch in ((b, LAT, 0), (b + 1, CTX, 1))[:2 if both else 1]:
            hk = g.h[:, m, toks]
            ins = dve.scalar_tensor_tensor(hk, g.ps[:, bank, 0:toks.stop - toks.start],
                                           g.mod[:, j * KD + m, wch:wch + 1], hk, ALU.mult, ALU.add)
        return ins
    return go


def stage_out(g, name, src, both, j=2):
    n0 = g.first[name]
    groups = [feature_group(g, n0 + m // 2, KD, P * (m % 2), src, both, "dve", add_gated(g, j, m, both))
              for m in range(KD)]
    stage_project(g, name, groups, n0 + 4)


def stage_ffn(g, name, src, both):
    w = g.w
    ups, downs = g.first[name + "_up"], g.first[name + "_down"]
    parts = ((0, LAT, 0), (1, CTX, 1))[:2 if both else 1]
    with Stage(g, name) as st, ExitStack() as mem:
        hid = mem.enter_context(g.nc.sbuf_tensor(f"{name}_hid", [P, KF, T], F32))
        act_buf = mem.enter_context(g.nc.sbuf_tensor(f"{name}_silu", [P, 2, T], F32))
        silu_ready, hid_ready = st.sem("silu_ready"), st.sem("hid_ready")
        with g.nc.Block() as block:
            def up_pair(pe, n, more, lead):
                for q in range(2):
                    w.arrived(pe, n + q, more)
                for m in range(2):
                    if lead is not None:
                        pe.wait_ge(hid_ready, lead + m)
                    for q in range(2):
                        for b, toks, _ in parts:
                            for k in range(KD):
                                mm = pe.matmul(g.ps[:, 4 * m + 2 * q + b, 0:toks.stop - toks.start],
                                               w.slot(n + q)[:, k, P * m:P * m + P], src[:, k, toks],
                                               start=(k == 0), stop=(k == KD - 1))
                    mm.then_inc(w.product_done, 1)

            @block.sync
            def _(sp):
                w.feed(sp, downs + 16)

            @block.tensor
            def _(pe):
                up_pair(pe, ups, 0, None)
                with pe.Fori(0, 5) as i:
                    for r in range(2):
                        up_pair(pe, ups + 2 + 2 * r, i * 16, i * 4 + (2 * r + 1))
                pe.wait_ge(hid_ready, KF)
                with pe.Fori(0, 4) as i:
                    for r in range(2):
                        pe.wait_ge(hid_ready, i * 2 + (KF - 1 + r))
                        for half in range(2):
                            n = downs + 2 * r + half
                            w.arrived(pe, n, i * 16)
                            for b, toks, _ in parts:
                                for k in range(11):
                                    mm = pe.matmul(g.ps[:, 4 * r + b, 0:toks.stop - toks.start],
                                                   w.slot(n, 11, P)[:, k, :], hid[:, 11 * half + k, toks],
                                                   start=(half == 0 and k == 0), stop=(half == 1 and k == 10))
                        mm.then_inc(w.product_done, 1)

            @block.scalar
            def _(act):
                def silu(m, done, more):
                    act.wait_ge(w.product_done, done)
                    if more is not None:
                        act.wait_ge(hid_ready, more)
                    for b, toks, _ in parts:
                        ins = act.activation(act_buf[:, m, toks], g.ps[:, 4 * m + b, 0:toks.stop - toks.start], ACT.Silu)
                    ins.then_inc(silu_ready, 1)

                base = w.before[ups]
                for m in range(2):
                    silu(m, base + m + 1, None)
                with act.Fori(0, 5) as i:
                    for r in range(4):
                        silu(r % 2, i * 4 + (base + 3 + r), i * 4 + (1 + r))

            @block.vector
            def _(dve):
                def up(tile, m, more):
                    dve.wait_ge(silu_ready, more)
                    for b, toks, _ in parts:
                        n = toks.stop - toks.start
                        ins = dve.tensor_tensor(hid[:, tile, toks], act_buf[:, m, toks], g.ps[:, 4 * m + 2 + b, 0:n], ALU.mult)
                    ins.then_inc(hid_ready, 1)

                for m in range(2):
                    up(m, m, m + 1)
                flat = hid[:, :, :].rearrange("p k t -> p (k t)")
                with dve.Fori(0, 5) as i:
                    for r in range(4):
                        dve.wait_ge(silu_ready, i * 4 + (3 + r))
                        for b, toks, _ in parts:
                            n = toks.stop - toks.start
                            at = i * (4 * T) + ((2 + r) * T + toks.start)
                            ins = dve.tensor_tensor(flat[:, bass.ds(at, n)], act_buf[:, r % 2, toks],
                                                    g.ps[:, 4 * (r % 2) + 2 + b, 0:n], ALU.mult)
                        ins.then_inc(hid_ready, 1)
                base = w.before[downs]
                hf = g.h[:, :, :].rearrange("p k t -> p (k t)")
                mf = g.mod[:, :, :].rearrange("p m w -> p (m w)")
                with dve.Fori(0, 4) as i:
                    for r in range(2):
                        dve.wait_ge(w.product_done, i * 2 + (base + 1 + r))
                        for b, toks, wch in parts:
                            n = toks.stop - toks.start
                            hk = hf[:, bass.ds(i * (2 * T) + (r * T + toks.start), n)]
                            gate = mf[:, bass.ds(i * 4 + (2 * (5 * KD + r) + wch), 1)]
                            ins = dve.scalar_tensor_tensor(hk, g.ps[:, 4 * r + b, 0:n], gate, hk, ALU.mult, ALU.add)
                        ins.then_inc(hid_ready, 1)

            @block.gpsimd
            def _(pool):
                st.begin(pool)


def stage_in0(g, a, qk, gz, v, raw, dt_raw):
    n0 = g.first["in0"]
    groups = []
    for e in range(4):
        for m in range(2):
            tile = 2 * e + m
            scale = 1.0 if tile < 4 else 64 ** -0.5
            def dst(toks, tile=tile):
                return qk[:, tile, toks]
            make = copy_act if tile % 2 else copy_dve
            groups.append(feature_group(g, n0 + e, KD, P * m, a, True, "act" if tile % 2 else "dve", make(g, dst, True, scale=scale)))
    for e in range(2):
        for tile in range(TT):
            def take(dve, b, e=e, tile=tile):
                return dve.tensor_copy(v[:, tile, 256 * e:256 * e + 256], g.ps[:, b, 0:256])
            groups.append(token_group(g, n0 + 4 + e, KD, 0, 256, 256, a, tile, "dve", take))
    for e in range(4):
        for m in range(2):
            def dst(toks, tile=2 * e + m):
                return gz[:, tile, toks]
            groups.append(feature_group(g, n0 + 6 + e, KD, P * m, a, True, "act", copy_act(g, dst, True, func=ACT.Silu)))
    for e in range(4):
        for m in range(2):
            def dst(toks, tile=2 * e + m):
                at = LAT_AT if toks is LAT else CTX_AT
                return raw[:, tile, at:at + toks.stop - toks.start]
            groups.append(feature_group(g, n0 + 10 + e, KD, P * m, a, True, "dve" if m else "act",
                                        (copy_dve if m else copy_act)(g, dst, True)))
    for tile in range(TT):
        def take(dve, b, tile=tile):
            return dve.tensor_copy(dt_raw[:, tile, :], g.ps[:, b, 0:16])
        groups.append(token_group(g, n0 + 14, KD, 0, 16, 16, a, tile, "dve", take))
    stage_project(g, "in0", groups, n0 + 15)


def stage_rope0(g, qk):
    with Stage(g, "rope0") as st, ExitStack() as mem:
        swap = mem.enter_context(g.nc.sbuf_tensor("rope0_swap", [P, P], F32))
        cs = mem.enter_context(g.nc.sbuf_tensor("rope0_cs", [P, 2, NL], F32))
        t = mem.enter_context(g.nc.sbuf_tensor("rope0_t", [P, 2, NL], F32))
        tables_in, swapped, dve_step = st.sem("tables_in"), st.sem("swapped"), st.sem("dve_step")
        with g.nc.Block() as block:
            @block.sync
            def _(sp):
                load_const(g, sp, swap[:, :], "swap0", tables_in)
                load_const(g, sp, cs[:, 0, :], "cos0", tables_in)
                load_const(g, sp, cs[:, 1, :], "sin0", tables_in)

            @block.tensor
            def _(pe):
                pe.wait_ge(tables_in, 48)
                for m in range(8):
                    pe.matmul(g.ps[:, m, :], swap[:, :], qk[:, m, LAT], start=True, stop=True).then_inc(swapped, 1)

            @block.vector
            def _(dve):
                step = Chain(dve, dve_step)
                dve.wait_ge(tables_in, 48)
                for m in range(8):
                    dve.wait_ge(swapped, m + 1)
                    step.done(dve.tensor_tensor(t[:, 0, :], g.ps[:, m, :], cs[:, 1, :], ALU.mult))
                    step.link(dve.tensor_tensor(t[:, 1, :], qk[:, m, LAT], cs[:, 0, :], ALU.mult))
                    step.link(dve.tensor_tensor(qk[:, m, LAT], t[:, 0, :], t[:, 1, :], ALU.add))

            @block.gpsimd
            def _(pool):
                st.begin(pool)


def stage_conv0(g, raw, xbc):
    n = XPAD - 4
    with Stage(g, "conv0") as st, ExitStack() as mem:
        acc = mem.enter_context(g.nc.sbuf_tensor("conv0_acc", [P, 2, n], F32))
        tap, summed, taken = st.sem("tap"), st.sem("summed"), st.sem("taken")
        padded = st.sem("padded")
        with g.nc.Block() as block:
            @block.gpsimd
            def _(pool):
                st.begin(pool)
                for lo, hi in ((0, 2), (2 + NC_, LAT_AT), (LAT_AT + NL, XPAD)):
                    ins = pool.memset(raw[:, :, lo:hi], 0.0)
                ins.then_inc(padded, 1)

            @block.vector
            def _(dve):
                step = Chain(dve, tap)
                dve.wait_ge(padded, 1)
                for m in range(8):
                    if m >= 2:
                        dve.wait_ge(taken, m - 1)
                    step.link(dve.tensor_scalar(acc[:, m % 2, :], raw[:, m, 0:n], col(g, "conv_w", m, 1), None, ALU.mult))
                    for j in range(1, 4):
                        step.link(dve.scalar_tensor_tensor(acc[:, m % 2, :], raw[:, m, j:j + n], col(g, "conv_w", 8 * j + m, 1),
                                                           acc[:, m % 2, :], ALU.mult, ALU.add))
                    dve.scalar_tensor_tensor(acc[:, m % 2, :], raw[:, m, 4:4 + n], col(g, "conv_w", 32 + m, 1),
                                             acc[:, m % 2, :], ALU.mult, ALU.add).then_inc(summed, 1)

            @block.scalar
            def _(act):
                for m in range(8):
                    act.wait_ge(summed, m + 1)
                    for toks, at in ((CTX, CTX_AT - 2), (LAT, LAT_AT - 2)):
                        ins = act.activation(xbc[:, m, toks], acc[:, m % 2, at:at + toks.stop - toks.start], ACT.Silu,
                                             bias=col(g, "conv_b", m, 1))
                    ins.then_inc(taken, 1)


def stage_decays0(g, dt_raw, dt, cum, cumT, ret_la, xbc, xs_tok):
    with Stage(g, "decays0") as st, ExitStack() as mem:
        tmp = mem.enter_context(g.nc.sbuf_tensor("decays0_tmp", [P, 4, 112], F32))
        tri = mem.enter_context(g.nc.sbuf_tensor("decays0_tri", [P, 2, P], F32))
        tables_in, prepared, exped, logged = st.sem("tables_in"), st.sem("prepared"), st.sem("exped"), st.sem("logged")
        dve_step, act_step, la_ready, summed = st.sem("dve_step"), st.sem("act_step"), st.sem("la_ready"), st.sem("summed")
        cum_ready, rows_made, x_turned, x_taken = st.sem("cum_ready"), st.sem("rows_made"), st.sem("x_turned"), st.sem("x_taken")
        x, small, la = tmp[:, 0, :], tmp[:, 1, :], tmp[:, 3, :]
        neg_a = tmp[:, 2, 0:16]
        n = 16 * TT
        with g.nc.Block() as block:
            @block.sync
            def _(sp):
                load_const(g, sp, tri[:, 0, :], "upto", tables_in)
                load_const(g, sp, tri[:, 1, :], "before", tables_in)

            @block.gpsimd
            def _(pool):
                st.begin(pool)

            @block.vector
            def _(dve):
                step = Chain(dve, dve_step)
                bias = col(g, "dt_bias").unsqueeze(1).to_broadcast([P, TT, 16])
                step.done(dve.tensor_tensor(x[:, 0:n].rearrange("p (t h) -> p t h", h=16), dt_raw[:, :, :], bias, ALU.add))
                step.link(dve.tensor_scalar(x[:, n:n + 16], col(g, "decay_logit"), -1.0, None, ALU.mult))
                dve.scalar_tensor_tensor(small, x, -1.0, x, ALU.mult, ALU.max).then_inc(prepared, 1)
                dve.wait_ge(logged, 1)
                step.link(dve.scalar_tensor_tensor(x, x, 0.0, small, ALU.max, ALU.add))
                step.done(dve.tensor_copy(dt[:, :, :], x[:, 0:n].rearrange("p (t h) -> p t h", h=16)))
                step.done(dve.tensor_scalar(ret_la[:, 0:16], x[:, n:n + 16], -1.0, None, ALU.mult))
                step.done(dve.tensor_scalar(neg_a, neg_a, -1.0, None, ALU.mult))
                step.settle()
                dve.tensor_tensor(la[:, 0:n].rearrange("p (t h) -> p t h", h=16), dt[:, :, :],
                                  neg_a.unsqueeze(1).to_broadcast([P, TT, 16]), ALU.mult).then_inc(la_ready, 1)
                step.done(dve.tensor_scalar(ret_la[:, 16:24], ret_la[:, 8:16], -1.0, None, ALU.mult))
                step.done(dve.tensor_scalar(ret_la[:, 24:32], ret_la[:, 8:16], float(T), None, ALU.mult))
                dve.wait_ge(summed, 1)
                sums = g.ps[:, 7, 0:n].rearrange("p (t h) -> p t h", h=16)
                step.link(dve.tensor_copy(cum[:, 0], sums))
                dve.tensor_scalar(cum[:, 1], cum[:, 0], -1.0, None, ALU.mult).then_inc(cum_ready, 1)
                dve.wait_ge(rows_made, 1)
                dve.tensor_copy(cumT[:, LAT], g.ps[0:16, 5, 0:NL]).then_inc(dve_step, 1)
                dve.tensor_copy(cumT[:, CTX], g.ps[0:16, 6, 0:NC_]).then_inc(dve_step, 1)

            @block.scalar
            def _(act):
                step = Chain(act, act_step)
                step.done(act.activation(neg_a, col(g, "a_log"), ACT.Exp))
                act.wait_ge(prepared, 1)
                step.link(act.activation(small, small, ACT.Exp, scale=-1.0))
                act.activation(small, small, ACT.Ln, bias=g.one).then_inc(logged, 1)
                for tile in range(TT):
                    act.wait_ge(x_turned, tile + 1)
                    act.activation(xs_tok[:, tile, :], g.ps[:, tile % 2, :], ACT.Copy).then_inc(x_taken, 1)

            @block.tensor
            def _(pe):
                for tile in range(TT):
                    if tile >= 2:
                        pe.wait_ge(x_taken, tile - 1)
                    for m in range(4):
                        mm = pe.transpose(g.ps[:, tile % 2, P * m:P * m + P], xbc[:, m, P * tile:P * tile + P], g.ident)
                    mm.then_inc(x_turned, 1)
                pe.wait_ge(tables_in, 32)
                pe.wait_ge(la_ready, 1)
                for order, tiles, own in ((0, range(TT), 0), (8, (2, 3, 4, 5, 0, 1), 1)):
                    for at, tile in enumerate(tiles):
                        out = g.ps[:, 7, 16 * tile + order:16 * tile + order + 8]
                        for before in tiles[:at]:
                            pe.matmul(out, g.ones, la[:, 16 * before + order:16 * before + order + 8],
                                      start=(before == tiles[0]), stop=False)
                        mm = pe.matmul(out, tri[:, own, :], la[:, 16 * tile + order:16 * tile + order + 8],
                                       start=(at == 0), stop=True)
                mm.then_inc(summed, 1)
                pe.wait_ge(cum_ready, 1)
                for tile in range(TT):
                    bank, at = (6, P * tile) if tile < 2 else (5, P * (tile - 2))
                    mm = pe.transpose(g.ps[0:16, bank, at:at + P], cum[:, 0, tile, :], g.ident)
                mm.then_inc(rows_made, 1)


def score_tiles():
    out = []
    for jt in range(TT):
        out.append((jt, LAT))
        if jt < 2:
            out.append((jt, CTX))
    return out


def scan_pe(g, pe, heads, kq, values, sems, first_of_head=None):
    scores_ready, probs_ready, sums_ready, sums_read = sems
    tiles = score_tiles()
    blocks = [(hi, u) for hi in range(len(heads)) for u in range(len(tiles))]

    def scores(n):
        hi, u = blocks[n]
        jt, toks = tiles[u]
        if n >= 4:
            pe.wait_ge(probs_ready, n - 3)
        k, q = kq(heads[hi])
        pe.matmul(g.ps[:, n % 4, 0:toks.stop - toks.start], k(slice(P * jt, P * jt + P)), q(toks),
                  start=True, stop=True).then_inc(scores_ready, 1)

    for n in range(3):
        scores(n)
    for n, (hi, u) in enumerate(blocks):
        if n + 3 < len(blocks):
            scores(n + 3)
        if u == 0:
            if first_of_head:
                first_of_head(hi)
            if hi > 0:
                pe.wait_ge(sums_read, hi)
        jt, toks = tiles[u]
        h = heads[hi]
        p0 = 64 * (h % 2)
        bank = 4 if toks is LAT else 5
        pe.wait_ge(probs_ready, n + 1)
        mm = pe.matmul(g.ps[p0:p0 + 64, bank, 0:toks.stop - toks.start], values(h, jt),
                       g.probs[:, n % 4, 0:toks.stop - toks.start], start=(jt == 0), stop=(jt == (TT - 1 if toks is LAT else 1)))
        mm.then_inc(sums_ready, 1)


def take_sums(g, act, heads, y, sems):
    sums_ready, sums_read = sems
    n = len(score_tiles())
    for hi, h in enumerate(heads):
        yield hi
        act.wait_ge(sums_ready, n * (hi + 1))
        p0 = 64 * (h % 2)
        act.activation(y[p0:p0 + 64, h // 2, CTX], g.ps[p0:p0 + 64, 5, 0:NC_], ACT.Copy)
        act.activation(y[p0:p0 + 64, h // 2, LAT], g.ps[p0:p0 + 64, 4, 0:NL], ACT.Copy).then_inc(sums_read, 1)


def stage_retention(g, qk, v, ret_la):
    with Stage(g, "ret") as st, ExitStack() as mem:
        def sb(name, n):
            return mem.enter_context(g.nc.sbuf_tensor(f"ret_{name}", [P, n], F32))
        ahead, behind, gap = sb("ahead", 896), sb("behind", 896), sb("gap", 640)
        near = [sb(f"near{i}", 896) for i in range(2)]
        far = [sb(f"far{i}", 640) for i in range(2)]
        far_b = [sb(f"far_b{i}", 640) for i in range(2)]
        names = ("tables_in", "scores_ready", "probs_ready", "sums_ready", "sums_read",
                 "powers_ready", "near_ready", "far_ready", "dve_step")
        (tables_in, scores_ready, probs_ready, sums_ready, sums_read,
         powers_ready, near_ready, far_ready, dve_step) = (st.sem(n) for n in names)
        heads = list(range(HEADS0))
        tiles = score_tiles()
        nt = len(tiles)
        with g.nc.Block() as block:
            @block.sync
            def _(sp):
                load_const(g, sp, ahead[:, :], "ahead", tables_in)
                load_const(g, sp, behind[:, :], "behind", tables_in)
                load_const(g, sp, gap[:, :], "gap_f", tables_in)

            @block.gpsimd
            def _(pool):
                st.begin(pool)

            @block.tensor
            def _(pe):
                def kq(h):
                    p0, t = 64 * (h % 2), h // 2
                    return (lambda s: qk[p0:p0 + 64, 4 + t, s]), (lambda s: qk[p0:p0 + 64, t, s])
                scan_pe(g, pe, heads, kq, lambda h, jt: v[:, jt, 64 * h:64 * h + 64],
                        (scores_ready, probs_ready, sums_ready, sums_read))

            @block.scalar
            def _(act):
                def decays(h):
                    act.wait_ge(powers_ready, h + 1)
                    act.activation(near[h % 2][:, :], near[h % 2][:, :], ACT.Exp).then_inc(near_ready, 1)
                    act.activation(far[h % 2][:, :], gap[:, :], ACT.Exp, scale=ret_la[:, h:h + 1])
                    act.activation(far_b[h % 2][:, :], gap[:, :], ACT.Exp, scale=ret_la[:, 16 + h:17 + h],
                                   bias=ret_la[:, 24 + h:25 + h]).then_inc(far_ready, 1)
                decays(0)
                for hi in take_sums(g, act, heads, qk, (sums_ready, sums_read)):
                    if hi + 1 < HEADS0:
                        decays(hi + 1)

            @block.vector
            def _(dve):
                step = Chain(dve, dve_step)

                def powers(h):
                    step.link(dve.tensor_scalar(near[h % 2][:, :], behind[:, :], ret_la[:, 8 + h:9 + h], None, ALU.mult))
                    dve.scalar_tensor_tensor(near[h % 2][:, :], ahead[:, :], ret_la[:, h:h + 1], near[h % 2][:, :],
                                             ALU.mult, ALU.add).then_inc(powers_ready, 1)
                dve.wait_ge(tables_in, 48)
                powers(0)
                for h in range(HEADS0):
                    if h + 1 < HEADS0:
                        if h >= 1:
                            dve.wait_ge(probs_ready, nt * h)
                        powers(h + 1)
                    dve.wait_ge(near_ready, h + 1)
                    dve.wait_ge(far_ready, h + 1)
                    step.link(dve.tensor_tensor(far[h % 2][:, :], far[h % 2][:, :], far_b[h % 2][:, :], ALU.add))
                    for u, (jt, toks) in enumerate(tiles):
                        n = nt * h + u
                        dve.wait_ge(scores_ready, n + 1)
                        if n >= 4:
                            dve.wait_ge(sums_ready, n - 3)
                        width = toks.stop - toks.start
                        if jt < 2 and toks is LAT:
                            dec = far[h % 2][:, P - P * jt:P - P * jt + width]
                        else:
                            own = jt if jt < 2 else jt - 2
                            dec = near[h % 2][:, 384 - P * own:384 - P * own + width]
                        dve.tensor_tensor(g.probs[:, n % 4, 0:width], g.ps[:, n % 4, 0:width], dec, ALU.mult).then_inc(probs_ready, 1)


def stage_ssd(g, xbc, qk, dt, cum, cumT, xs_tok):
    with Stage(g, "ssd") as st, ExitStack() as mem:
        def sb(name, shape):
            return mem.enter_context(g.nc.sbuf_tensor(f"ssd_{name}", [P] + shape, F32))
        select = mem.enter_context(g.nc.sbuf_tensor("ssd_select", [16, 16, P], F32))
        tri = sb("tri", [2, P])
        rows = sb("rows", [2, T])
        diag = sb("diag", [TT, 2, P])
        wd = sb("wd", [TT, P])
        off = sb("off", [2, 2 * NL + P])
        wf = sb("wf", [2, NL])
        names = ("tables_in", "scores_ready", "probs_ready", "sums_ready", "sums_read",
                 "rows_made", "rows_read", "expo_ready", "diag_ready", "off_ready", "dve_step")
        (tables_in, scores_ready, probs_ready, sums_ready, sums_read, rows_made, rows_read,
         expo_ready, diag_ready, off_ready, dve_step) = (st.sem(n) for n in names)
        heads = list(range(HEADS0))
        tiles = score_tiles()
        nt = len(tiles)

        upto = [sum(1 for j, _ in tiles if j <= jt) for jt in range(TT)]

        with g.nc.Block() as block:
            @block.sync
            def _(sp):
                for r in range(16):
                    at, width = g.cat[f"row{r}"]
                    sp.dma_start(select[:, r, :], g.A["consts"][0:16, at:at + width]).then_inc(tables_in, 16)
                load_const(g, sp, tri[:, 0, :], "lower", tables_in)
                load_const(g, sp, tri[:, 1, :], "upper", tables_in)

            @block.gpsimd
            def _(pool):
                st.begin(pool)

            @block.tensor
            def _(pe):
                pe.wait_ge(tables_in, 16 * 18)

                def make_row(n):
                    if n > 0:
                        pe.wait_ge(rows_read, n)
                    r = 8 * (n % 2) + heads[n // 2]
                    pe.matmul(g.ps[:, 6, 0:NL], select[:, r, :], cumT[:, LAT], start=True, stop=True)
                    pe.matmul(g.ps[:, 7, 0:NC_], select[:, r, :], cumT[:, CTX], start=True, stop=True).then_inc(rows_made, 1)

                def next_rows(hi):
                    make_row(2 * hi + 1)
                    if hi + 1 < HEADS0:
                        make_row(2 * hi + 2)
                make_row(0)

                def kq(h):
                    grp = h // 4
                    return (lambda s: xbc[:, 4 + grp, s]), (lambda s: xbc[:, 6 + grp, s])
                scan_pe(g, pe, heads, kq, lambda h, jt: xs_tok[:, jt, 64 * h:64 * h + 64],
                        (scores_ready, probs_ready, sums_ready, sums_read),
                        first_of_head=next_rows)

            @block.scalar
            def _(act):
                def take_rows(h):
                    for d in range(2):
                        act.wait_ge(rows_made, 2 * h + d + 1)
                        if d == 0 and h > 0:
                            act.wait_ge(expo_ready, h)
                            act.wait_ge(off_ready, 6 * h)
                        sign = 1.0 - 2.0 * d
                        act.activation(rows[:, d, LAT], g.ps[:, 6, 0:NL], ACT.Copy, scale=sign)
                        ins = act.activation(rows[:, d, CTX], g.ps[:, 7, 0:NC_], ACT.Copy, scale=sign)
                        ins.then_inc(rows_read, 1)

                def offs(h, jt):
                    m = 6 * h + jt
                    if m >= 2:
                        hu, ju = (m - 2) // 6, (m - 2) % 6
                        act.wait_ge(probs_ready, nt * hu + upto[ju])
                    nc_j, e_j = cum[:, 1, jt, h:h + 1], cum[:, 0, jt, 8 + h:9 + h]
                    o = off[:, m % 2]
                    if jt < 2:
                        act.activation(o[:, 0:NL], rows[:, 0, LAT], ACT.Exp, bias=nc_j)
                        act.activation(o[:, NL:2 * NL], rows[:, 1, LAT], ACT.Exp, bias=e_j)
                        other = rows[:, 0, P:2 * P] if jt == 0 else rows[:, 1, 0:P]
                        last = act.activation(o[:, 2 * NL:], other, ACT.Exp, bias=nc_j if jt == 0 else e_j)
                    else:
                        lo, hi = P * (jt - 2), P * (jt - 1)
                        if hi < NL:
                            last = act.activation(o[:, hi:NL], rows[:, 0, NC_ + hi:T], ACT.Exp, bias=nc_j)
                        if lo > 0:
                            last = act.activation(o[:, 0:lo], rows[:, 1, NC_:NC_ + lo], ACT.Exp, bias=e_j)
                    last.then_inc(off_ready, 1)

                for h in range(HEADS0):
                    take_rows(h)
                    if h > 0:
                        act.wait_ge(sums_ready, nt * h)
                        hp = h - 1
                        p0 = 64 * (hp % 2)
                        act.activation(qk[p0:p0 + 64, 4 + hp // 2, CTX], g.ps[p0:p0 + 64, 5, 0:NC_], ACT.Copy)
                        act.activation(qk[p0:p0 + 64, 4 + hp // 2, LAT], g.ps[p0:p0 + 64, 4, 0:NL], ACT.Copy).then_inc(sums_read, 1)
                    act.wait_ge(expo_ready, h + 1)
                    act.activation(diag[:, :, :, :], diag[:, :, :, :], ACT.Exp).then_inc(diag_ready, 1)
                    for jt in range(TT):
                        offs(h, jt)
                act.wait_ge(sums_ready, nt * HEADS0)
                act.activation(qk[64:128, 7, CTX], g.ps[64:128, 5, 0:NC_], ACT.Copy)
                act.activation(qk[64:128, 7, LAT], g.ps[64:128, 4, 0:NL], ACT.Copy).then_inc(sums_read, 1)

            @block.vector
            def _(dve):
                step = Chain(dve, dve_step)
                dve.wait_ge(tables_in, 16 * 18)
                cross = step
                for h in range(HEADS0):
                    dve.wait_ge(rows_read, 2 * h + 2)
                    for jt in range(TT):
                        own = slice(P * jt, P * jt + P)
                        dve.tensor_scalar(diag[:, jt, 0, :], rows[:, 0, own], cum[:, 1, jt, h:h + 1], 0.0, ALU.add, ALU.min)
                        ins = dve.tensor_scalar(diag[:, jt, 1, :], rows[:, 1, own], cum[:, 0, jt, 8 + h:9 + h], 0.0, ALU.add, ALU.min)
                    ins.then_inc(expo_ready, 1)
                    dve.wait_ge(diag_ready, h + 1)
                    for jt in range(TT):
                        for d in range(2):
                            ins = dve.scalar_tensor_tensor(diag[:, jt, d, :], diag[:, jt, d, :], dt[:, jt, 8 * d + h:8 * d + h + 1],
                                                           tri[:, d, :], ALU.mult, ALU.mult)
                    step.link(ins)
                    step.link(dve.tensor_tensor(wd[:, :, :], diag[:, :, 0, :], diag[:, :, 1, :], ALU.add))
                    for u, (jt, toks) in enumerate(tiles):
                        n = nt * h + u
                        m = 6 * h + jt
                        o = off[:, m % 2]
                        dtf, dtb = dt[:, jt, h:h + 1], dt[:, jt, 8 + h:9 + h]
                        if toks is LAT:
                            dve.wait_ge(off_ready, m + 1)
                        dve.wait_ge(scores_ready, n + 1)
                        if n >= 4:
                            dve.wait_ge(sums_ready, n - 3)
                        prob, score = g.probs[:, n % 4], g.ps[:, n % 4]
                        if jt < 2 and toks is LAT:
                            step.link(dve.tensor_scalar(wf[:, 1, :], o[:, NL:2 * NL], dtb, None, ALU.mult))
                            step.link(dve.scalar_tensor_tensor(wf[:, 0, :], o[:, 0:NL], dtf, wf[:, 1, :], ALU.mult, ALU.add))
                            dve.tensor_tensor(prob[:, 0:NL], score[:, 0:NL], wf[:, 0, :], ALU.mult).then_inc(probs_ready, 1)
                            continue
                        own = P * (jt if jt < 2 else jt - 2)
                        if toks is CTX:
                            parts = [(P - own, o[:, 2 * NL:], dtf if jt == 0 else dtb, P)]
                        else:
                            parts = [(own + P, o[:, own + P:NL], dtf, NL - own - P), (0, o[:, 0:own], dtb, own)]
                        for c0, dec, scale, width in parts:
                            if width:
                                dve.scalar_tensor_tensor(prob[:, c0:c0 + width], dec, scale, score[:, c0:c0 + width], ALU.mult, ALU.mult)
                        dve.tensor_tensor(prob[:, own:own + P], score[:, own:own + P], wd[:, jt, :], ALU.mult).then_inc(probs_ready, 1)


def stage_finish0(g, qk, gz, xbc):
    with Stage(g, "finish0") as st, ExitStack() as mem:
        blk = mem.enter_context(g.nc.sbuf_tensor("finish0_blk", [P, P], F32))
        sq = mem.enter_context(g.nc.sbuf_tensor("finish0_sq", [P, 2, T], F32))
        rs = mem.enter_context(g.nc.sbuf_tensor("finish0_rs", [P, 2, T], F32))
        table_in, summed, centred, squared = st.sem("table_in"), st.sem("summed"), st.sem("centred"), st.sem("squared")
        squares_summed, rooted, act_step, dve_step = (st.sem("squares_summed"), st.sem("rooted"), st.sem("act_step"), st.sem("dve_step"))
        halves = ((0, LAT), (1, CTX))
        with g.nc.Block() as block:
            @block.sync
            def _(sp):
                load_const(g, sp, blk[:, :], "blk64", table_in)

            @block.gpsimd
            def _(pool):
                st.begin(pool)

            @block.tensor
            def _(pe):
                pe.wait_ge(table_in, 16)
                for m in range(4):
                    for b, toks in halves:
                        mm = pe.matmul(g.ps[:, 2 * (m % 2) + b, 0:toks.stop - toks.start], blk[:, :], qk[:, m, toks], start=True, stop=True)
                    mm.then_inc(summed, 1)
                    pe.wait_ge(squared, m + 1)
                    if m >= 2:
                        pe.wait_ge(rooted, m - 1)
                    for b, toks in halves:
                        mm = pe.matmul(g.ps[:, 4 + 2 * (m % 2) + b, 0:toks.stop - toks.start], blk[:, :], sq[:, m % 2, toks], start=True, stop=True)
                    mm.then_inc(squares_summed, 1)

            @block.scalar
            def _(act):
                step = Chain(act, act_step)
                for m in range(4):
                    act.wait_ge(centred, m + 1)
                    act.activation(sq[:, m % 2, :], qk[:, m, :], ACT.Square).then_inc(squared, 1)
                    act.wait_ge(squares_summed, m + 1)
                    if m >= 2:
                        act.wait_ge(dve_step, 2 * (m - 1))
                    for b, toks in halves:
                        ins = act.activation(rs[:, m % 2, toks], g.ps[:, 4 + 2 * (m % 2) + b, 0:toks.stop - toks.start], ACT.Ln,
                                             bias=g.eps, scale=1.0 / 64)
                    step.link(ins)
                    act.activation(rs[:, m % 2, :], rs[:, m % 2, :], ACT.Exp, scale=-0.5).then_inc(rooted, 1)

            @block.vector
            def _(dve):
                step = Chain(dve, dve_step)
                for m in range(4):
                    dve.wait_ge(summed, m + 1)
                    for b, toks in halves:
                        ins = dve.scalar_tensor_tensor(qk[:, m, toks], g.ps[:, 2 * (m % 2) + b, 0:toks.stop - toks.start], -1.0 / 64,
                                                       qk[:, m, toks], ALU.mult, ALU.add)
                    ins.then_inc(centred, 1)
                    dve.wait_ge(rooted, m + 1)
                    step.link(dve.scalar_tensor_tensor(qk[:, m, :], qk[:, m, :], col(g, "gn0", m, 1), rs[:, m % 2, :], ALU.mult, ALU.mult))
                    step.link(dve.tensor_tensor(qk[:, m, :], qk[:, m, :], gz[:, m, :], ALU.mult))
                for m in range(4):
                    y = qk[:, 4 + m, :]
                    step.link(dve.scalar_tensor_tensor(y, xbc[:, m, :], col(g, "ssd_d", m, 1), y, ALU.mult, ALU.add))
                    step.link(dve.tensor_tensor(y, y, gz[:, 4 + m, :], ALU.mult))


def first_layer(g, A):
    stage_ada(g, "ada0", "b_ada0", 0)
    with ExitStack() as mem:
        def sb(name, shape):
            return mem.enter_context(g.nc.sbuf_tensor(name, [P] + shape, F32))
        a = sb("a0", [KD, T])
        qk = sb("qk0", [8, T])
        gz = sb("gz0", [8, T])
        v = sb("v0", [TT, 512])
        xs_tok = sb("xs_tok", [TT, 512])
        dt_raw, dt = sb("dt_raw", [TT, 16]), sb("dt", [TT, 16])
        cum, ret_la = sb("cum", [2, TT, 16]), sb("ret_la", [32])
        cumT = mem.enter_context(g.nc.sbuf_tensor("cumT", [16, T], F32))
        stage_norm(g, "norm0a", g.h, a, KD, norm_parts(g, 0, True))
        with ExitStack() as raw_mem:
            raw = raw_mem.enter_context(g.nc.sbuf_tensor("xbc_raw", [P, 8, XPAD], F32))
            stage_in0(g, a, qk, gz, v, raw, dt_raw)
            stage_conv0(g, raw, a)
        stage_rope0(g, qk)
        stage_decays0(g, dt_raw, dt, cum, cumT, ret_la, a, xs_tok)
        g.probs = mem.enter_context(g.nc.sbuf_tensor("probs", [P, 4, NL], F32))
        stage_retention(g, qk, v, ret_la)
        stage_ssd(g, a, qk, dt, cum, cumT, xs_tok)
        stage_finish0(g, qk, gz, a)
        stage_norm(g, "norm0s", qk[:, 4:8, :], qk[:, 4:8, :], 4,
                   [(t, lambda k: col(g, "ssd_norm", k, 1), None) for t in (LAT, CTX)])
        stage_out(g, "out0", qk, True)
    with ExitStack() as mem:
        a = mem.enter_context(g.nc.sbuf_tensor("a0f", [P, KD, T], F32))
        stage_norm(g, "norm0b", g.h, a, KD, norm_parts(g, 3, True))
        stage_ffn(g, "ffn0", a, True)


def stage_in1(g, a, cq, ckv, kpe):
    n0 = g.first["in1"]
    groups = []
    for tile in range(8):
        who = "act" if tile % 2 else "dve"
        make = copy_act if tile % 2 else copy_dve
        if tile < 6:
            def dst(toks, tile=tile):
                return cq[:, tile, :]
        else:
            def dst(toks, tile=tile):
                return ckv[:, tile - 6, toks]
        groups.append(feature_group(g, n0 + tile // 2, KD, P * (tile % 2), a, tile >= 6, who, make(g, dst, tile >= 6)))

    def outs(b):
        def lhsT(k):
            return g.w.slot(n0 + 4, KD, ROPE)[:, k, :]
        return [(g.ps[64:96, b, 0:NL], lhsT, lambda k: a[:, k, LAT]), (g.ps[64:96, b + 1, 0:NC_], lhsT, lambda k: a[:, k, CTX])]

    def take(act, b):
        act.activation(kpe[64:96, LAT], g.ps[64:96, b, 0:NL], ACT.Copy)
        return act.activation(kpe[64:96, CTX], g.ps[64:96, b + 1, 0:NC_], ACT.Copy)
    groups.append((n0 + 4, KD, outs, "act", take))
    stage_project(g, "in1", groups, n0 + 5)


def stage_heads(g, cq, ckv, kpe, o_tok):
    w, n0 = g.w, g.first["heads"]
    base = w.before[n0]
    scale = float(NOPE + ROPE) ** -0.5
    HALF = T // 2
    with Stage(g, "heads") as st, ExitStack() as mem:
        def sb(name, shape):
            return mem.enter_context(g.nc.sbuf_tensor(f"heads_{name}", [P] + shape, F32))
        q = [sb(f"q{i}", [NL]) for i in range(2)]
        k = [sb(f"k{i}", [T]) for i in range(2)]
        v = [sb(f"v{i}", [TT, VH + 1]) for i in range(2)]
        probs = sb("probs", [TT, NL])
        swap, cs, t = sb("swap", [2 * ROPE]), sb("cs", [2, NL]), sb("t", [2, NL])
        neg_max, denom = sb("neg_max", [2, 4]), sb("denom", [4])
        names = ("tables_in", "fixed_ready", "kpe_swapped", "kpe_roped", "q_copied", "k_copied", "kv_copied", "q_swapped", "q_roped",
                 "scored", "max_done", "rows_made", "row_copied", "keyed", "exp_done", "summed", "o_done", "dve_step")
        (tables_in, fixed_ready, kpe_swapped, kpe_roped, q_copied, k_copied, kv_copied, q_swapped, q_roped,
         scored, max_done, rows_made, row_copied, keyed, exp_done, summed, o_done, dve_step) = (st.sem(n) for n in names)

        def at(i, r, per, more):
            return i * (4 * per) + (per * r + more)

        def all_heads(engine, body):
            with engine.Fori(0, 3) as i:
                for r in range(4):
                    body(i, r, True)
            for r in range(4):
                body(3, r, r < 3)

        pe_rows = slice(64, 96)
        with g.nc.Block() as block:
            @block.sync
            def _(sp):
                load_const(g, sp, swap[:, :], "swap1", tables_in)
                load_const(g, sp, cs[:, 0, :], "cos1", tables_in)
                load_const(g, sp, cs[:, 1, :], "sin1", tables_in)
                w.feed(sp, n0 + MLA_HEADS)

            @block.gpsimd
            def _(pool):
                st.begin(pool)

            @block.tensor
            def _(pe):
                def project(i, r):
                    n, b = n0 + r, r % 2
                    w.arrived(pe, n, i * 32)
                    wq, wkv = w.slot(n, 6, 96), w.slot(n, 2, P, 576)
                    for kk in range(6):
                        pe.matmul(g.ps[0:96, 0, :], wq[:, kk, :], cq[:, kk, :], start=(kk == 0), stop=(kk == 5))
                    for bank, toks in ((1, LAT), (2, CTX)):
                        for kk in range(2):
                            pe.matmul(g.ps[0:64, bank, 0:toks.stop - toks.start], wkv[:, kk, 0:64], ckv[:, kk, toks],
                                      start=(kk == 0), stop=(kk == 1))
                    for tile in range(TT):
                        for kk in range(2):
                            mm = pe.matmul(g.ps[:, 3, VH * tile:VH * tile + VH], ckv[:, kk, P * tile:P * tile + P],
                                           wkv[:, kk, 64:128], start=(kk == 0), stop=(kk == 1))
                    mm.then_inc(w.product_done, 1)

                def swap_q(i, r):
                    pe.wait_ge(q_copied, at(i, r, 1, 1))
                    pe.matmul(g.ps[64:128, 0, :], swap[pe_rows, :], q[r % 2][pe_rows, :], start=True, stop=True).then_inc(q_swapped, 1)

                def body(i, r, more):
                    b = r % 2
                    pe.wait_ge(q_roped, at(i, r, 1, 1))
                    pe.wait_ge(k_copied, at(i, r, 1, 1))
                    pe.wait_ge(kv_copied, at(i, r, 1, 1))
                    for qt in range(4):
                        if qt >= 2:
                            pe.wait_ge(max_done, at(i, r, 4, qt - 1))
                        for s in range(2):
                            mm = pe.matmul(g.ps[:, 4 + 2 * (qt % 2) + s, 0:HALF], q[b][0:96, P * qt:P * qt + P],
                                           k[b][0:96, HALF * s:HALF * s + HALF], start=True, stop=True)
                        mm.then_inc(scored, 1)
                    if more:
                        project(i, r + 1)
                    pe.wait_ge(max_done, at(i, r, 4, 4))
                    for qt in range(4):
                        mm = pe.matmul(g.ps[96:97, 4, P * qt:P * qt + P], neg_max[:, b, qt:qt + 1], g.ident, start=True, stop=True)
                    mm.then_inc(rows_made, 1)
                    pe.wait_ge(row_copied, at(i, r, 1, 1))
                    for kt in range(TT):
                        if kt >= 3:
                            pe.wait_ge(exp_done, at(i, r, TT, kt - 2))
                        pe.matmul(g.ps[:, 5 + kt % 3, :], k[b][0:97, P * kt:P * kt + P], q[b][0:97, :], start=True, stop=True).then_inc(keyed, 1)
                    if more:
                        swap_q(i, r + 1)
                    pe.wait_ge(exp_done, at(i, r, TT, TT))
                    for qt in range(4):
                        for kt in range(TT):
                            mm = pe.matmul(g.ps[:, 4, P * qt:P * qt + VH + 1], probs[:, kt, P * qt:P * qt + P], v[b][:, kt, :],
                                           start=(kt == 0), stop=(kt == TT - 1))
                    mm.then_inc(summed, 1)
                    pe.wait_ge(o_done, at(i, r, 1, 1))

                pe.wait_ge(tables_in, 48)
                pe.matmul(g.ps[64:128, 4, :], swap[pe_rows, :], kpe[pe_rows, LAT], start=True, stop=True).then_inc(kpe_swapped, 1)
                project(0, 0)
                swap_q(0, 0)
                pe.wait_ge(fixed_ready, 4)
                pe.wait_ge(kpe_roped, 2)
                all_heads(pe, body)

            @block.scalar
            def _(act):
                def take(i, r):
                    b = r % 2
                    act.wait_ge(w.product_done, at(i, r, 1, base + 1))
                    act.activation(q[b][0:96, :], g.ps[0:96, 0, :], ACT.Copy).then_inc(q_copied, 1)
                    act.activation(k[b][0:64, LAT], g.ps[0:64, 1, :], ACT.Copy).then_inc(k_copied, 1)

                def body(i, r, more):
                    b = r % 2
                    if more:
                        take(i, r + 1)
                    act.wait_ge(rows_made, at(i, r, 1, 1))
                    act.activation(q[b][96:97, :], g.ps[96:97, 4, :], ACT.Copy).then_inc(row_copied, 1)
                    for kt in range(TT):
                        act.wait_ge(keyed, at(i, r, TT, kt + 1))
                        act.activation(probs[:, kt, :], g.ps[:, 5 + kt % 3, :], ACT.Exp, scale=scale).then_inc(exp_done, 1)
                take(0, 0)
                all_heads(act, body)

            @block.vector
            def _(dve):
                step = Chain(dve, dve_step)

                def rope(x, swapped):
                    dve.tensor_tensor(t[pe_rows, 0, :], swapped, cs[pe_rows, 1, :], ALU.mult)
                    return dve.tensor_tensor(t[pe_rows, 1, :], x, cs[pe_rows, 0, :], ALU.mult)

                def take(i, r):
                    b = r % 2
                    dve.wait_ge(w.product_done, at(i, r, 1, base + 1))
                    dve.tensor_copy(k[b][0:64, CTX], g.ps[0:64, 2, 0:NC_])
                    dve.tensor_copy(v[b][:, :, 0:VH], g.ps[:, 3, 0:TT * VH].rearrange("p (t e) -> p t e", e=VH)).then_inc(kv_copied, 1)

                def rope_q(i, r, first=False):
                    b = r % 2
                    dve.wait_ge(q_swapped, at(i, r, 1, 1))
                    rope(q[b][pe_rows, :], g.ps[pe_rows, 0, :]).then_inc(dve_step, 1)
                    dve.wait_ge(dve_step, at(i, r, 2, 2 if first else 1))
                    dve.tensor_tensor(q[b][pe_rows, :], t[pe_rows, 0, :], t[pe_rows, 1, :], ALU.add).then_inc(q_roped, 1)

                def body(i, r, more):
                    b = r % 2
                    for qt in range(4):
                        dve.wait_ge(scored, at(i, r, 4, qt + 1))
                        pair = 4 + 2 * (qt % 2)
                        dve.tensor_reduce(neg_max[:, b, qt:qt + 1], g.ps[:, pair:pair + 2, 0:HALF], AX.XY, ALU.max, negate=True).then_inc(max_done, 1)
                    if more:
                        take(i, r + 1)
                        rope_q(i, r + 1)
                    dve.wait_ge(summed, at(i, r, 1, 1))
                    sums = g.ps[:, 4, :].rearrange("p (t e) -> p t e", e=P)
                    dve.reciprocal(denom[:, :].unsqueeze(2), sums[:, :, VH:VH + 1]).then_inc(dve_step, 1)
                    dve.wait_ge(dve_step, at(i, r, 2, 4 if more else 3))
                    dve.tensor_tensor(o_tok[:, :, bass.ds(at(i, r, VH, 0), VH)], sums[:, :, 0:VH],
                                      denom[:, :].unsqueeze(2).to_broadcast([P, 4, VH]), ALU.mult).then_inc(o_done, 1)

                for b in range(2):
                    dve.memset(k[b][96:97, :], 1.0).then_inc(fixed_ready, 1)
                    dve.memset(v[b][:, :, VH:VH + 1], 1.0).then_inc(fixed_ready, 1)
                dve.wait_ge(tables_in, 48)
                dve.wait_ge(kpe_swapped, 1)
                rope(kpe[pe_rows, LAT], g.ps[pe_rows, 4, :]).then_inc(dve_step, 1)
                dve.wait_ge(dve_step, 1)
                for b in range(2):
                    dve.tensor_copy(k[b][pe_rows, CTX], kpe[pe_rows, CTX])
                    dve.tensor_tensor(k[b][pe_rows, LAT], t[pe_rows, 0, :], t[pe_rows, 1, :], ALU.add).then_inc(kpe_roped, 1)
                take(0, 0)
                dve.wait_ge(kpe_roped, 2)
                rope_q(0, 0, True)
                all_heads(dve, body)


def stage_turn(g, o_tok, oT):
    with Stage(g, "turn") as st:
        turned, taken = st.sem("turned"), st.sem("taken")
        with g.nc.Block() as block:
            @block.gpsimd
            def _(pool):
                st.begin(pool)

            @block.tensor
            def _(pe):
                for m in range(KD):
                    for t in range(4):
                        mm = pe.transpose(g.ps[:, m, P * t:P * t + P], o_tok[:, t, P * m:P * m + P], g.ident)
                    mm.then_inc(turned, 1)

            @block.scalar
            def _(act):
                for m in range(0, KD, 2):
                    act.wait_ge(turned, m + 1)
                    act.activation(oT[:, m, LAT], g.ps[:, m, :], ACT.Copy).then_inc(taken, 1)

            @block.vector
            def _(dve):
                for m in range(1, KD, 2):
                    dve.wait_ge(turned, m + 1)
                    dve.tensor_copy(oT[:, m, LAT], g.ps[:, m, :]).then_inc(taken, 1)


def second_layer(g, A):
    stage_ada(g, "ada1", "b_ada1", 0)
    with ExitStack() as mem:
        def sb(name, shape):
            return mem.enter_context(g.nc.sbuf_tensor(name, [P] + shape, F32))
        a = sb("a1", [KD, T])
        cq, ckv, kpe, o_tok = sb("cq", [6, NL]), sb("ckv", [2, T]), sb("kpe", [T]), sb("o_tok", [4, D])
        stage_norm(g, "norm1a", g.h, a, KD, norm_parts(g, 0, True))
        stage_in1(g, a, cq, ckv, kpe)
        stage_norm(g, "norm1q", cq, cq, 6, [(slice(0, NL), lambda k: col(g, "q_norm", k, 1), None)])
        stage_norm(g, "norm1kv", ckv, ckv, 2, [(t, lambda k: col(g, "kv_norm", k, 1), None) for t in (LAT, CTX)])
        stage_heads(g, cq, ckv, kpe, o_tok)
        stage_turn(g, o_tok, a)
        stage_out(g, "out1", a, False)
    with ExitStack() as mem:
        a = mem.enter_context(g.nc.sbuf_tensor("a1f", [P, KD, T], F32))
        stage_norm(g, "norm1b", g.h, a, KD, norm_parts(g, 3, False))
        stage_ffn(g, "ffn1", a, False)
    stage_norm(g, "norm1f", g.h, g.h, KD, [(LAT, lambda k: col(g, "final_norm", k, 1), None)])


GW, GR = GRID_W, NL // GRID_W
NR = 14
DECAY_FLOOR = float(np.exp(-0.5))


def stage_context2(g, A):
    with Stage(g, "context2") as st:
        context_in = st.sem("context_in")
        with g.nc.Block() as block:
            @block.gpsimd
            def _(pool):
                st.begin(pool)

            @block.sync
            def _(sp):
                sp.dma_start(g.h[:, :, CTX], A["ctx2T"].rearrange("(k p) t -> p k t", p=P)).then_inc(context_in, 16)
                sp.wait_ge(context_in, 16)


def stage_in2(g, a, raw, cv):
    n0 = g.first["in2"]
    groups = []
    for tile in range(26):
        who = "act" if tile % 2 else "dve"
        make = copy_act if tile % 2 else copy_dve
        if tile < NR:
            def dst(toks, tile=tile):
                return raw[:, tile, toks]
        else:
            def dst(toks, tile=tile):
                return cv[:, tile - NR, :]
        groups.append(feature_group(g, n0 + tile // 2, KD, P * (tile % 2), a, tile < NR, who, make(g, dst, tile < NR)))
    stage_project(g, "in2", groups, n0 + 13)


def stage_shift(g, raw, mix, cv, y):
    with Stage(g, "shift") as st, ExitStack() as mem:
        mods = mem.enter_context(g.nc.sbuf_tensor("shift_mods", [P, 6], F32))
        coef = mem.enter_context(g.nc.sbuf_tensor("shift_coef", [P, 7, NR], F32))
        tables_in, dve_step = st.sem("tables_in"), st.sem("dve_step")
        with g.nc.Block() as block:
            @block.gpsimd
            def _(pool):
                st.begin(pool)

            @block.sync
            def _(sp):
                load_const(g, sp, mods[:, 0:4], "mod4", tables_in)
                load_const(g, sp, mods[:, 4:6], "mod2", tables_in)

            @block.vector
            def _(dve):
                step = Chain(dve, dve_step)
                dve.wait_ge(tables_in, 32)
                for d in range(6):
                    step.done(dve.tensor_scalar(coef[:, d, :], col(g, "shift_mu"), mods[:, d:d + 1], None, ALU.mult))
                step.link(dve.tensor_scalar(coef[:, 6, :], col(g, "shift_mu"), -1.0, 1.0, ALU.mult, ALU.add))
                for m in range(NR):
                    step.link(dve.tensor_scalar(mix[:, m, :], raw[:, m, :], coef[:, 6, m:m + 1], None, ALU.mult))

                    def add(to, of, d):
                        return dve.scalar_tensor_tensor(to, of, coef[:, d, m:m + 1], to, ALU.mult, ALU.add)
                    x = raw[:, m, LAT].rearrange("p (r c) -> p r c", c=GW)
                    o = mix[:, m, LAT].rearrange("p (r c) -> p r c", c=GW)
                    xc, oc = raw[:, m, CTX], mix[:, m, CTX]
                    step.link(add(o[:, :, 1:GW], x[:, :, 0:GW - 1], 0))
                    step.done(add(oc[:, 1:NC_], xc[:, 0:NC_ - 1], 4))
                    step.link(add(o[:, :, 0:GW - 1], x[:, :, 1:GW], 1))
                    step.done(add(oc[:, 0:NC_ - 1], xc[:, 1:NC_], 5))
                    step.link(add(o[:, 1:GR, :], x[:, 0:GR - 1, :], 2))
                    step.link(add(o[:, 0:GR - 1, :], x[:, 1:GR, :], 3))
                for m in range(4):
                    b, u, out = cv[:, m, :], cv[:, 4 + m, :], y[:, 4 + m, LAT]
                    step.link(dve.tensor_tensor(u, u, cv[:, 8 + m, :], ALU.mult))
                    step.link(dve.tensor_scalar(out, u, col(g, "conv3", 4 + m, 1), None, ALU.mult))
                    step.link(dve.scalar_tensor_tensor(out[:, 1:NL], u[:, 0:NL - 1], col(g, "conv3", m, 1), out[:, 1:NL], ALU.mult, ALU.add))
                    step.link(dve.scalar_tensor_tensor(out[:, 0:NL - 1], u[:, 1:NL], col(g, "conv3", 8 + m, 1), out[:, 0:NL - 1], ALU.mult, ALU.add))
                    step.link(dve.tensor_tensor(out, out, b, ALU.mult))


def stage_keys(g, mix, nk, ka):
    with Stage(g, "keys") as st, ExitStack() as mem:
        blk = mem.enter_context(g.nc.sbuf_tensor("keys_blk", [P, P], F32))
        sq = mem.enter_context(g.nc.sbuf_tensor("keys_sq", [P, 2, T], F32))
        rs = mem.enter_context(g.nc.sbuf_tensor("keys_rs", [P, 2, T], F32))
        names = ("table_in", "kk_ready", "squared", "summed", "floored", "rooted", "act_step", "dve_step")
        table_in, kk_ready, squared, summed, floored, rooted, act_step, dve_step = (st.sem(n) for n in names)
        halves = ((0, LAT), (1, CTX))
        with g.nc.Block() as block:
            @block.gpsimd
            def _(pool):
                st.begin(pool)

            @block.sync
            def _(sp):
                load_const(g, sp, blk[:, :], "blk64", table_in)

            @block.tensor
            def _(pe):
                pe.wait_ge(table_in, 16)
                for m in range(4):
                    pe.wait_ge(squared, m + 1)
                    if m >= 2:
                        pe.wait_ge(floored, m - 1)
                    for b, toks in halves:
                        mm = pe.matmul(g.ps[:, 2 * (m % 2) + b, 0:toks.stop - toks.start], blk[:, :], sq[:, m % 2, toks], start=True, stop=True)
                    mm.then_inc(summed, 1)

            @block.scalar
            def _(act):
                step = Chain(act, act_step)
                for m in range(4):
                    act.wait_ge(kk_ready, m + 1)
                    if m >= 2:
                        act.wait_ge(summed, m - 1)
                    act.activation(sq[:, m % 2, :], nk[:, m, :], ACT.Square).then_inc(squared, 1)
                step.done(act.activation(mix[0:64, 12, :], mix[0:64, 12, :], ACT.Tanh))
                for m in range(4):
                    act.wait_ge(floored, m + 1)
                    step.link(act.activation(rs[:, m % 2, :], rs[:, m % 2, :], ACT.Ln, scale=2.0 ** 20))
                    act.activation(rs[:, m % 2, :], rs[:, m % 2, :], ACT.Exp, scale=-0.5, bias=g.basic[:, 2 * P + 5:2 * P + 6]).then_inc(rooted, 1)

            @block.vector
            def _(dve):
                step = Chain(dve, dve_step)
                for m in range(4):
                    dve.tensor_scalar(nk[:, m, :], mix[:, 4 + m, :], col(g, "k_k", m, 1), None, ALU.mult).then_inc(kk_ready, 1)
                for m in range(4):
                    step.link(dve.tensor_scalar(ka[:, m, :], mix[:, 4 + m, :], col(g, "k_a", m, 1), None, ALU.mult))
                    step.link(dve.tensor_tensor(mix[:, 4 + m, :], mix[:, 4 + m, :], ka[:, m, :], ALU.subtract))
                for m in range(4):
                    dve.wait_ge(summed, m + 1)
                    if m >= 2:
                        step.settle()
                    for b, toks in halves:
                        ins = dve.tensor_scalar(rs[:, m % 2, toks], g.ps[:, 2 * (m % 2) + b, 0:toks.stop - toks.start], 1e-24, None, ALU.max)
                    ins.then_inc(floored, 1)
                    dve.wait_ge(rooted, m + 1)
                    step.done(dve.scalar_tensor_tensor(nk[:, m, :], nk[:, m, :], -1.0, rs[:, m % 2, :], ALU.mult, ALU.mult))


def stage_recurrence(g, name, steps, fwd_at, bwd_at, mix, nk, ka, state, y):
    with Stage(g, name) as st, ExitStack() as mem:
        def sb(n, shape):
            return mem.enter_context(g.nc.sbuf_tensor(f"{name}_{n}", [P] + shape, F32))
        lora = sb("lora", [2, 512])
        pairs, levels, eye = sb("pairs", [2, P]), sb("levels", [6, 2, 64]), sb("eye", [64])
        restart = sb("restart", [2, 256])
        shape = [2, 4, 64]
        wa = sb("wa", [2, 64])
        wr = sb("wr", [2, 2, 4, 64])
        cum, up, down = sb("cum", shape), sb("up", shape), sb("down", shape)
        ar = sb("ar", [2, 4, 2, 64])
        bt, kt = sb("bt", shape), sb("kt", shape)
        lb, lk = sb("lb", [2, 4, 2, 64]), sb("lk", [2, 4, 2, 64])
        bktok, vtok = sb("bktok", [2, 2, 4, 64]), sb("vtok", shape)
        x, xt, ys = sb("x", shape), sb("xt", shape), sb("ys", shape)
        vs = ys
        lt = sb("lt", [2] + shape)
        u = lt[:, 0]
        names = ("tables_in", "wa_copied", "low_rank_done", "v_turned", "vtok_ready", "biased", "tanhed", "cum_ready", "exps_done",
                 "before_ready", "upx_done", "v_copied", "bt_ready", "kt_ready", "ar_ready", "products_done", "turned", "lb_ready",
                 "x_ready", "tokens_copied", "w_done", "w_copied", "u_done", "u_copied", "y_done", "ds_done", "dve_step")
        sem = {n: st.sem(n) for n in names}
        for l in range(1, 6):
            for n in ("masked", "y", "copied", "summed", "added"):
                sem[f"level{l}_{n}"] = st.sem(f"level{l}_{n}")

        def flat(t):
            return t.rearrange("p m c -> p (m c)")

        def heads():
            for p0 in (0, 64):
                for m in range(4):
                    yield m, slice(p0, p0 + 64)

        def bank(d, b, half=0):
            return g.ps[:, 4 * d + b, 256 * half:256 * half + 256].rearrange("p (m c) -> p m c", m=4)

        def once(i, d):
            return i * 2 + (d + 1)

        with g.nc.Block() as block:
            @block.sync
            def _(sp):
                sp.dma_start(lora[0:64, :, :], g.A["w_lora_up_2"][0].rearrange("d k n -> k d n")).then_inc(sem["tables_in"], 16)
                sp.dma_start(lora[64:128, :, :], g.A["a_lora_up_2"][0].rearrange("d k n -> k d n")).then_inc(sem["tables_in"], 16)
                load_const(g, sp, pairs[:, :, :].rearrange("p a b -> p (a b)"), "pairs", sem["tables_in"])
                load_const(g, sp, levels[:, :, :, :].rearrange("p a b c -> p (a b c)"), "levels", sem["tables_in"])
                load_const(g, sp, eye[:, :], "eye64", sem["tables_in"])
                load_const(g, sp, restart[:, 0, :], "restart", sem["tables_in"])
                load_const(g, sp, restart[:, 1, :], "restart_b", sem["tables_in"])

            @block.gpsimd
            def _(pool):
                st.begin(pool)
                pool.wait_ge(sem["tables_in"], 16 * 7)
                with pool.Fori(0, steps) as i:
                    for l in range(1, 6):
                        for d in range(2):
                            if l == 1:
                                pool.wait_ge(sem["lb_ready"], once(i, d))
                            if l >= 3:
                                pool.wait_ge(sem[f"level{l - 2}_y"], once(i, d))
                            pool.tensor_tensor(lt[:, l % 2, d], lb[:, d, :, 0, :], levels[:, l, d, :].unsqueeze(1).to_broadcast([P, 4, 64]),
                                               ALU.mult).then_inc(sem[f"level{l}_masked"], 1)

            @block.tensor
            def _(pe):
                pe.wait_ge(sem["tables_in"], 16 * 7)
                with pe.Fori(0, steps) as i:
                    def wait(*waits):
                        pe.wait_ge(sem["tables_in"], 16 * 7)
                        for n, count in waits:
                            pe.wait_ge(sem[n], count)
                    for d in range(2):
                        wait(("wa_copied", once(i, d)))
                        for m in range(4):
                            pe.matmul(bank(d, 0)[:, m, :], lora[0:64, d, P * m:P * m + P], wa[0:64, d, :], start=True, stop=True)
                            mm = pe.matmul(bank(d, 2)[:, m, :], lora[64:128, d, P * m:P * m + P], wa[64:128, d, :], start=True, stop=True)
                        mm.then_inc(sem["low_rank_done"], 1)
                        wait(("v_copied", once(i, d)))
                        for m, r in heads():
                            mm = pe.matmul(bank(d, 3)[r, m, :], vs[r, d, m, :], g.ident[r, r], start=True, stop=True)
                        mm.then_inc(sem["v_turned"], 1)
                    for d in range(2):
                        wait(*((n, once(i, d)) for n in ("bt_ready", "kt_ready", "ar_ready", "vtok_ready")))
                        for m, r in heads():
                            two = ar[r, d, m, :, :].rearrange("p s c -> p (s c)")
                            pe.matmul(g.ps[r, 4 * d + 1, P * m:P * m + P], bt[r, d, m, :], two, start=True, stop=True)
                            pe.matmul(bank(d, 3)[r, m, :], ar[r, d, m, 0, :], bt[r, d, m, :], start=True, stop=True)
                            mm = pe.matmul(g.ps[r, 4 * d + 2, P * m:P * m + P], kt[r, d, m, :], two, start=True, stop=True)
                        mm.then_inc(sem["products_done"], 1)
                        for m, r in heads():
                            pe.matmul(bank(d, 0)[r, m, :], bt[r, d, m, :], g.ident[r, r], start=True, stop=True)
                            mm = pe.matmul(bank(d, 0, 1)[r, m, :], kt[r, d, m, :], g.ident[r, r], start=True, stop=True)
                        mm.then_inc(sem["turned"], 1)
                    for l in range(1, 6):
                        for d in range(2):
                            wait((f"level{l}_masked", once(i, d)),
                                 ("x_ready", once(i, d)) if l == 1 else (f"level{l - 1}_added", once(i, d)))
                            for m, r in heads():
                                mm = pe.matmul(bank(d, 1)[r, m, :], lt[r, l % 2, d, m, :], x[r, d, m, :], start=True, stop=True)
                            mm.then_inc(sem[f"level{l}_y"], 1)
                        if l == 1:
                            for d in range(2):
                                wait(("tokens_copied", once(i, d)))
                                for m, r in heads():
                                    pe.matmul(bank(d, 0)[r, m, :], ar[r, d, m, 0, :], state[r, d, m, :], start=True, stop=False)
                                    mm = pe.matmul(bank(d, 0)[r, m, :], lk[r, d, m, 0, :], vtok[r, d, m, :], start=False, stop=True)
                                mm.then_inc(sem["w_done"], 1)
                        for d in range(2):
                            wait((f"level{l}_copied", once(i, d)))
                            for m, r in heads():
                                if l < 5:
                                    pe.matmul(bank(d, 2)[r, m, :], xt[r, d, m, :], ys[r, d, m, :], start=True, stop=True)
                                mm = pe.matmul(bank(d, 3)[r, m, :], ys[r, d, m, :], xt[r, d, m, :], start=True, stop=True)
                            mm.then_inc(sem[f"level{l}_summed"], 1)
                    for d in range(2):
                        wait(("w_copied", once(i, d)), ("level5_added", once(i, d)))
                        for m, r in heads():
                            mm = pe.matmul(bank(d, 1)[r, m, :], xt[r, d, m, :], x[r, d, m, :], start=True, stop=True)
                        mm.then_inc(sem["u_done"], 1)
                    for d in range(2):
                        wait(("u_copied", once(i, d)))
                        for m, r in heads():
                            pe.matmul(bank(d, 3)[r, m, :], bktok[r, d, 0, m, :], u[r, d, m, :], start=True, stop=False)
                            mm = pe.matmul(bank(d, 3)[r, m, :], bktok[r, d, 1, m, :], vtok[r, d, m, :], start=False, stop=True)
                        if y is not None:
                            for m, r in heads():
                                pe.matmul(bank(d, 2)[r, m, :], state[r, d, m, :], ar[r, d, m, 1, :], start=True, stop=False)
                                pe.matmul(bank(d, 2)[r, m, :], u[r, d, m, :], lb[r, d, m, 1, :], start=False, stop=False)
                                mm = pe.matmul(bank(d, 2)[r, m, :], vtok[r, d, m, :], lk[r, d, m, 1, :], start=False, stop=True)
                        mm.then_inc(sem["ds_done"], 1)

            @block.scalar
            def _(act):
                with act.Fori(0, steps) as i:
                    def wait(n, d):
                        act.wait_ge(sem[n], once(i, d))
                    at = [fwd_at(i), bwd_at(i)]
                    for d in range(2):
                        wait("wa_copied", d)
                        act.activation(vs[:, d], mix[:, 8:12, bass.ds(at[d], CHUNK)], ACT.Copy).then_inc(sem["v_copied"], 1)
                    for d in range(2):
                        wait("biased", d)
                        both = wr[:, d].rearrange("p s m c -> p (s m c)")
                        act.activation(both, both, ACT.Tanh, scale=0.5).then_inc(sem["tanhed"], 1)
                        wait("v_turned", d)
                        act.activation(flat(vtok[:, d]), flat(bank(d, 3)), ACT.Copy).then_inc(sem["vtok_ready"], 1)
                    for d in range(2):
                        wait("cum_ready", d)
                        act.activation(flat(down[:, d]), flat(cum[:, d]), ACT.Exp, scale=-1.0)
                        act.activation(flat(up[:, d]), flat(cum[:, d]), ACT.Exp).then_inc(sem["exps_done"], 1)
                        wait("before_ready", d)
                        act.activation(flat(wr[:, d, 0]), flat(wr[:, d, 0]), ACT.Exp).then_inc(sem["upx_done"], 1)
                    for d in range(2):
                        wait("turned", d)
                        act.activation(bktok[:, d].rearrange("p s m c -> p (s m c)"), g.ps[:, 4 * d, :], ACT.Copy).then_inc(sem["tokens_copied"], 1)
                    for l in range(1, 6):
                        for d in range(2):
                            act.wait_ge(sem[f"level{l}_y"], once(i, d))
                            if l > 1:
                                act.wait_ge(sem[f"level{l - 1}_summed"], once(i, d))
                            act.activation(flat(ys[:, d]), flat(bank(d, 1)), ACT.Copy).then_inc(sem[f"level{l}_copied"], 1)
                    for d in range(2):
                        wait("w_done", d)
                        act.wait_ge(sem["level5_y"], once(i, d))
                        act.activation(flat(x[:, d]), flat(bank(d, 0)), ACT.Copy).then_inc(sem["w_copied"], 1)
                    for d in range(2):
                        wait("u_done", d)
                        act.activation(flat(u[:, d]), flat(bank(d, 1)), ACT.Copy).then_inc(sem["u_copied"], 1)

            @block.vector
            def _(dve):
                PER = 12
                dve.wait_ge(sem["tables_in"], 16 * 7)
                if y is None:
                    dve.memset(state.rearrange("p d m c -> p (d m c)"), 0.0)
                else:
                    dve.memset(y[:, 0:4, LAT], 0.0)
                with dve.Fori(0, steps) as i:
                    n = [0]

                    def link(ins):
                        n[0] += 1
                        ins.then_inc(sem["dve_step"], 1)
                        dve.wait_ge(sem["dve_step"], i * PER + n[0])

                    def wait(s, d):
                        dve.wait_ge(sem[s], once(i, d))
                    at = [bass.ds(fwd_at(i), CHUNK), bass.ds(bwd_at(i), CHUNK)]
                    first = g.at["w0"][0]
                    bias = g.params[:, first:first + 16].rearrange("p (s d m) -> p s d m", s=2, d=2)
                    for d in range(2):
                        dve.tensor_copy(wa[:, d, :], mix[:, 12, at[d]]).then_inc(sem["wa_copied"], 1)
                    for d in range(2):
                        wait("low_rank_done", d)
                        dve.tensor_tensor(wr[:, d], g.ps[:, 4 * d:4 * d + 3:2, 0:256].rearrange("p s (m c) -> p s m c", m=4),
                                          bias[:, :, d, :].unsqueeze(3).to_broadcast([P, 2, 4, 64]), ALU.add).then_inc(sem["biased"], 1)
                    for d in range(2):
                        lw, rate = wr[:, d, 0], wr[:, d, 1]
                        wait("tanhed", d)
                        dve.tensor_scalar(flat(rate), flat(rate), 0.5, 0.5, ALU.mult, ALU.add)
                        link(dve.tensor_scalar(flat(lw), flat(lw), -0.5 * DECAY_FLOOR, -0.5 * DECAY_FLOOR, ALU.mult, ALU.add))
                        if d == 0:
                            scan = dve.tensor_tensor_scan(flat(cum[:, d]), restart[:, d, :], flat(lw), 0.0, ALU.mult, ALU.add)
                        else:
                            scan = dve.tensor_tensor_scan(flat(cum[:, d])[:, ::-1], restart[:, d, ::-1], flat(lw)[:, ::-1], 0.0, ALU.mult, ALU.add)
                        scan.then_inc(sem["cum_ready"], 1)
                        wait("cum_ready", d)
                        dve.tensor_tensor(flat(lw), flat(cum[:, d]), flat(lw), ALU.subtract).then_inc(sem["before_ready"], 1)
                        dve.tensor_tensor(bt[:, d], nk[:, :, at[d]], rate, ALU.mult)
                        link(dve.tensor_tensor(kt[:, d], ka[:, :, at[d]], rate, ALU.mult))
                        link(dve.tensor_tensor(kt[:, d], kt[:, d], mix[:, 4:8, at[d]], ALU.add))
                    for d in range(2):
                        wait("exps_done", d)
                        dve.scalar_tensor_tensor(flat(bt[:, d]), flat(bt[:, d]), -1.0, flat(down[:, d]), ALU.mult, ALU.mult).then_inc(sem["bt_ready"], 1)
                        dve.tensor_tensor(flat(kt[:, d]), flat(kt[:, d]), flat(down[:, d]), ALU.mult).then_inc(sem["kt_ready"], 1)
                        dve.tensor_tensor(ar[:, d, :, 1, :], mix[:, 0:4, at[d]], up[:, d], ALU.mult)
                        wait("upx_done", d)
                        dve.tensor_tensor(ar[:, d, :, 0, :], nk[:, :, at[d]], wr[:, d, 0], ALU.mult).then_inc(sem["ar_ready"], 1)
                    for d in range(2):
                        wait("products_done", d)
                        mask = pairs[:, d, :].unsqueeze(1).to_broadcast([P, 4, P])
                        both = eye[:, :].unsqueeze(1).to_broadcast([P, 4, 64])
                        dve.tensor_tensor(lb[:, d].rearrange("p m s c -> p m (s c)"), g.ps[:, 4 * d + 1, :].rearrange("p (m c) -> p m c", c=P), mask,
                                          ALU.mult).then_inc(sem["lb_ready"], 1)
                        wait("lb_ready", d)
                        dve.tensor_tensor(x[:, d], bank(d, 3), levels[:, 0, 1 - d, :].unsqueeze(1).to_broadcast([P, 4, 64]), ALU.mult)
                        link(dve.tensor_tensor(xt[:, d], lb[:, d, :, 0, :], levels[:, 0, d, :].unsqueeze(1).to_broadcast([P, 4, 64]), ALU.mult))
                        dve.tensor_tensor(x[:, d], x[:, d], both, ALU.add)
                        dve.tensor_tensor(xt[:, d], xt[:, d], both, ALU.add)
                        dve.tensor_tensor(lk[:, d].rearrange("p m s c -> p m (s c)"), g.ps[:, 4 * d + 2, :].rearrange("p (m c) -> p m c", c=P), mask,
                                          ALU.mult).then_inc(sem["x_ready"], 1)
                    for l in range(1, 6):
                        for d in range(2):
                            dve.wait_ge(sem[f"level{l}_summed"], once(i, d))
                            if l == 1:
                                wait("x_ready", d)
                            else:
                                dve.wait_ge(sem[f"level{l - 1}_added"], once(i, d))
                            if l < 5:
                                dve.tensor_tensor(flat(x[:, d]), flat(x[:, d]), flat(bank(d, 2)), ALU.add)
                            dve.tensor_tensor(flat(xt[:, d]), flat(xt[:, d]), flat(bank(d, 3)), ALU.add).then_inc(sem[f"level{l}_added"], 1)
                    for d in range(2):
                        wait("ds_done", d)
                        if y is not None:
                            out = y[:, 0:4, bass.ds(([fwd_at(i), bwd_at(i)])[d], CHUNK)]
                            dve.tensor_tensor(out, out, bank(d, 2), ALU.add)
                        link(dve.tensor_tensor(flat(state[:, d]), flat(state[:, d]), flat(bank(d, 3)), ALU.add))
                        last = (CHUNK - 1, 0)[d]
                        link(dve.tensor_tensor(state[:, d], state[:, d], up[:, d, :, last:last + 1].to_broadcast([P, 4, 64]), ALU.mult))
                    assert n[0] == PER, n


def stage_rwkv_out(g, mix, ka, y):
    with Stage(g, "rwkv_out") as st, ExitStack() as mem:
        def sb(n, shape):
            return mem.enter_context(g.nc.sbuf_tensor(f"rwkv_out_{n}", [P] + shape, F32))
        lora, gate_up, blk = sb("lora", [2, 512]), sb("gate_up", [512]), sb("blk", [P])
        half_a0 = sb("half_a0", [8])
        rate, rk, sq, rs, gate = (sb(n, [2, NL]) for n in ("rate", "rk", "sq", "rs", "gate"))
        names = ("tables_in", "half_ready", "gate_in", "rates_done", "tanhed", "rk_ready", "bonus_done", "gate_done", "mean_done",
                 "centred", "squared", "var_done", "rooted", "act_step", "dve_step", "gate_taken")
        (tables_in, half_ready, gate_in, rates_done, tanhed, rk_ready, bonus_done, gate_done, mean_done, centred, squared,
         var_done, rooted, act_step, dve_step, gate_taken) = (st.sem(n) for n in names)
        with g.nc.Block() as block:
            @block.gpsimd
            def _(pool):
                st.begin(pool)

            @block.sync
            def _(sp):
                sp.dma_start(lora[64:128, :, :], g.A["a_lora_up_2"][0].rearrange("d k n -> k d n")).then_inc(tables_in, 16)
                sp.dma_start(gate_up[:, :], g.A["g_lora_up_2"][0]).then_inc(tables_in, 16)
                load_const(g, sp, blk[:, :], "blk64", tables_in)

            @block.tensor
            def _(pe):
                pe.wait_ge(tables_in, 48)
                for m in range(4):
                    if m:
                        pe.wait_ge(tanhed, m)
                    for d in range(2):
                        mm = pe.matmul(g.ps[:, d, :], lora[64:128, d, P * m:P * m + P], mix[64:128, 12, LAT], start=True, stop=True)
                    mm.then_inc(rates_done, 1)
                    if m == 0:
                        pe.wait_ge(gate_in, 1)
                    if m:
                        pe.wait_ge(dve_step, 6 * m)
                        pe.wait_ge(gate_taken, m)
                    pe.matmul(g.ps[:, 3, :], gate_up[:, P * m:P * m + P], mix[:, 13, LAT], start=True, stop=True).then_inc(gate_done, 1)
                    pe.matmul(g.ps[:, 4, :], blk[:, :], y[:, m, LAT], start=True, stop=True).then_inc(mean_done, 1)
                    pe.wait_ge(rk_ready, m + 1)
                    pe.matmul(g.ps[:, 2, :], blk[:, :], rk[:, m % 2, :], start=True, stop=True).then_inc(bonus_done, 1)
                    pe.wait_ge(squared, m + 1)
                    pe.matmul(g.ps[:, 5, :], blk[:, :], sq[:, m % 2, :], start=True, stop=True).then_inc(var_done, 1)

            @block.scalar
            def _(act):
                step = Chain(act, act_step)
                act.activation(mix[:, 13, LAT], mix[:, 13, LAT], ACT.Tanh, scale=0.5).then_inc(act_step, 1)
                step.n = 1
                act.wait_ge(half_ready, 1)
                for m in range(4):
                    act.wait_ge(rates_done, m + 1)
                    if m:
                        act.wait_ge(rk_ready, m)
                    for d in range(2):
                        ins = act.activation(rate[:, d, :], g.ps[:, d, :], ACT.Tanh, scale=0.5, bias=half_a0[:, 4 * d + m:4 * d + m + 1])
                    ins.then_inc(tanhed, 1)
                    act.wait_ge(gate_done, m + 1)
                    act.activation(gate[:, m % 2, :], g.ps[:, 3, :], ACT.Copy).then_inc(gate_taken, 1)
                    act.wait_ge(centred, m + 1)
                    act.activation(sq[:, m % 2, :], y[:, m, LAT], ACT.Square).then_inc(squared, 1)
                    act.wait_ge(var_done, m + 1)
                    step.link(act.activation(rs[:, m % 2, :], g.ps[:, 5, :], ACT.Ln, bias=g.gn_eps, scale=1.0 / 64))
                    act.activation(rs[:, m % 2, :], rs[:, m % 2, :], ACT.Exp, scale=-0.5).then_inc(rooted, 1)

            @block.vector
            def _(dve):
                step = Chain(dve, dve_step)
                dve.tensor_scalar(half_a0[:, :], col(g, "a0"), 0.5, None, ALU.mult).then_inc(half_ready, 1)
                dve.wait_ge(act_step, 1)
                dve.tensor_scalar(mix[:, 13, LAT], mix[:, 13, LAT], 0.5, 0.5, ALU.mult, ALU.add).then_inc(gate_in, 1)
                for m in range(4):
                    dve.wait_ge(tanhed, m + 1)
                    s = rk[:, m % 2, :]
                    step.link(dve.scalar_tensor_tensor(s, rate[:, 0, :], 2.0, rate[:, 1, :], ALU.add, ALU.add))
                    step.link(dve.scalar_tensor_tensor(s, s, 0.5, ka[:, m, LAT], ALU.mult, ALU.mult))
                    step.link(dve.scalar_tensor_tensor(s, mix[:, 4 + m, LAT], 2.0, s, ALU.mult, ALU.add))
                    dve.scalar_tensor_tensor(s, s, col(g, "r_k", m, 1), mix[:, m, LAT], ALU.mult, ALU.mult).then_inc(rk_ready, 1)
                    dve.wait_ge(mean_done, m + 1)
                    dve.scalar_tensor_tensor(y[:, m, LAT], g.ps[:, 4, :], -1.0 / 64, y[:, m, LAT], ALU.mult, ALU.add).then_inc(centred, 1)
                    dve.wait_ge(bonus_done, m + 1)
                    step.done(dve.tensor_tensor(s, g.ps[:, 2, :], mix[:, 8 + m, LAT], ALU.mult))
                    dve.wait_ge(rooted, m + 1)
                    step.link(dve.scalar_tensor_tensor(y[:, m, LAT], y[:, m, LAT], col(g, "gn_g", m, 1), rs[:, m % 2, :], ALU.mult, ALU.mult))
                    dve.wait_ge(gate_taken, m + 1)
                    step.link(dve.scalar_tensor_tensor(y[:, m, LAT], y[:, m, LAT], col(g, "gn_b", m, 1), s, ALU.add, ALU.add))
                    dve.tensor_tensor(y[:, m, LAT], y[:, m, LAT], gate[:, m % 2, :], ALU.mult)


def stage_router(g, a, a_tok, aff, idx):
    with Stage(g, "router") as st, ExitStack() as mem:
        def sb(n, shape, parts=P):
            return mem.enter_context(g.nc.sbuf_tensor(f"router_{n}", [parts] + shape, F32))
        rw = sb("rw", [KD, EXPERTS])
        expd, small = sb("expd", [4, EXPERTS]), sb("small", [3, 4])
        affT, work, best = sb("affT", [NL], 16), sb("work", [2, NL], 16), sb("best", [8], 16)
        idxT, ones_row = sb("idxT", [NL], 16), sb("ones_row", [NL], 16)
        names = ("router_in", "logits_done", "max_ready", "exps_done", "aff_ready", "rows_done", "idx_ready", "idx_turned",
                 "turned", "taken_a", "taken_v", "dve_step", "act_step")
        (router_in, logits_done, max_ready, exps_done, aff_ready, rows_done, idx_ready, idx_turned, turned, taken_a, taken_v,
         dve_step, act_step) = (st.sem(n) for n in names)
        with g.nc.Block() as block:
            @block.gpsimd
            def _(pool):
                st.begin(pool)

            @block.sync
            def _(sp):
                sp.dma_start(rw[:, :, :], g.A["router_w_2"][0].rearrange("(k p) n -> p k n", p=P)).then_inc(router_in, 16)
                g.w.feed(sp, g.first["experts"])

            @block.tensor
            def _(pe):
                pe.wait_ge(router_in, 16)
                for t in range(4):
                    for k in range(KD):
                        mm = pe.matmul(g.ps[:, 0, EXPERTS * t:EXPERTS * t + EXPERTS], a[:, k, NC_ + P * t:NC_ + P * t + P], rw[:, k, :],
                                       start=(k == 0), stop=(k == KD - 1))
                mm.then_inc(logits_done, 1)
                for n in range(8):
                    t, half = n // 2, n % 2
                    if n >= 4:
                        pe.wait_ge(taken_a, n - 3)
                    for q in range(4):
                        mm = pe.transpose(g.ps[:, 2 + n % 4, P * q:P * q + P], a[:, 4 * half + q, NC_ + P * t:NC_ + P * t + P], g.ident)
                    mm.then_inc(turned, 1)
                pe.wait_ge(aff_ready, 1)
                for t in range(4):
                    mm = pe.transpose(g.ps[0:16, 1, P * t:P * t + P], aff[:, t, :], g.ident)
                mm.then_inc(rows_done, 1)
                pe.wait_ge(idx_ready, 1)
                for t in range(4):
                    mm = pe.transpose(g.ps[:, 6, 16 * t:16 * t + 16], idxT[:, P * t:P * t + P], g.ident[0:16, 0:16])
                mm.then_inc(idx_turned, 1)

            @block.scalar
            def _(act):
                act.wait_ge(max_ready, 1)
                for t in range(4):
                    ins = act.activation(expd[:, t, :], g.ps[:, 0, EXPERTS * t:EXPERTS * t + EXPERTS], ACT.Exp,
                                         bias=small[:, 0, t:t + 1], accum_out=small[:, 1, t:t + 1])
                ins.then_inc(exps_done, 1)
                for n in range(8):
                    act.wait_ge(turned, n + 1)
                    act.activation(a_tok[:, n // 2, 512 * (n % 2):512 * (n % 2) + 512], g.ps[:, 2 + n % 4, :], ACT.Copy).then_inc(taken_a, 1)

            @block.vector
            def _(dve):
                step = Chain(dve, dve_step)
                dve.memset(ones_row[:, :], 1.0)
                dve.wait_ge(logits_done, 1)
                logits = g.ps[:, 0, 0:4 * EXPERTS].rearrange("p (t e) -> p t e", e=EXPERTS)
                dve.tensor_reduce(small[:, 0, :], logits, AX.X, ALU.max, negate=True).then_inc(max_ready, 1)
                dve.wait_ge(exps_done, 1)
                step.link(dve.reciprocal(small[:, 2, :], small[:, 1, :]))
                dve.tensor_tensor(aff[:, :, :], expd[:, :, :], small[:, 2, :].unsqueeze(2).to_broadcast([P, 4, EXPERTS]), ALU.mult).then_inc(aff_ready, 1)
                dve.wait_ge(rows_done, 1)
                step.link(dve.tensor_copy(work[:, 0, :], g.ps[0:16, 1, :]))
                for n in range(CAP // 8):
                    step.link(dve.max(best[:, :], work[:, n % 2, :]))
                    step.link(dve.match_replace(work[:, (n + 1) % 2, :], best[:, :], work[:, n % 2, :], -1.0))
                chosen, count = work[:, 0, :], work[:, 1, :]
                step.link(dve.tensor_scalar(chosen, chosen, 0.0, None, ALU.is_lt))
                step.link(dve.tensor_tensor_scan(count, ones_row[:, :], chosen, 0.0, ALU.mult, ALU.add))
                step.link(dve.tensor_tensor(count, count, chosen, ALU.mult))
                dve.tensor_scalar(idxT[:, :], count, -1.0, None, ALU.add).then_inc(idx_ready, 1)
                dve.wait_ge(idx_turned, 1)
                dve.tensor_copy(idx[:, :, :], g.ps[:, 6, 0:64].rearrange("p (t e) -> p t e", e=EXPERTS))


def stage_experts(g, a_tok, aff, idx, made, pickT):
    w, n0 = g.w, g.first["experts"]
    base = w.before[n0]
    with Stage(g, "experts") as st, ExitStack() as mem:
        def sb(n, shape):
            return mem.enter_context(g.nc.sbuf_tensor(f"experts_{n}", [P] + shape, F32))
        iota = sb("iota", [CAP])
        pick = sb("pick", [2, 4, CAP])
        own = sb("own", [2, 4])
        val = sb("val", [2, 1])
        xs = sb("xs", [2, KD, CAP])
        sg, hs = sb("sg", [2, NL]), sb("hs", [D])
        hT = sb("hT", [2, KD, CAP])
        names = ("table_in", "pick_ready", "gathered", "xs_ready", "pick_turned", "pickT_ready", "valued", "val_ready",
                 "silu_ready", "hs_ready", "hs_turned", "hT_ready", "out_taken")
        (table_in, pick_ready, gathered, xs_ready, pick_turned, pickT_ready, valued, val_ready, silu_ready, hs_ready,
         hs_turned, hT_ready, out_taken) = (st.sem(n) for n in names)
        TURNS = EXPERTS // 2

        def at(i, r, per, more):
            return i * (2 * per) + (per * r + more)

        with g.nc.Block() as block:
            @block.gpsimd
            def _(pool):
                st.begin(pool)

            @block.sync
            def _(sp):
                load_const(g, sp, iota[:, :], "iota64", table_in)
                w.feed(sp, n0 + 12 * EXPERTS)

            @block.tensor
            def _(pe):
                with pe.Fori(0, TURNS) as i:
                    for r in range(2):
                        b = slice(64 * r, 64 * r + 64)
                        pe.wait_ge(pick_ready, at(i, r, 1, 1))
                        for k in range(KD):
                            for t in range(4):
                                mm = pe.matmul(g.ps[:, 0, CAP * k:CAP * k + CAP], a_tok[:, t, P * k:P * k + P], pick[:, r, t, :],
                                               start=(t == 0), stop=(t == 3))
                        mm.then_inc(gathered, 1)
                        for t in range(4):
                            mm = pe.matmul(g.ps[b, 5, P * t:P * t + P], pick[:, r, t, :], g.ident, start=True, stop=True)
                        mm.then_inc(pick_turned, 1)
                        pe.wait_ge(xs_ready, at(i, r, 1, 1))
                        for t in range(4):
                            mm = pe.matmul(g.ps[b, 0, 0:1], pick[:, r, t, :], own[:, r, t:t + 1], start=(t == 0), stop=(t == 3))
                        mm.then_inc(valued, 1)
                        for half in range(2):
                            for q, bank in enumerate((1 + 2 * half, 2 + 2 * half)):
                                for c in range(2):
                                    e = 4 * half + 2 * q + c
                                    n = n0 + 12 * r + e
                                    w.arrived(pe, n, i * (16 * 24 // RING))
                                    for k in range(KD):
                                        mm = pe.matmul(g.ps[b, bank, 256 * c:256 * c + 256], xs[:, r, k, :], w.slot(n)[:, k, :],
                                                       start=(k == 0), stop=(k == KD - 1))
                                    mm.then_inc(w.product_done, 1)
                        pe.wait_ge(hs_ready, at(i, r, 2, 2))
                        pe.wait_ge(pickT_ready, at(i, r, 1, 1))
                        for k in range(KD):
                            mm = pe.matmul(g.ps[:, 5, CAP * k:CAP * k + CAP], hs[b, P * k:P * k + P], g.ident[b, b], start=True, stop=True)
                        mm.then_inc(hs_turned, 1)
                        pe.wait_ge(hT_ready, at(i, r, 1, 1))
                        pe.wait_ge(val_ready, at(i, r, 1, 1))
                        for c in range(4):
                            n = n0 + 12 * r + 8 + c
                            w.arrived(pe, n, i * (16 * 24 // RING))
                            for k in range(KD):
                                mm = pe.matmul(g.ps[b, 6 + c // 2, 256 * (c % 2):256 * (c % 2) + 256], hT[:, r, k, :], w.slot(n)[:, k, :],
                                               start=(k == 0), stop=(k == KD - 1))
                            mm.then_inc(w.product_done, 1)

            @block.scalar
            def _(act):
                with act.Fori(0, TURNS) as i:
                    for r in range(2):
                        b = slice(64 * r, 64 * r + 64)
                        act.wait_ge(gathered, at(i, r, 1, 1))
                        act.activation(xs[:, r, :, :].rearrange("p k c -> p (k c)"), g.ps[:, 0, :], ACT.Copy).then_inc(xs_ready, 1)
                        for half in range(2):
                            act.wait_ge(w.product_done, at(i, r, 12, base + 4 * half + 2))
                            act.activation(sg[b, half, :], g.ps[b, 1 + 2 * half, :], ACT.Silu).then_inc(silu_ready, 1)
                        act.wait_ge(hs_turned, at(i, r, 1, 1))
                        act.activation(hT[:, r, :, :].rearrange("p k c -> p (k c)"), g.ps[:, 5, :], ACT.Copy).then_inc(hT_ready, 1)
                        act.wait_ge(val_ready, at(i, r, 1, 1))
                        act.wait_ge(w.product_done, at(i, r, 12, base + 12))
                        flat = made[:, :, :].rearrange("p e n -> p (e n)")
                        for c in range(2):
                            ins = act.activation(flat[b, bass.ds(i * D + 512 * c, 512)], g.ps[b, 6 + c, :], ACT.Copy, scale=val[b, r, :])
                        ins.then_inc(out_taken, 1)
                        act.wait_ge(out_taken, at(i, r, 1, 1))

            @block.vector
            def _(dve):
                dve.wait_ge(table_in, 16)

                def choose(i, r):
                    e = at(i, r, 1, 0)
                    dve.tensor_copy(own[:, r, :].unsqueeze(2), aff[:, :, bass.ds(e, 1)])
                    for t in range(4):
                        fl = idx[:, :, :].rearrange("p t e -> p (t e)")
                        ins = dve.tensor_scalar(pick[:, r, t, :], iota[:, :], fl[:, bass.ds(at(i, r, 1, EXPERTS * t), 1)], None, ALU.is_equal)
                    ins.then_inc(pick_ready, 1)

                with dve.Fori(0, TURNS) as i:
                    for r in range(2):
                        b = slice(64 * r, 64 * r + 64)
                        choose(i, r)
                        dve.wait_ge(pick_turned, at(i, r, 1, 1))
                        pf = pickT[:, :, :].rearrange("p e n -> p (e n)")
                        dve.tensor_copy(pf[b, bass.ds(i * NL, NL)], g.ps[b, 5, :]).then_inc(pickT_ready, 1)
                        dve.wait_ge(valued, at(i, r, 1, 1))
                        dve.tensor_copy(val[b, r, :], g.ps[b, 0, 0:1]).then_inc(val_ready, 1)
                        for half in range(2):
                            dve.wait_ge(w.product_done, at(i, r, 12, base + 4 * half + 4))
                            dve.wait_ge(silu_ready, at(i, r, 2, half + 1))
                            dve.tensor_tensor(hs[b, 512 * half:512 * half + 512], sg[b, half, :], g.ps[b, 2 + 2 * half, :], ALU.mult).then_inc(hs_ready, 1)


def stage_scatter(g, made, pickT):
    with Stage(g, "scatter") as st:
        summed, added = st.sem("summed"), st.sem("added")
        pairs = EXPERTS // 2
        with g.nc.Block() as block:
            @block.gpsimd
            def _(pool):
                st.begin(pool)

            @block.tensor
            def _(pe):
                for m in range(KD):
                    for e in range(pairs):
                        mm = pe.matmul(g.ps[:, m, :], made[:, e, P * m:P * m + P], pickT[:, e, :], start=(e == 0), stop=(e == pairs - 1))
                    mm.then_inc(summed, 1)

            @block.vector
            def _(dve):
                for m in range(KD):
                    dve.wait_ge(summed, m + 1)
                    dve.scalar_tensor_tensor(g.h[:, m, LAT], g.ps[:, m, :], g.mod[:, 5 * KD + m, 0:1], g.h[:, m, LAT],
                                             ALU.mult, ALU.add).then_inc(added, 1)


def third_layer(g, A):
    stage_context2(g, A)
    stage_ada(g, "ada2", "b_ada2", 1, gains=("norm1_g", "norm2_g"))
    with ExitStack() as mem:
        def sb(name, shape):
            return mem.enter_context(g.nc.sbuf_tensor(name, [P] + shape, F32))
        a = sb("a2", [KD, T])
        mix = sb("mix", [NR, T])
        stage_norm(g, "norm2a", g.h, a, KD, norm_parts(g, 0, True))
        with ExitStack() as inner:
            raw = inner.enter_context(g.nc.sbuf_tensor("raw2", [P, NR, T], F32))
            cv = inner.enter_context(g.nc.sbuf_tensor("cv", [P, 12, NL], F32))
            stage_in2(g, a, raw, cv)
            stage_shift(g, raw, mix, cv, a)
        nk, ka, state = sb("nk", [4, T]), sb("ka", [4, T]), sb("state", [2, 4, 64])
        stage_keys(g, mix, nk, ka)
        nctx, nlat = NC_ // CHUNK, NL // CHUNK
        stage_recurrence(g, "ctx_rec", nctx, lambda i: i * CHUNK, lambda i: i * (-CHUNK) + (NC_ - CHUNK), mix, nk, ka, state, None)
        stage_recurrence(g, "lat_rec", nlat, lambda i: i * CHUNK + NC_, lambda i: i * (-CHUNK) + (T - CHUNK), mix, nk, ka, state, a)
        stage_rwkv_out(g, mix, ka, a)
        stage_out(g, "out2", a, False)
    with ExitStack() as mem:
        def sb(name, shape):
            return mem.enter_context(g.nc.sbuf_tensor(name, [P] + shape, F32))
        a_tok, aff, idx = sb("a_tok", [4, D]), sb("aff", [4, EXPERTS]), sb("idx", [4, EXPERTS])
        made, pickT = sb("made", [EXPERTS // 2, D]), sb("pickT", [EXPERTS // 2, NL])
        with ExitStack() as inner:
            a = inner.enter_context(g.nc.sbuf_tensor("a2f", [P, KD, T], F32))
            stage_norm(g, "norm2b", g.h, a, KD, norm_parts(g, 3, False))
            stage_router(g, a, a_tok, aff, idx)
        stage_experts(g, a_tok, aff, idx, made, pickT)
        stage_scatter(g, made, pickT)
    stage_norm(g, "norm2f", g.h, g.h, KD, [(LAT, lambda k: col(g, "final_g", k, 1), None)], store=A["out"])


def program(nc, A, at, cat):
    with ExitStack() as keep:
        g = Prog(nc)
        g.keep, g.A, g.at, g.cat = keep, A, at, cat
        vector_memory(g, A)
        g.first = plan_weights(g, A)
        stage_start(g, A)
        first_layer(g, A)
        second_layer(g, A)
        third_layer(g, A)


_WEIGHTS = ["w_ada", "w_ffn_gate", "w_ffn_up", "w_ffn_down", "ret_ssd_w_in", "ret_ssd_w_out", "mla_w_in",
            "mla_w_uq", "mla_w_ukv", "mla_w_out", "ada_w_2", "w_in_2", "w_lora_up_2", "a_lora_up_2",
            "g_lora_up_2", "w_out_2", "router_w_2", "exp_w_gate_2", "exp_w_up_2", "exp_w_down_2"]


def lay_out(inputs):
    x = {k: np.asarray(v) for k, v in inputs.items()}
    params, at = lay_params(x)
    consts, cat = constants()
    arrays = {k: np.ascontiguousarray(x[k]) for k in _WEIGHTS}
    arrays["params"], arrays["consts"] = params, consts
    for name, src in (("xT", "x"), ("ctxT", "ctx"), ("ctx2T", "ctx_2")):
        arrays[name] = np.ascontiguousarray(x[src][0].T)
    return arrays, at, cat


def kernel(**inputs):
    import concourse.bacc as bacc
    from concourse.bass_utils import run_bass_kernel_spmd

    arrays, at, cat = lay_out(inputs)
    nc = bacc.Bacc("TRN2", target_bir_lowering=False, num_devices=1)
    A = {k: nc.dram_tensor(f"in_{k}", v.shape, F32, kind="ExternalInput").ap() for k, v in arrays.items()}
    A["out"] = nc.dram_tensor("out", (D, NL), F32, kind="ExternalOutput").ap()
    program(nc, A, at, cat)
    r = run_bass_kernel_spmd(nc, [{f"in_{k}": v for k, v in arrays.items()}], core_ids=[0])
    return np.ascontiguousarray(np.asarray(r.results[0]["out"]).T)[None]
```

```python
from contextlib import ExitStack

import numpy as np

import concourse.bass as bass
from concourse import mybir

F32 = mybir.dt.float32
F32R = mybir.dt.float32r
ALU = mybir.AluOpType
ACT = mybir.ActivationFunctionType
AX = mybir.AxisListType

P = 128
D = 1024
KD = D // P
NC_, NL = 256, 512
T = NC_ + NL
TT = T // P
CTX, LAT, ALL = slice(0, NC_), slice(NC_, T), slice(0, T)
GRID_W = 64
EPS = 1e-6
GN_EPS = 64e-5
HEADS0 = 8
D_FF = 2816
KF = D_FF // P
XPAD = 2 + NC_ + 4 + NL + 2
CTX_AT, LAT_AT = 2, NC_ + 6
MLA_HEADS, NOPE, ROPE, VH = 16, 64, 32, 64
CHUNK = 64
EXPERTS, CAP = 16, 64
RING, SLOT = 4, 2048


def columns(v):
    return np.ascontiguousarray(v, dtype=np.float32).reshape(-1, P).T


def spread(v):
    return np.broadcast_to(np.asarray(v).reshape(1, -1), (P, np.asarray(v).size))


def lay_params(x):
    at, cols, n = {}, [], 0
    pairs = {"cond1": ("c", "c_ctx"), "cond2": ("c_2", "c_ctx_2")}
    items = [(k, np.stack([columns(x[a].reshape(-1)), columns(x[b].reshape(-1))], -1).reshape(P, -1))
             for k, (a, b) in pairs.items()]
    items += [("b_ada0", columns(x["b_ada"][0])), ("b_ada1", columns(x["b_ada"][1])),
              ("b_ada2", columns(x["ada_b_2"][0]))]
    items += [("conv_w", np.concatenate([columns(x["ssd_conv_w"][0, j]) for j in range(5)], 1)),
              ("conv_b", columns(x["ssd_conv_b"][0])),
              ("ssd_norm", columns(x["ssd_norm_w"][0])), ("gn0", columns(x["ret_gn_w"][0])),
              ("ssd_d", columns(np.repeat(x["ssd_d"][0], 64))),
              ("dt_bias", spread(x["ssd_dt_bias"][0])), ("a_log", spread(x["ssd_a_log"][0])),
              ("decay_logit", spread(x["ret_decay_logit"][0])),
              ("q_norm", columns(x["mla_q_norm_w"][0])), ("kv_norm", columns(x["mla_kv_norm_w"][0])),
              ("final_norm", columns(x["final_norm_w"])),
              ("norm1_g", columns(x["norm1_g_2"][0])), ("norm2_g", columns(x["norm2_g_2"][0])),
              ("shift_mu", columns(x["shift_mu_2"][0])),
              ("w0", np.concatenate([columns(x["w0_2"][0, d]) for d in range(2)], 1)),
              ("a0", np.concatenate([columns(x["a0_2"][0, d]) for d in range(2)], 1)),
              ("k_k", columns(x["k_k_2"][0])), ("k_a", columns(x["k_a_2"][0])),
              ("r_k", columns(x["r_k_2"][0].reshape(-1))),
              ("gn_g", columns(x["gn_g_2"][0])), ("gn_b", columns(x["gn_b_2"][0])),
              ("conv3", np.concatenate([columns(x["conv_w_2"][0, j]) for j in range(3)], 1)),
              ("final_g", columns(x["final_g_2"]))]
    for name, a in items:
        at[name] = (n, a.shape[1])
        cols.append(a)
        n += a.shape[1]
    return np.ascontiguousarray(np.concatenate(cols, 1), dtype=np.float32), at


def constants():
    p = np.arange(P)[:, None]
    f = np.arange(P)[None, :]
    out = {}
    out["ident"] = (p == f)
    out["ones"] = np.ones((P, P))
    out["blk64"] = (p // 64 == f // 64)
    out["upto"] = (p <= f)
    out["before"] = (p < f)
    half = 32
    sw = np.zeros((P, P))
    for m in range(P):
        base, r = m // 64 * 64, m % 64
        if r < half:
            sw[base + r + half, m] = -1.0
        else:
            sw[base + r - half, m] = 1.0
    out["swap0"] = sw
    sw = np.zeros((P, 64))
    for b in (0, 32, 64, 96):
        for m in range(32):
            if m < 16:
                sw[b + m + 16, m] = -1.0
            else:
                sw[b + m - 16, m] = 1.0
    out["swap1"] = sw
    row = np.repeat(np.arange(NL // GRID_W), GRID_W).astype(np.float32)
    col = np.tile(np.arange(GRID_W), NL // GRID_W).astype(np.float32)
    for name, rot in (("0", 64), ("1", 32)):
        nf = rot // 4
        inv = (np.float32(10000.0) ** (-np.arange(nf, dtype=np.float32) / nf)).astype(np.float32)
        ang = np.concatenate([row[:, None] * inv, col[:, None] * inv], -1).astype(np.float32)
        which = np.arange(P) % (rot // 2)
        out["cos" + name] = np.cos(ang).T[which]
        out["sin" + name] = np.sin(ang).T[which]
    d1 = np.arange(896)[None, :] - 384 - p
    out["ahead"] = np.maximum(d1, 0)
    out["behind"] = np.maximum(-d1, 0)
    d2 = np.arange(640)[None, :] - 128 - p
    out["gap_f"] = d2 + NC_
    out["lower"] = (f >= p)
    out["upper"] = (f < p)
    for r in range(16):
        out[f"row{r}"] = np.broadcast_to(p == r, (P, P))
    q = p % 64
    g = np.arange(64)[None, :]
    fwd = [q < g, q <= g]
    bwd = [q > g, q >= g]
    out["pairs"] = np.concatenate([np.concatenate(fwd, 1), np.concatenate(bwd, 1)], 1)
    levels = []
    for size in (1, 2, 4, 8, 16, 32):
        same = (q // (2 * size) == g // (2 * size))
        low = same & (q // size % 2 == 0) & (g // size % 2 == 1)
        up = same & (q // size % 2 == 1) & (g // size % 2 == 0)
        levels += [low, up]
    out["levels"] = np.concatenate(levels, 1)
    out["eye64"] = (q == g)
    out["iota64"] = np.broadcast_to(g, (P, 64))
    out["restart"] = np.broadcast_to((np.arange(256)[None, :] % 64 != 0), (P, 256))
    out["restart_b"] = np.broadcast_to((np.arange(256)[None, :] % 64 != 63), (P, 256))
    out["mod4"] = (p % 4 == np.arange(4)[None, :])
    out["mod2"] = (p % 2 == np.arange(2)[None, :])
    small = np.zeros((P, 8))
    small[:, 0], small[:, 1], small[:, 2], small[:, 3] = EPS, GN_EPS, 1.0, 0.0
    small[:, 4], small[:, 5] = 1e-24, 10 * np.log(2.0)
    out["small"] = small
    at, cols, n = {}, [], 0
    for k, a in out.items():
        at[k] = (n, a.shape[1])
        cols.append(a.astype(np.float32))
        n += a.shape[1]
    return np.ascontiguousarray(np.concatenate(cols, 1), dtype=np.float32), at


class Stage:

    def __init__(self, prog, name):
        self.prog, self.name, self.kept, self.sems = prog, name, ExitStack(), []

    def __enter__(self):
        return self

    def sem(self, name):
        s = self.kept.enter_context(self.prog.nc.semaphore(f"{self.name}_{name}"))
        self.sems.append(s)
        return s

    def begin(self, pool):
        if self.prog.last_stage:
            for s in self.prog.last_stage.sems:
                pool.sem_clear(s)

    def __exit__(self, *_):
        if self.prog.last_stage:
            self.prog.last_stage.kept.close()
        self.prog.last_stage = self


class Chain:

    def __init__(self, engine, sem):
        self.engine, self.sem, self.n = engine, sem, 0

    def done(self, ins):
        self.n += 1
        ins.then_inc(self.sem, 1)
        return self.n

    def settle(self):
        self.engine.wait_ge(self.sem, self.n)

    def link(self, ins):
        self.done(ins)
        self.settle()


class Weights:

    def __init__(self):
        self.entries, self.before, self.freed, self.landed = [], [0], [], []
        self.issued, self.slot_count = 0, [0] * RING

    def add(self, parts, uses, also=0):
        n = len(self.entries)
        self.entries.append(parts)
        self.before.append(self.before[-1] + uses)
        self.freed.append(self.before[-1] + also)
        self.slot_count[n % RING] += 16 * len(parts)
        self.landed.append(self.slot_count[n % RING])

    def add_block(self, src, kt, cols, uses, also=0):
        self.add([(src, kt, cols, 0)], uses, also)

    def slot(self, n, kt=8, cols=256, at=0):
        return self.ring[:, n % RING, at:at + kt * cols].rearrange("p (k n) -> p k n", k=kt)

    def arrived(self, pe, n, more=0):
        pe.wait_ge(self.landed_sems[n % RING], self.landed[n] + more)

    def feed(self, sp, end):
        while self.issued < min(end + RING, len(self.entries)):
            n = self.issued
            if n >= RING:
                sp.wait_ge(self.product_done, self.freed[n - RING])
            self.load(sp, n)

    def load(self, sp, n):
        for src, kt, cols, at in self.entries[n]:
            sp.dma_start(self.slot(n, kt, cols, at), src).then_inc(self.landed_sems[n % RING], 16)
        self.issued = n + 1


class Prog:
    def __init__(self, nc):
        self.nc, self.last_stage = nc, None
        self.w = Weights()


class Split:

    def __init__(self, g, st, mem, name, n0, src_hi, src_lo):
        self.g, self.n0, self.src = g, n0, (src_hi, src_lo)
        self.parts = [mem.enter_context(g.nc.sbuf_tensor(f"{name}_w_{n}", [P, 2, SLOT], F32R)) for n in ("hi", "lo")]
        self.hi_made, self.lo_made = st.sem("hi_made"), st.sem("lo_made")

    def place(self, n, part):
        m = sum(kt * cols for _, kt, cols, _ in self.g.w.entries[n])
        return self.parts[part][:, (n - self.n0) % 2, 0:m]

    def own(self, n):
        m = sum(kt * cols for _, kt, cols, _ in self.g.w.entries[n])
        return self.g.w.ring[:, n % RING, 0:m]

    def make_hi(self, act, n, landed=0, done=None):
        w = self.g.w
        w.arrived(act, n, landed)
        if n >= self.n0 + 2:
            act.wait_ge(w.product_done, done(w.freed[n - 2]) if done else w.freed[n - 2])
        act.activation(self.place(n, 0), self.own(n), ACT.Copy).then_inc(self.hi_made, 1)

    def make_lo(self, pool, n, made):
        pool.wait_ge(self.hi_made, made)
        pool.tensor_tensor(self.place(n, 1), self.own(n), self.place(n, 0).bitcast(F32), ALU.subtract).then_inc(self.lo_made, 1)

    def weight(self, n, part, kt=8, cols=256, at=0):
        return self.parts[part][:, (n - self.n0) % 2, at:at + kt * cols].rearrange("p (k n) -> p k n", k=kt)

    def source(self, part, k, toks):
        return self.src[part][:, k, toks]


PRODUCTS = ((0, 0), (0, 1), (1, 0))


def k_major(ap, c0, c1, k0=0, k1=None):
    k1 = ap.shape[0] // P if k1 is None else k1
    return ap[k0 * P:k1 * P, c0:c1].rearrange("(k p) n -> p k n", p=P)


def plan_weights(g, A):
    w, first = g.w, {}

    def ada(name, ap):
        first[name] = len(w.entries)
        for e in range(24):
            w.add_block(k_major(ap, 256 * e, 256 * e + 256), 8, 256, 1)

    def ffn(name, l):
        first[name + "_up"] = len(w.entries)
        for m in range(KF):
            w.add([(k_major(A["w_ffn_gate"][l], P * m, P * m + P), 8, P, 0),
                   (k_major(A["w_ffn_up"][l], P * m, P * m + P), 8, P, KD * P)], 1)
        first[name + "_down"] = len(w.entries)
        for m in range(8):
            for half in range(2):
                w.add_block(k_major(A["w_ffn_down"][l], P * m, P * m + P, 11 * half, 11 * half + 11), 11, P, half, 1 - half)

    def plain(name, ap, widths, uses):
        first[name] = len(w.entries)
        c = 0
        for width, u in zip(widths, uses):
            w.add_block(k_major(ap, c, c + width), ap.shape[0] // P, width, u)
            c += width

    ada("ada0", A["w_ada"][0])
    plain("in0", A["ret_ssd_w_in"][0], [256] * 14 + [16], [2] * 4 + [6, 6] + [2] * 8 + [6])
    plain("out0", A["ret_ssd_w_out"][0], [256] * 4, [2] * 4)
    ffn("ffn0", 0)
    ada("ada1", A["w_ada"][1])
    plain("in1", A["mla_w_in"][0], [256] * 4 + [32], [2] * 4 + [1])
    first["heads"] = len(w.entries)
    for h in range(MLA_HEADS):
        w.add([(k_major(A["mla_w_uq"][0], 96 * h, 96 * h + 96), 6, 96, 0),
               (k_major(A["mla_w_ukv"][0], 128 * h, 128 * h + 128), 2, 128, 576)], 1)
    plain("out1", A["mla_w_out"][0], [256] * 4, [2] * 4)
    ffn("ffn1", 1)
    ada("ada2", A["ada_w_2"][0])
    plain("in2", A["w_in_2"][0], [256] * 13, [2] * 13)
    plain("out2", A["w_out_2"][0], [256] * 4, [2] * 4)
    first["experts"] = len(w.entries)
    for e in range(EXPERTS):
        for half in range(2):
            for name in ("exp_w_gate_2", "exp_w_up_2"):
                for c in range(2):
                    lo = 512 * half + 256 * c
                    w.add_block(k_major(A[name][0, e], lo, lo + 256), 8, 256, 1)
        for c in range(4):
            w.add_block(k_major(A["exp_w_down_2"][0, e], 256 * c, 256 * c + 256), 8, 256, 1)
    return first


def vector_memory(g, A):
    nc, keep = g.nc, g.keep

    def sb(name, shape):
        return keep.enter_context(nc.sbuf_tensor(name, shape, F32))

    g.h = sb("h", [P, KD, T])
    g.params = sb("params", [P, A["params"].shape[1]])
    g.basic = sb("basic", [P, 2 * P + 8])
    g.ident, g.ones = g.basic[:, 0:P], g.basic[:, P:2 * P]
    g.eps, g.gn_eps = g.basic[:, 2 * P:2 * P + 1], g.basic[:, 2 * P + 1:2 * P + 2]
    g.one, g.tiny = g.basic[:, 2 * P + 2:2 * P + 3], g.basic[:, 2 * P + 4:2 * P + 5]
    g.zero = g.basic[:, 2 * P + 3:2 * P + 4]
    g.mod = sb("mod", [P, 6 * KD, 2])
    g.cond = sb("cond", [P, 2, KD, 2])
    g.w.ring = sb("weight_ring", [P, RING, SLOT])
    g.ps = keep.enter_context(nc.psum_tensor("ps", [P, 8, 512], F32))
    g.w.product_done = keep.enter_context(nc.semaphore("product_done"))
    g.w.landed_sems = [keep.enter_context(nc.semaphore(f"weights_landed{i}")) for i in range(RING)]
    g.out_stored = keep.enter_context(nc.semaphore("out_stored"))


def col(g, name, i=0, n=None):
    at, width = g.at[name]
    return g.params[:, at + i:at + (width if n is None else i + n)]


def load_const(g, eng, tile, name, sem):
    at, width = g.cat[name]
    eng.dma_start(tile, g.A["consts"][:, at:at + width]).then_inc(sem, 16)


def stage_start(g, A):
    with Stage(g, "start") as st:
        params_in, tokens_in = st.sem("params_in"), st.sem("tokens_in")
        with g.nc.Block() as block:
            @block.sync
            def _(sp):
                sp.dma_start(g.params[:, :], A["params"]).then_inc(params_in, 16)
                for name, lo, hi in (("ident", 0, P), ("ones", P, 2 * P), ("small", 2 * P, 2 * P + 8)):
                    load_const(g, sp, g.basic[:, lo:hi], name, params_in)
                sp.dma_start(g.h[:, :, LAT], A["xT"].rearrange("(k p) t -> p k t", p=P)).then_inc(tokens_in, 16)
                sp.dma_start(g.h[:, :, CTX], A["ctxT"].rearrange("(k p) t -> p k t", p=P)).then_inc(tokens_in, 16)
                g.w.feed(sp, 0)
                sp.wait_ge(tokens_in, 32)

            @block.scalar
            def _(act):
                act.wait_ge(params_in, 64)
                for b, name in enumerate(("cond1", "cond2")):
                    nc_out = g.cond[:, b].rearrange("p k w -> p (k w)")
                    act.activation(nc_out, col(g, name), ACT.Silu)


def stage_ada(g, name, bias, cond, gains=(None, None)):
    w, n0 = g.w, g.first[name]
    base = w.before[n0]
    TURN = 8
    with Stage(g, name) as st, ExitStack() as mem:
        rows = mem.enter_context(g.nc.sbuf_tensor(f"{name}_rows", [2, 256 * TURN], F32))
        mod_step, rows_ready, turned = st.sem("mod_step"), st.sem("rows_ready"), st.sem("turned")
        with g.nc.Block() as block:
            @block.sync
            def _(sp):
                w.feed(sp, n0 + 24)

            @block.tensor
            def _(pe):
                with pe.Fori(0, 24 // TURN) as i:
                    for e in range(TURN):
                        w.arrived(pe, n0 + e, i * (16 * TURN // RING))
                        for k in range(KD):
                            mm = pe.matmul(g.ps[0:2, e // 2, 256 * (e % 2):256 * (e % 2) + 256], g.cond[:, cond, k, :],
                                           w.slot(n0 + e)[:, k, :], start=(k == 0), stop=(k == KD - 1))
                        mm.then_inc(w.product_done, 1)
                    pe.wait_ge(rows_ready, i * 4 + 4)
                    for q in range(2 * TURN):
                        mm = pe.matmul(g.ps[:, 7, bass.ds(i * (4 * TURN) + 2 * q, 2)], rows[:, P * q:P * q + P], g.ident[0:2, 0:2],
                                       start=True, stop=True)
                    mm.then_inc(turned, 1)

            @block.scalar
            def _(act):
                with act.Fori(0, 24 // TURN) as i:
                    for b in range(4):
                        act.wait_ge(w.product_done, i * TURN + (base + 2 * b + 2))
                        act.activation(rows[:, 512 * b:512 * b + 512], g.ps[0:2, b, :], ACT.Copy).then_inc(rows_ready, 1)
                    act.wait_ge(turned, i + 1)

            @block.vector
            def _(dve):
                step = Chain(dve, mod_step)
                dve.wait_ge(turned, 24 // TURN)
                b = col(g, bias).unsqueeze(2).to_broadcast([P, 48, 2])
                step.link(dve.tensor_tensor(g.mod[:, :, :], g.ps[:, 7, 0:96].rearrange("p (m w) -> p m w", w=2), b, ALU.add))
                for j, gain in zip((1, 4), gains):
                    part = g.mod[:, j * KD:j * KD + KD, :]
                    step.done(dve.tensor_scalar(part, part, 1.0, None, ALU.add))
                step.settle()
                for j, gain in zip((1, 4), gains):
                    if gain is not None:
                        part = g.mod[:, j * KD:j * KD + KD, :]
                        step.done(dve.tensor_tensor(part, part, col(g, gain).unsqueeze(2).to_broadcast([P, KD, 2]), ALU.mult))

            @block.gpsimd
            def _(pool):
                st.begin(pool)


def norm_parts(g, j, both):
    parts = [(LAT, lambda k: g.mod[:, (j + 1) * KD + k, 0:1], lambda k: g.mod[:, j * KD + k, 0:1])]
    if both:
        parts.append((CTX, lambda k: g.mod[:, (j + 1) * KD + k, 1:2], lambda k: g.mod[:, j * KD + k, 1:2]))
    return parts


def stage_norm(g, name, src, dst, nk, parts, store=None, upper=None):
    lo, hi = min(t.start for t, _, _ in parts), max(t.stop for t, _, _ in parts)
    shifted = parts[0][2] is not None
    with Stage(g, name) as st, ExitStack() as mem:
        sq = mem.enter_context(g.nc.sbuf_tensor(f"{name}_sq", [P, 2, T], F32))
        rs = mem.enter_context(g.nc.sbuf_tensor(f"{name}_rs", [P, T], F32))
        squared, summed = st.sem("squared"), st.sem("summed")
        root_step, scaled, ready, rounded = (st.sem(n) for n in ("root_step", "scaled", "ready", "rounded"))
        rest = {"dve": st.sem("rest_dve"), "pool": st.sem("rest_pool")}
        if upper is not None:
            whole = mem.enter_context(g.nc.sbuf_tensor(f"{name}_whole", [P, 4, T], F32))

        def work(k, toks):
            return dst[:, k, toks] if upper is None else whole[:, k % 4, toks]

        def take_rest(engine, k):
            engine.wait_ge(rounded, k + 1)
            engine.tensor_tensor(dst[:, k, lo:hi], whole[:, k % 4, lo:hi], upper[:, k, lo:hi].bitcast(F32),
                                 ALU.subtract).then_inc(rest["pool" if k % 4 else "dve"], 1)

        with g.nc.Block() as block:
            @block.scalar
            def _(act):
                for k in range(nk):
                    if k >= 2:
                        act.wait_ge(summed, k - 1)
                    act.activation(sq[:, k % 2, lo:hi], src[:, k, lo:hi], ACT.Square).then_inc(squared, 1)
                act.wait_ge(summed, nk)
                step = Chain(act, root_step)
                for b, (toks, _, _) in enumerate(parts):
                    n = toks.stop - toks.start
                    step.done(act.activation(rs[:, toks], g.ps[:, b, 0:n], ACT.Ln, bias=g.eps, scale=1.0 / (nk * P)))
                step.settle()
                step.done(act.activation(rs[:, lo:hi], rs[:, lo:hi], ACT.Exp, scale=-0.5))
                if shifted:
                    for k in range(nk):
                        for b, (toks, _, shift) in enumerate(parts):
                            act.wait_ge(scaled, len(parts) * k + b + 1)
                            act.activation(work(k, toks), work(k, toks), ACT.Identity, bias=shift(k)).then_inc(ready, 1)

            @block.tensor
            def _(pe):
                for k in range(nk):
                    pe.wait_ge(squared, k + 1)
                    for b, (toks, _, _) in enumerate(parts):
                        mm = pe.matmul(g.ps[:, b, 0:toks.stop - toks.start], g.ones, sq[:, k % 2, toks],
                                       start=(k == 0), stop=(k == nk - 1))
                    mm.then_inc(summed, 1)

            @block.vector
            def _(dve):
                dve.wait_ge(root_step, len(parts) + 1)
                def round_off(k):
                    dve.wait_ge(ready, len(parts) * (k + 1))
                    dve.tensor_copy(upper[:, k, lo:hi], whole[:, k % 4, lo:hi]).then_inc(rounded, 1)
                    if k % 4 == 0:
                        take_rest(dve, k)

                for k in range(nk):
                    if upper is not None and k >= 4:
                        q = k - 4
                        dve.wait_ge(rest["pool" if q % 4 else "dve"], q // 4 * 3 + q % 4 if q % 4 else q // 4 + 1)
                    for toks, gain, _ in parts:
                        dve.scalar_tensor_tensor(work(k, toks), src[:, k, toks], gain(k), rs[:, toks],
                                                 ALU.mult, ALU.mult).then_inc(scaled, 1)
                    if upper is not None and k >= 2:
                        round_off(k - 2)
                if upper is not None:
                    for k in (nk - 2, nk - 1):
                        round_off(k)

            @block.gpsimd
            def _(pool):
                st.begin(pool)
                if upper is not None:
                    for k in range(nk):
                        if k % 4:
                            take_rest(pool, k)

            @block.sync
            def _(sp):
                if store is not None:
                    for k in range(nk):
                        sp.wait_ge(scaled, k + 1)
                        sp.dma_start(store[k * P:k * P + P, :], dst[:, k, parts[0][0]]).then_inc(g.out_stored, 16)
                    sp.wait_ge(g.out_stored, 16 * nk)


def stage_project(g, name, groups, end, split=None):
    w = g.w
    base = w.before[groups[0][0]]
    turn = {"act": [0], "dve": [0]}
    for gr in groups:
        for e in turn:
            turn[e].append(turn[e][-1] + (gr[3] == e))
    with Stage(g, name) as st, ExitStack() as mem:
        read = {"act": st.sem("act_read"), "dve": st.sem("dve_read")}
        entries = sorted({gr[0] for gr in groups})
        sp_ = Split(g, st, mem, name, entries[0], *split) if split else None
        with g.nc.Block() as block:
            @block.sync
            def _(sp):
                w.feed(sp, end)

            @block.tensor
            def _(pe):
                last = None
                for j, (n, kt, outs, _, _) in enumerate(groups):
                    if n != last:
                        if split:
                            pe.wait_ge(sp_.lo_made, n - entries[0] + 1)
                        else:
                            w.arrived(pe, n)
                        last = n
                    if j >= 4:
                        who = groups[j - 4][3]
                        pe.wait_ge(read[who], turn[who][j - 3])
                    for out, lhsT, rhs in outs(2 * (j % 4), sp_):
                        for k in range(kt):
                            if split:
                                for wt, sr in PRODUCTS:
                                    mm = pe.matmul(out, lhsT(k, wt, sr), rhs(k, wt, sr), start=(k == 0 and wt + sr == 0),
                                                   stop=(k == kt - 1 and wt == 1))
                            else:
                                mm = pe.matmul(out, lhsT(k), rhs(k), start=(k == 0), stop=(k == kt - 1))
                    mm.then_inc(w.product_done, 1)

            def take(engine, who):
                begun = set()
                for j, gr in enumerate(groups):
                    if split and who == "act" and gr[0] not in begun:
                        for n in [gr[0] + 1] if begun else [gr[0], gr[0] + 1]:
                            if n <= entries[-1]:
                                sp_.make_hi(engine, n)
                        begun.add(gr[0])
                    if gr[3] == who:
                        engine.wait_ge(w.product_done, base + j + 1)
                        gr[4](engine, 2 * (j % 4)).then_inc(read[who], 1)

            @block.scalar
            def _(act):
                take(act, "act")

            @block.vector
            def _(dve):
                take(dve, "dve")

            @block.gpsimd
            def _(pool):
                st.begin(pool)
                for n in entries if split else ():
                    sp_.make_lo(pool, n, n - entries[0] + 1)


def feature_group(g, n, kt, c0, src, both, who, evacuate, m=P, width=256):
    def outs(b, sp_):
        def lhsT(k, wt=0, sr=0):
            return (sp_.weight(n, wt, kt, width) if sp_ else g.w.slot(n, kt, width))[:, k, c0:c0 + m]

        def rhs(toks):
            return lambda k, wt=0, sr=0: sp_.source(sr, k, toks) if sp_ else src[:, k, toks]
        made = [(g.ps[0:m, b, 0:NL], lhsT, rhs(LAT))]
        if both:
            made.append((g.ps[0:m, b + 1, 0:NC_], lhsT, rhs(CTX)))
        return made
    return (n, kt, outs, who, evacuate)


def token_group(g, n, kt, c0, width, slot_width, src, tile, who, evacuate):
    def outs(b, sp_):
        toks = slice(P * tile, P * tile + P)

        def lhsT(k, wt=0, sr=0):
            return sp_.source(sr, k, toks) if sp_ else src[:, k, toks]

        def rhs(k, wt=0, sr=0):
            return (sp_.weight(n, wt, kt, slot_width) if sp_ else g.w.slot(n, kt, slot_width))[:, k, c0:c0 + width]
        return [(g.ps[:, b, 0:width], lhsT, rhs)]
    return (n, kt, outs, who, evacuate)


def copy_act(g, dst, both, func=ACT.Copy, scale=1.0, m=P):
    def go(act, b):
        for bank, toks in ((b, LAT), (b + 1, CTX))[:2 if both else 1]:
            ins = act.activation(dst(toks), g.ps[0:m, bank, 0:toks.stop - toks.start], func, scale=scale)
        return ins
    return go


def copy_dve(g, dst, both, scale=1.0, m=P):
    def go(dve, b):
        for bank, toks in ((b, LAT), (b + 1, CTX))[:2 if both else 1]:
            ins = dve.tensor_scalar(dst(toks), g.ps[0:m, bank, 0:toks.stop - toks.start], scale, None, ALU.mult)
        return ins
    return go


def add_gated(g, j, m, both):
    def go(dve, b):
        for bank, toks, wch in ((b, LAT, 0), (b + 1, CTX, 1))[:2 if both else 1]:
            hk = g.h[:, m, toks]
            ins = dve.scalar_tensor_tensor(hk, g.ps[:, bank, 0:toks.stop - toks.start],
                                           g.mod[:, j * KD + m, wch:wch + 1], hk, ALU.mult, ALU.add)
        return ins
    return go


def stage_out(g, name, src, both, j=2):
    n0 = g.first[name]
    groups = [feature_group(g, n0 + m // 2, KD, P * (m % 2), src, both, "dve", add_gated(g, j, m, both))
              for m in range(KD)]
    stage_project(g, name, groups, n0 + 4)


def stage_ffn(g, name, src, src_hi, both):
    w = g.w
    ups, downs = g.first[name + "_up"], g.first[name + "_down"]
    parts = ((0, LAT, 0), (1, CTX, 1))[:2 if both else 1]
    with Stage(g, name) as st, ExitStack() as mem:
        hid = mem.enter_context(g.nc.sbuf_tensor(f"{name}_hid", [P, KF, T], F32))
        silu_ready, hid_ready = st.sem("silu_ready"), st.sem("hid_ready")
        sp_ = Split(g, st, mem, name, ups, src_hi, src)
        base = w.before[ups]
        with g.nc.Block() as block:
            def up_tile(pe, t, made, lead):
                pe.wait_ge(sp_.lo_made, made)
                if lead is not None:
                    pe.wait_ge(hid_ready, lead)
                for q in range(2):
                    for b, toks, _ in parts:
                        for k in range(KD):
                            for wt, sr in PRODUCTS:
                                mm = pe.matmul(g.ps[:, 4 * (t % 2) + 2 * q + b, 0:toks.stop - toks.start],
                                               sp_.weight(ups + t, wt, 8, P, KD * P * q)[:, k, :], sp_.source(sr, k, toks),
                                               start=(k == 0 and wt + sr == 0), stop=(k == KD - 1 and wt == 1))
                mm.then_inc(w.product_done, 1)

            @block.sync
            def _(sp):
                w.feed(sp, downs + 16)

            @block.tensor
            def _(pe):
                for t in range(2):
                    up_tile(pe, t, t + 1, None)
                with pe.Fori(0, 5) as i:
                    for r in range(4):
                        up_tile(pe, 2 + r, i * 4 + (3 + r), i * 4 + (1 + r))
                pe.wait_ge(hid_ready, KF)
                with pe.Fori(0, 4) as i:
                    for r in range(2):
                        pe.wait_ge(hid_ready, i * 2 + (KF - 1 + r))
                        for half in range(2):
                            n = downs + 2 * r + half
                            w.arrived(pe, n, i * 16)
                            for b, toks, _ in parts:
                                for k in range(11):
                                    mm = pe.matmul(g.ps[:, 4 * r + b, 0:toks.stop - toks.start],
                                                   w.slot(n, 11, P)[:, k, :], hid[:, 11 * half + k, toks],
                                                   start=(half == 0 and k == 0), stop=(half == 1 and k == 10))
                        mm.then_inc(w.product_done, 1)

            @block.scalar
            def _(act):
                flat = hid[:, :, :].rearrange("p k t -> p (k t)")

                def silu(tile, m, done):
                    act.wait_ge(w.product_done, done)
                    for b, toks, _ in parts:
                        n = toks.stop - toks.start
                        ins = act.activation(flat[:, bass.ds(tile * T + toks.start, n)], g.ps[:, 4 * m + b, 0:n], ACT.Silu)
                    ins.then_inc(silu_ready, 1)

                for t in range(2):
                    sp_.make_hi(act, ups + t)
                for t in range(2):
                    silu(t, t, base + t + 1)
                    sp_.make_hi(act, ups + 2 + t)
                with act.Fori(0, 4) as i:
                    for r in range(4):
                        silu(i * 4 + (2 + r), r % 2, i * 4 + (base + 3 + r))
                        n = ups + 4 + r
                        sp_.make_hi(act, n, i * 32, lambda freed: i * 4 + freed)
                for t in range(18, KF):
                    silu(t, t % 2, base + t + 1)
                    if t < KF - 2:
                        sp_.make_hi(act, ups + t + 2)

            @block.vector
            def _(dve):
                flat = hid[:, :, :].rearrange("p k t -> p (k t)")

                def up(tile, m):
                    dve.wait_ge(silu_ready, tile + 1)
                    for b, toks, _ in parts:
                        n = toks.stop - toks.start
                        own = flat[:, bass.ds(tile * T + toks.start, n)]
                        ins = dve.tensor_tensor(own, own, g.ps[:, 4 * m + 2 + b, 0:n], ALU.mult)
                    ins.then_inc(hid_ready, 1)

                for t in range(2):
                    up(t, t)
                with dve.Fori(0, 5) as i:
                    for r in range(4):
                        up(i * 4 + (2 + r), r % 2)
                base = w.before[downs]
                hf = g.h[:, :, :].rearrange("p k t -> p (k t)")
                mf = g.mod[:, :, :].rearrange("p m w -> p (m w)")
                with dve.Fori(0, 4) as i:
                    for r in range(2):
                        dve.wait_ge(w.product_done, i * 2 + (base + 1 + r))
                        for b, toks, wch in parts:
                            n = toks.stop - toks.start
                            hk = hf[:, bass.ds(i * (2 * T) + (r * T + toks.start), n)]
                            gate = mf[:, bass.ds(i * 4 + (2 * (5 * KD + r) + wch), 1)]
                            ins = dve.scalar_tensor_tensor(hk, g.ps[:, 4 * r + b, 0:n], gate, hk, ALU.mult, ALU.add)
                        ins.then_inc(hid_ready, 1)

            @block.gpsimd
            def _(pool):
                st.begin(pool)
                for t in range(2):
                    sp_.make_lo(pool, ups + t, t + 1)
                with pool.Fori(0, 5) as i:
                    for r in range(4):
                        sp_.make_lo(pool, ups + 2 + r, i * 4 + (3 + r))


def stage_in0(g, a, qk, gz, v, raw, dt_raw):
    n0 = g.first["in0"]
    groups = []
    for e in range(4):
        for m in range(2):
            tile = 2 * e + m
            scale = 1.0 if tile < 4 else 64 ** -0.5
            def dst(toks, tile=tile):
                return qk[:, tile, toks]
            make = copy_act if tile % 2 else copy_dve
            groups.append(feature_group(g, n0 + e, KD, P * m, a, True, "act" if tile % 2 else "dve", make(g, dst, True, scale=scale)))
    for e in range(2):
        for tile in range(TT):
            def take(dve, b, e=e, tile=tile):
                return dve.tensor_copy(v[:, tile, 256 * e:256 * e + 256], g.ps[:, b, 0:256])
            groups.append(token_group(g, n0 + 4 + e, KD, 0, 256, 256, a, tile, "dve", take))
    for e in range(4):
        for m in range(2):
            def dst(toks, tile=2 * e + m):
                return gz[:, tile, toks]
            groups.append(feature_group(g, n0 + 6 + e, KD, P * m, a, True, "act", copy_act(g, dst, True, func=ACT.Silu)))
    for e in range(4):
        for m in range(2):
            def dst(toks, tile=2 * e + m):
                at = LAT_AT if toks is LAT else CTX_AT
                return raw[:, tile, at:at + toks.stop - toks.start]
            groups.append(feature_group(g, n0 + 10 + e, KD, P * m, a, True, "dve" if m else "act",
                                        (copy_dve if m else copy_act)(g, dst, True)))
    for tile in range(TT):
        def take(dve, b, tile=tile):
            return dve.tensor_copy(dt_raw[:, tile, :], g.ps[:, b, 0:16])
        groups.append(token_group(g, n0 + 14, KD, 0, 16, 16, a, tile, "dve", take))
    stage_project(g, "in0", groups, n0 + 15)


def stage_rope0(g, qk):
    with Stage(g, "rope0") as st, ExitStack() as mem:
        swap = mem.enter_context(g.nc.sbuf_tensor("rope0_swap", [P, P], F32))
        cs = mem.enter_context(g.nc.sbuf_tensor("rope0_cs", [P, 2, NL], F32))
        t = mem.enter_context(g.nc.sbuf_tensor("rope0_t", [P, 2, NL], F32))
        tables_in, swapped, dve_step = st.sem("tables_in"), st.sem("swapped"), st.sem("dve_step")
        with g.nc.Block() as block:
            @block.sync
            def _(sp):
                load_const(g, sp, swap[:, :], "swap0", tables_in)
                load_const(g, sp, cs[:, 0, :], "cos0", tables_in)
                load_const(g, sp, cs[:, 1, :], "sin0", tables_in)

            @block.tensor
            def _(pe):
                pe.wait_ge(tables_in, 48)
                for m in range(8):
                    pe.matmul(g.ps[:, m, :], swap[:, :], qk[:, m, LAT], start=True, stop=True).then_inc(swapped, 1)

            @block.vector
            def _(dve):
                step = Chain(dve, dve_step)
                dve.wait_ge(tables_in, 48)
                for m in range(8):
                    dve.wait_ge(swapped, m + 1)
                    step.done(dve.tensor_tensor(t[:, 0, :], g.ps[:, m, :], cs[:, 1, :], ALU.mult))
                    step.link(dve.tensor_tensor(t[:, 1, :], qk[:, m, LAT], cs[:, 0, :], ALU.mult))
                    step.link(dve.tensor_tensor(qk[:, m, LAT], t[:, 0, :], t[:, 1, :], ALU.add))

            @block.gpsimd
            def _(pool):
                st.begin(pool)


def stage_conv0(g, raw, xbc):
    n = XPAD - 4
    with Stage(g, "conv0") as st, ExitStack() as mem:
        acc = mem.enter_context(g.nc.sbuf_tensor("conv0_acc", [P, 2, n], F32))
        tap, summed, taken = st.sem("tap"), st.sem("summed"), st.sem("taken")
        padded = st.sem("padded")
        with g.nc.Block() as block:
            @block.gpsimd
            def _(pool):
                st.begin(pool)
                for lo, hi in ((0, 2), (2 + NC_, LAT_AT), (LAT_AT + NL, XPAD)):
                    ins = pool.memset(raw[:, :, lo:hi], 0.0)
                ins.then_inc(padded, 1)

            @block.vector
            def _(dve):
                step = Chain(dve, tap)
                dve.wait_ge(padded, 1)
                for m in range(8):
                    if m >= 2:
                        dve.wait_ge(taken, m - 1)
                    step.link(dve.tensor_scalar(acc[:, m % 2, :], raw[:, m, 0:n], col(g, "conv_w", m, 1), None, ALU.mult))
                    for j in range(1, 4):
                        step.link(dve.scalar_tensor_tensor(acc[:, m % 2, :], raw[:, m, j:j + n], col(g, "conv_w", 8 * j + m, 1),
                                                           acc[:, m % 2, :], ALU.mult, ALU.add))
                    dve.scalar_tensor_tensor(acc[:, m % 2, :], raw[:, m, 4:4 + n], col(g, "conv_w", 32 + m, 1),
                                             acc[:, m % 2, :], ALU.mult, ALU.add).then_inc(summed, 1)

            @block.scalar
            def _(act):
                for m in range(8):
                    act.wait_ge(summed, m + 1)
                    for toks, at in ((CTX, CTX_AT - 2), (LAT, LAT_AT - 2)):
                        ins = act.activation(xbc[:, m, toks], acc[:, m % 2, at:at + toks.stop - toks.start], ACT.Silu,
                                             bias=col(g, "conv_b", m, 1))
                    ins.then_inc(taken, 1)


def stage_decays0(g, dt_raw, dt, cum, cumT, ret_la, xbc, xs_tok):
    with Stage(g, "decays0") as st, ExitStack() as mem:
        tmp = mem.enter_context(g.nc.sbuf_tensor("decays0_tmp", [P, 4, 112], F32))
        tri = mem.enter_context(g.nc.sbuf_tensor("decays0_tri", [P, 2, P], F32))
        tables_in, prepared, exped, logged = st.sem("tables_in"), st.sem("prepared"), st.sem("exped"), st.sem("logged")
        dve_step, act_step, la_ready, summed = st.sem("dve_step"), st.sem("act_step"), st.sem("la_ready"), st.sem("summed")
        cum_ready, rows_made, x_turned, x_taken = st.sem("cum_ready"), st.sem("rows_made"), st.sem("x_turned"), st.sem("x_taken")
        x, small, la = tmp[:, 0, :], tmp[:, 1, :], tmp[:, 3, :]
        neg_a = tmp[:, 2, 0:16]
        n = 16 * TT
        with g.nc.Block() as block:
            @block.sync
            def _(sp):
                load_const(g, sp, tri[:, 0, :], "upto", tables_in)
                load_const(g, sp, tri[:, 1, :], "before", tables_in)

            @block.gpsimd
            def _(pool):
                st.begin(pool)

            @block.vector
            def _(dve):
                step = Chain(dve, dve_step)
                bias = col(g, "dt_bias").unsqueeze(1).to_broadcast([P, TT, 16])
                step.done(dve.tensor_tensor(x[:, 0:n].rearrange("p (t h) -> p t h", h=16), dt_raw[:, :, :], bias, ALU.add))
                step.link(dve.tensor_scalar(x[:, n:n + 16], col(g, "decay_logit"), -1.0, None, ALU.mult))
                dve.scalar_tensor_tensor(small, x, -1.0, x, ALU.mult, ALU.max).then_inc(prepared, 1)
                dve.wait_ge(logged, 1)
                step.link(dve.scalar_tensor_tensor(x, x, 0.0, small, ALU.max, ALU.add))
                step.done(dve.tensor_copy(dt[:, :, :], x[:, 0:n].rearrange("p (t h) -> p t h", h=16)))
                step.done(dve.tensor_scalar(ret_la[:, 0:16], x[:, n:n + 16], -1.0, None, ALU.mult))
                step.done(dve.tensor_scalar(neg_a, neg_a, -1.0, None, ALU.mult))
                step.settle()
                dve.tensor_tensor(la[:, 0:n].rearrange("p (t h) -> p t h", h=16), dt[:, :, :],
                                  neg_a.unsqueeze(1).to_broadcast([P, TT, 16]), ALU.mult).then_inc(la_ready, 1)
                step.done(dve.tensor_scalar(ret_la[:, 16:24], ret_la[:, 8:16], -1.0, None, ALU.mult))
                step.done(dve.tensor_scalar(ret_la[:, 24:32], ret_la[:, 8:16], float(T), None, ALU.mult))
                dve.wait_ge(summed, 1)
                sums = g.ps[:, 7, 0:n].rearrange("p (t h) -> p t h", h=16)
                step.link(dve.tensor_copy(cum[:, 0], sums))
                dve.tensor_scalar(cum[:, 1], cum[:, 0], -1.0, None, ALU.mult).then_inc(cum_ready, 1)
                dve.wait_ge(rows_made, 1)
                dve.tensor_copy(cumT[:, LAT], g.ps[0:16, 5, 0:NL]).then_inc(dve_step, 1)
                dve.tensor_copy(cumT[:, CTX], g.ps[0:16, 6, 0:NC_]).then_inc(dve_step, 1)

            @block.scalar
            def _(act):
                step = Chain(act, act_step)
                step.done(act.activation(neg_a, col(g, "a_log"), ACT.Exp))
                act.wait_ge(prepared, 1)
                step.link(act.activation(small, small, ACT.Exp, scale=-1.0))
                act.activation(small, small, ACT.Ln, bias=g.one).then_inc(logged, 1)
                for tile in range(TT):
                    act.wait_ge(x_turned, tile + 1)
                    act.activation(xs_tok[:, tile, :], g.ps[:, tile % 2, :], ACT.Copy).then_inc(x_taken, 1)

            @block.tensor
            def _(pe):
                for tile in range(TT):
                    if tile >= 2:
                        pe.wait_ge(x_taken, tile - 1)
                    for m in range(4):
                        mm = pe.transpose(g.ps[:, tile % 2, P * m:P * m + P], xbc[:, m, P * tile:P * tile + P], g.ident)
                    mm.then_inc(x_turned, 1)
                pe.wait_ge(tables_in, 32)
                pe.wait_ge(la_ready, 1)
                for order, tiles, own in ((0, range(TT), 0), (8, (2, 3, 4, 5, 0, 1), 1)):
                    for at, tile in enumerate(tiles):
                        out = g.ps[:, 7, 16 * tile + order:16 * tile + order + 8]
                        for before in tiles[:at]:
                            pe.matmul(out, g.ones, la[:, 16 * before + order:16 * before + order + 8],
                                      start=(before == tiles[0]), stop=False)
                        mm = pe.matmul(out, tri[:, own, :], la[:, 16 * tile + order:16 * tile + order + 8],
                                       start=(at == 0), stop=True)
                mm.then_inc(summed, 1)
                pe.wait_ge(cum_ready, 1)
                for tile in range(TT):
                    bank, at = (6, P * tile) if tile < 2 else (5, P * (tile - 2))
                    mm = pe.transpose(g.ps[0:16, bank, at:at + P], cum[:, 0, tile, :], g.ident)
                mm.then_inc(rows_made, 1)


def score_tiles():
    out = []
    for jt in range(TT):
        out.append((jt, LAT))
        if jt < 2:
            out.append((jt, CTX))
    return out


def scan_pe(g, pe, heads, kq, values, sems, first_of_head=None):
    scores_ready, probs_ready, sums_ready, sums_read = sems
    tiles = score_tiles()
    blocks = [(hi, u) for hi in range(len(heads)) for u in range(len(tiles))]

    def scores(n):
        hi, u = blocks[n]
        jt, toks = tiles[u]
        if n >= 4:
            pe.wait_ge(probs_ready, n - 3)
        k, q = kq(heads[hi])
        pe.matmul(g.ps[:, n % 4, 0:toks.stop - toks.start], k(slice(P * jt, P * jt + P)), q(toks),
                  start=True, stop=True).then_inc(scores_ready, 1)

    for n in range(3):
        scores(n)
    for n, (hi, u) in enumerate(blocks):
        if n + 3 < len(blocks):
            scores(n + 3)
        if u == 0:
            if first_of_head:
                first_of_head(hi)
            if hi > 0:
                pe.wait_ge(sums_read, hi)
        jt, toks = tiles[u]
        h = heads[hi]
        p0 = 64 * (h % 2)
        bank = 4 if toks is LAT else 5
        pe.wait_ge(probs_ready, n + 1)
        mm = pe.matmul(g.ps[p0:p0 + 64, bank, 0:toks.stop - toks.start], values(h, jt),
                       g.probs[:, n % 4, 0:toks.stop - toks.start], start=(jt == 0), stop=(jt == (TT - 1 if toks is LAT else 1)))
        mm.then_inc(sums_ready, 1)


def take_sums(g, act, heads, y, sems):
    sums_ready, sums_read = sems
    n = len(score_tiles())
    for hi, h in enumerate(heads):
        yield hi
        act.wait_ge(sums_ready, n * (hi + 1))
        p0 = 64 * (h % 2)
        act.activation(y[p0:p0 + 64, h // 2, CTX], g.ps[p0:p0 + 64, 5, 0:NC_], ACT.Copy)
        act.activation(y[p0:p0 + 64, h // 2, LAT], g.ps[p0:p0 + 64, 4, 0:NL], ACT.Copy).then_inc(sums_read, 1)


def stage_retention(g, qk, v, ret_la):
    with Stage(g, "ret") as st, ExitStack() as mem:
        def sb(name, n):
            return mem.enter_context(g.nc.sbuf_tensor(f"ret_{name}", [P, n], F32))
        ahead, behind, gap = sb("ahead", 896), sb("behind", 896), sb("gap", 640)
        near = [sb(f"near{i}", 896) for i in range(2)]
        far = [sb(f"far{i}", 640) for i in range(2)]
        far_b = [sb(f"far_b{i}", 640) for i in range(2)]
        names = ("tables_in", "scores_ready", "probs_ready", "sums_ready", "sums_read",
                 "powers_ready", "near_ready", "far_ready", "dve_step")
        (tables_in, scores_ready, probs_ready, sums_ready, sums_read,
         powers_ready, near_ready, far_ready, dve_step) = (st.sem(n) for n in names)
        heads = list(range(HEADS0))
        tiles = score_tiles()
        nt = len(tiles)
        with g.nc.Block() as block:
            @block.sync
            def _(sp):
                load_const(g, sp, ahead[:, :], "ahead", tables_in)
                load_const(g, sp, behind[:, :], "behind", tables_in)
                load_const(g, sp, gap[:, :], "gap_f", tables_in)

            @block.gpsimd
            def _(pool):
                st.begin(pool)

            @block.tensor
            def _(pe):
                def kq(h):
                    p0, t = 64 * (h % 2), h // 2
                    return (lambda s: qk[p0:p0 + 64, 4 + t, s]), (lambda s: qk[p0:p0 + 64, t, s])
                scan_pe(g, pe, heads, kq, lambda h, jt: v[:, jt, 64 * h:64 * h + 64],
                        (scores_ready, probs_ready, sums_ready, sums_read))

            @block.scalar
            def _(act):
                def decays(h):
                    act.wait_ge(powers_ready, h + 1)
                    act.activation(near[h % 2][:, :], near[h % 2][:, :], ACT.Exp).then_inc(near_ready, 1)
                    act.activation(far[h % 2][:, :], gap[:, :], ACT.Exp, scale=ret_la[:, h:h + 1])
                    act.activation(far_b[h % 2][:, :], gap[:, :], ACT.Exp, scale=ret_la[:, 16 + h:17 + h],
                                   bias=ret_la[:, 24 + h:25 + h]).then_inc(far_ready, 1)
                decays(0)
                for hi in take_sums(g, act, heads, qk, (sums_ready, sums_read)):
                    if hi + 1 < HEADS0:
                        decays(hi + 1)

            @block.vector
            def _(dve):
                step = Chain(dve, dve_step)

                def powers(h):
                    step.link(dve.tensor_scalar(near[h % 2][:, :], behind[:, :], ret_la[:, 8 + h:9 + h], None, ALU.mult))
                    dve.scalar_tensor_tensor(near[h % 2][:, :], ahead[:, :], ret_la[:, h:h + 1], near[h % 2][:, :],
                                             ALU.mult, ALU.add).then_inc(powers_ready, 1)
                dve.wait_ge(tables_in, 48)
                powers(0)
                for h in range(HEADS0):
                    if h + 1 < HEADS0:
                        if h >= 1:
                            dve.wait_ge(probs_ready, nt * h)
                        powers(h + 1)
                    dve.wait_ge(near_ready, h + 1)
                    dve.wait_ge(far_ready, h + 1)
                    step.link(dve.tensor_tensor(far[h % 2][:, :], far[h % 2][:, :], far_b[h % 2][:, :], ALU.add))
                    for u, (jt, toks) in enumerate(tiles):
                        n = nt * h + u
                        dve.wait_ge(scores_ready, n + 1)
                        if n >= 4:
                            dve.wait_ge(sums_ready, n - 3)
                        width = toks.stop - toks.start
                        if jt < 2 and toks is LAT:
                            dec = far[h % 2][:, P - P * jt:P - P * jt + width]
                        else:
                            own = jt if jt < 2 else jt - 2
                            dec = near[h % 2][:, 384 - P * own:384 - P * own + width]
                        dve.tensor_tensor(g.probs[:, n % 4, 0:width], g.ps[:, n % 4, 0:width], dec, ALU.mult).then_inc(probs_ready, 1)


def stage_ssd(g, xbc, qk, dt, cum, cumT, xs_tok):
    with Stage(g, "ssd") as st, ExitStack() as mem:
        def sb(name, shape):
            return mem.enter_context(g.nc.sbuf_tensor(f"ssd_{name}", [P] + shape, F32))
        select = mem.enter_context(g.nc.sbuf_tensor("ssd_select", [16, 16, P], F32))
        tri = sb("tri", [2, P])
        rows = sb("rows", [2, T])
        diag = sb("diag", [TT, 2, P])
        wd = sb("wd", [TT, P])
        off = sb("off", [2, 2 * NL + P])
        wf = sb("wf", [2, NL])
        names = ("tables_in", "scores_ready", "probs_ready", "sums_ready", "sums_read",
                 "rows_made", "rows_read", "expo_ready", "diag_ready", "off_ready", "dve_step")
        (tables_in, scores_ready, probs_ready, sums_ready, sums_read, rows_made, rows_read,
         expo_ready, diag_ready, off_ready, dve_step) = (st.sem(n) for n in names)
        heads = list(range(HEADS0))
        tiles = score_tiles()
        nt = len(tiles)

        upto = [sum(1 for j, _ in tiles if j <= jt) for jt in range(TT)]

        with g.nc.Block() as block:
            @block.sync
            def _(sp):
                for r in range(16):
                    at, width = g.cat[f"row{r}"]
                    sp.dma_start(select[:, r, :], g.A["consts"][0:16, at:at + width]).then_inc(tables_in, 16)
                load_const(g, sp, tri[:, 0, :], "lower", tables_in)
                load_const(g, sp, tri[:, 1, :], "upper", tables_in)

            @block.gpsimd
            def _(pool):
                st.begin(pool)

            @block.tensor
            def _(pe):
                pe.wait_ge(tables_in, 16 * 18)

                def make_row(n):
                    if n > 0:
                        pe.wait_ge(rows_read, n)
                    r = 8 * (n % 2) + heads[n // 2]
                    pe.matmul(g.ps[:, 6, 0:NL], select[:, r, :], cumT[:, LAT], start=True, stop=True)
                    pe.matmul(g.ps[:, 7, 0:NC_], select[:, r, :], cumT[:, CTX], start=True, stop=True).then_inc(rows_made, 1)

                def next_rows(hi):
                    make_row(2 * hi + 1)
                    if hi + 1 < HEADS0:
                        make_row(2 * hi + 2)
                make_row(0)

                def kq(h):
                    grp = h // 4
                    return (lambda s: xbc[:, 4 + grp, s]), (lambda s: xbc[:, 6 + grp, s])
                scan_pe(g, pe, heads, kq, lambda h, jt: xs_tok[:, jt, 64 * h:64 * h + 64],
                        (scores_ready, probs_ready, sums_ready, sums_read),
                        first_of_head=next_rows)

            @block.scalar
            def _(act):
                def take_rows(h):
                    for d in range(2):
                        act.wait_ge(rows_made, 2 * h + d + 1)
                        if d == 0 and h > 0:
                            act.wait_ge(expo_ready, h)
                            act.wait_ge(off_ready, 6 * h)
                        sign = 1.0 - 2.0 * d
                        act.activation(rows[:, d, LAT], g.ps[:, 6, 0:NL], ACT.Copy, scale=sign)
                        ins = act.activation(rows[:, d, CTX], g.ps[:, 7, 0:NC_], ACT.Copy, scale=sign)
                        ins.then_inc(rows_read, 1)

                def offs(h, jt):
                    m = 6 * h + jt
                    if m >= 2:
                        hu, ju = (m - 2) // 6, (m - 2) % 6
                        act.wait_ge(probs_ready, nt * hu + upto[ju])
                    nc_j, e_j = cum[:, 1, jt, h:h + 1], cum[:, 0, jt, 8 + h:9 + h]
                    o = off[:, m % 2]
                    if jt < 2:
                        act.activation(o[:, 0:NL], rows[:, 0, LAT], ACT.Exp, bias=nc_j)
                        act.activation(o[:, NL:2 * NL], rows[:, 1, LAT], ACT.Exp, bias=e_j)
                        other = rows[:, 0, P:2 * P] if jt == 0 else rows[:, 1, 0:P]
                        last = act.activation(o[:, 2 * NL:], other, ACT.Exp, bias=nc_j if jt == 0 else e_j)
                    else:
                        lo, hi = P * (jt - 2), P * (jt - 1)
                        if hi < NL:
                            last = act.activation(o[:, hi:NL], rows[:, 0, NC_ + hi:T], ACT.Exp, bias=nc_j)
                        if lo > 0:
                            last = act.activation(o[:, 0:lo], rows[:, 1, NC_:NC_ + lo], ACT.Exp, bias=e_j)
                    last.then_inc(off_ready, 1)

                for h in range(HEADS0):
                    take_rows(h)
                    if h > 0:
                        act.wait_ge(sums_ready, nt * h)
                        hp = h - 1
                        p0 = 64 * (hp % 2)
                        act.activation(qk[p0:p0 + 64, 4 + hp // 2, CTX], g.ps[p0:p0 + 64, 5, 0:NC_], ACT.Copy)
                        act.activation(qk[p0:p0 + 64, 4 + hp // 2, LAT], g.ps[p0:p0 + 64, 4, 0:NL], ACT.Copy).then_inc(sums_read, 1)
                    act.wait_ge(expo_ready, h + 1)
                    act.activation(diag[:, :, :, :], diag[:, :, :, :], ACT.Exp).then_inc(diag_ready, 1)
                    for jt in range(TT):
                        offs(h, jt)
                act.wait_ge(sums_ready, nt * HEADS0)
                act.activation(qk[64:128, 7, CTX], g.ps[64:128, 5, 0:NC_], ACT.Copy)
                act.activation(qk[64:128, 7, LAT], g.ps[64:128, 4, 0:NL], ACT.Copy).then_inc(sums_read, 1)

            @block.vector
            def _(dve):
                step = Chain(dve, dve_step)
                dve.wait_ge(tables_in, 16 * 18)
                for h in range(HEADS0):
                    dve.wait_ge(rows_read, 2 * h + 2)
                    for jt in range(TT):
                        own = slice(P * jt, P * jt + P)
                        dve.tensor_scalar(diag[:, jt, 0, :], rows[:, 0, own], cum[:, 1, jt, h:h + 1], 0.0, ALU.add, ALU.min)
                        ins = dve.tensor_scalar(diag[:, jt, 1, :], rows[:, 1, own], cum[:, 0, jt, 8 + h:9 + h], 0.0, ALU.add, ALU.min)
                    ins.then_inc(expo_ready, 1)
                    dve.wait_ge(diag_ready, h + 1)
                    for jt in range(TT):
                        for d in range(2):
                            ins = dve.scalar_tensor_tensor(diag[:, jt, d, :], diag[:, jt, d, :], dt[:, jt, 8 * d + h:8 * d + h + 1],
                                                           tri[:, d, :], ALU.mult, ALU.mult)
                    step.link(ins)
                    step.link(dve.tensor_tensor(wd[:, :, :], diag[:, :, 0, :], diag[:, :, 1, :], ALU.add))
                    for u, (jt, toks) in enumerate(tiles):
                        n = nt * h + u
                        m = 6 * h + jt
                        o = off[:, m % 2]
                        dtf, dtb = dt[:, jt, h:h + 1], dt[:, jt, 8 + h:9 + h]
                        if toks is LAT:
                            dve.wait_ge(off_ready, m + 1)
                        dve.wait_ge(scores_ready, n + 1)
                        if n >= 4:
                            dve.wait_ge(sums_ready, n - 3)
                        prob, score = g.probs[:, n % 4], g.ps[:, n % 4]
                        if jt < 2 and toks is LAT:
                            step.link(dve.tensor_scalar(wf[:, 1, :], o[:, NL:2 * NL], dtb, None, ALU.mult))
                            step.link(dve.scalar_tensor_tensor(wf[:, 0, :], o[:, 0:NL], dtf, wf[:, 1, :], ALU.mult, ALU.add))
                            dve.tensor_tensor(prob[:, 0:NL], score[:, 0:NL], wf[:, 0, :], ALU.mult).then_inc(probs_ready, 1)
                            continue
                        own = P * (jt if jt < 2 else jt - 2)
                        if toks is CTX:
                            parts = [(P - own, o[:, 2 * NL:], dtf if jt == 0 else dtb, P)]
                        else:
                            parts = [(own + P, o[:, own + P:NL], dtf, NL - own - P), (0, o[:, 0:own], dtb, own)]
                        for c0, dec, scale, width in parts:
                            if width:
                                dve.scalar_tensor_tensor(prob[:, c0:c0 + width], dec, scale, score[:, c0:c0 + width], ALU.mult, ALU.mult)
                        dve.tensor_tensor(prob[:, own:own + P], score[:, own:own + P], wd[:, jt, :], ALU.mult).then_inc(probs_ready, 1)


def stage_finish0(g, qk, gz, xbc):
    with Stage(g, "finish0") as st, ExitStack() as mem:
        blk = mem.enter_context(g.nc.sbuf_tensor("finish0_blk", [P, P], F32))
        sq = mem.enter_context(g.nc.sbuf_tensor("finish0_sq", [P, 2, T], F32))
        rs = mem.enter_context(g.nc.sbuf_tensor("finish0_rs", [P, 2, T], F32))
        table_in, summed, centred, squared = st.sem("table_in"), st.sem("summed"), st.sem("centred"), st.sem("squared")
        squares_summed, rooted, act_step, dve_step = (st.sem("squares_summed"), st.sem("rooted"), st.sem("act_step"), st.sem("dve_step"))
        halves = ((0, LAT), (1, CTX))
        with g.nc.Block() as block:
            @block.sync
            def _(sp):
                load_const(g, sp, blk[:, :], "blk64", table_in)

            @block.gpsimd
            def _(pool):
                st.begin(pool)

            @block.tensor
            def _(pe):
                pe.wait_ge(table_in, 16)
                for m in range(4):
                    for b, toks in halves:
                        mm = pe.matmul(g.ps[:, 2 * (m % 2) + b, 0:toks.stop - toks.start], blk[:, :], qk[:, m, toks], start=True, stop=True)
                    mm.then_inc(summed, 1)
                    pe.wait_ge(squared, m + 1)
                    if m >= 2:
                        pe.wait_ge(rooted, m - 1)
                    for b, toks in halves:
                        mm = pe.matmul(g.ps[:, 4 + 2 * (m % 2) + b, 0:toks.stop - toks.start], blk[:, :], sq[:, m % 2, toks], start=True, stop=True)
                    mm.then_inc(squares_summed, 1)

            @block.scalar
            def _(act):
                step = Chain(act, act_step)
                for m in range(4):
                    act.wait_ge(centred, m + 1)
                    act.activation(sq[:, m % 2, :], qk[:, m, :], ACT.Square).then_inc(squared, 1)
                    act.wait_ge(squares_summed, m + 1)
                    if m >= 2:
                        act.wait_ge(dve_step, 2 * (m - 1))
                    for b, toks in halves:
                        ins = act.activation(rs[:, m % 2, toks], g.ps[:, 4 + 2 * (m % 2) + b, 0:toks.stop - toks.start], ACT.Ln,
                                             bias=g.eps, scale=1.0 / 64)
                    step.link(ins)
                    act.activation(rs[:, m % 2, :], rs[:, m % 2, :], ACT.Exp, scale=-0.5).then_inc(rooted, 1)

            @block.vector
            def _(dve):
                step = Chain(dve, dve_step)
                for m in range(4):
                    dve.wait_ge(summed, m + 1)
                    for b, toks in halves:
                        ins = dve.scalar_tensor_tensor(qk[:, m, toks], g.ps[:, 2 * (m % 2) + b, 0:toks.stop - toks.start], -1.0 / 64,
                                                       qk[:, m, toks], ALU.mult, ALU.add)
                    ins.then_inc(centred, 1)
                    dve.wait_ge(rooted, m + 1)
                    step.link(dve.scalar_tensor_tensor(qk[:, m, :], qk[:, m, :], col(g, "gn0", m, 1), rs[:, m % 2, :], ALU.mult, ALU.mult))
                    step.link(dve.tensor_tensor(qk[:, m, :], qk[:, m, :], gz[:, m, :], ALU.mult))
                for m in range(4):
                    y = qk[:, 4 + m, :]
                    step.link(dve.scalar_tensor_tensor(y, xbc[:, m, :], col(g, "ssd_d", m, 1), y, ALU.mult, ALU.add))
                    step.link(dve.tensor_tensor(y, y, gz[:, 4 + m, :], ALU.mult))


def first_layer(g):
    stage_ada(g, "ada0", "b_ada0", 0)
    with ExitStack() as mem:
        def sb(name, shape):
            return mem.enter_context(g.nc.sbuf_tensor(name, [P] + shape, F32))
        a = sb("a0", [KD, T])
        qk = sb("qk0", [8, T])
        gz = sb("gz0", [8, T])
        v = sb("v0", [TT, 512])
        dt_raw = sb("dt_raw", [TT, 16])
        with ExitStack() as raw_mem:
            raw = raw_mem.enter_context(g.nc.sbuf_tensor("xbc_raw", [P, 8, XPAD], F32))
            stage_norm(g, "norm0a", g.h, a, KD, norm_parts(g, 0, True))
            stage_in0(g, a, qk, gz, v, raw, dt_raw)
            stage_conv0(g, raw, a)
        stage_rope0(g, qk)
        xs_tok, dt = sb("xs_tok", [TT, 512]), sb("dt", [TT, 16])
        cum, ret_la = sb("cum", [2, TT, 16]), sb("ret_la", [32])
        cumT = mem.enter_context(g.nc.sbuf_tensor("cumT", [16, T], F32))
        stage_decays0(g, dt_raw, dt, cum, cumT, ret_la, a, xs_tok)
        g.probs = mem.enter_context(g.nc.sbuf_tensor("probs", [P, 4, NL], F32))
        stage_retention(g, qk, v, ret_la)
        stage_ssd(g, a, qk, dt, cum, cumT, xs_tok)
        stage_finish0(g, qk, gz, a)
        stage_norm(g, "norm0s", qk[:, 4:8, :], qk[:, 4:8, :], 4,
                   [(t, lambda k: col(g, "ssd_norm", k, 1), None) for t in (LAT, CTX)])
        stage_out(g, "out0", qk, True)
    with ExitStack() as mem:
        a_hi, a_lo = (mem.enter_context(g.nc.sbuf_tensor(f"a0f_{n}", [P, KD, T], F32R)) for n in ("hi", "lo"))
        stage_norm(g, "norm0b", g.h, a_lo, KD, norm_parts(g, 3, True), upper=a_hi)
        stage_ffn(g, "ffn0", a_lo, a_hi, True)


def stage_in1(g, a_lo, a_hi, cq, ckv, kpe):
    n0 = g.first["in1"]
    groups = []
    for tile in range(8):
        who = "act" if tile % 2 else "dve"
        make = copy_act if tile % 2 else copy_dve
        if tile < 6:
            def dst(toks, tile=tile):
                return cq[:, tile, :]
        else:
            def dst(toks, tile=tile):
                return ckv[:, tile - 6, toks]
        groups.append(feature_group(g, n0 + tile // 2, KD, P * (tile % 2), None, tile >= 6, who, make(g, dst, tile >= 6)))

    def outs(b, sp_):
        def lhsT(k, wt, sr):
            return sp_.weight(n0 + 4, wt, KD, ROPE)[:, k, :]

        def rhs(toks):
            return lambda k, wt, sr: sp_.source(sr, k, toks)
        return [(g.ps[0:32, b, 0:NL], lhsT, rhs(LAT)), (g.ps[0:32, b + 1, 0:NC_], lhsT, rhs(CTX))]

    def take(act, b):
        act.activation(kpe[64:96, LAT], g.ps[0:32, b, 0:NL], ACT.Copy)
        return act.activation(kpe[64:96, CTX], g.ps[0:32, b + 1, 0:NC_], ACT.Copy)
    groups.append((n0 + 4, KD, outs, "act", take))
    stage_project(g, "in1", groups, n0 + 5, (a_hi, a_lo))


def stage_heads(g, cq, ckv, kpe, o_tok):
    w, n0 = g.w, g.first["heads"]
    base = w.before[n0]
    scale = float(NOPE + ROPE) ** -0.5
    HALF = T // 2
    with Stage(g, "heads") as st, ExitStack() as mem:
        def sb(name, shape):
            return mem.enter_context(g.nc.sbuf_tensor(f"heads_{name}", [P] + shape, F32))
        q = [sb(f"q{i}", [NL]) for i in range(2)]
        k = [sb(f"k{i}", [T]) for i in range(2)]
        v = [sb(f"v{i}", [TT, VH + 1]) for i in range(2)]
        probs = sb("probs", [TT, NL])
        swap, cs, t = sb("swap", [2 * ROPE]), sb("cs", [2, NL]), sb("t", [2, NL])
        neg_max, denom = sb("neg_max", [2, 4]), sb("denom", [4])
        names = ("tables_in", "fixed_ready", "kpe_swapped", "kpe_roped", "q_copied", "k_copied", "kv_copied", "q_swapped", "q_roped",
                 "scored", "max_done", "rows_made", "row_copied", "keyed", "exp_done", "summed", "o_done", "dve_step")
        (tables_in, fixed_ready, kpe_swapped, kpe_roped, q_copied, k_copied, kv_copied, q_swapped, q_roped,
         scored, max_done, rows_made, row_copied, keyed, exp_done, summed, o_done, dve_step) = (st.sem(n) for n in names)

        def at(i, r, per, more):
            return i * (4 * per) + (per * r + more)

        def all_heads(engine, body):
            with engine.Fori(0, 3) as i:
                for r in range(4):
                    body(i, r, True)
            for r in range(4):
                body(3, r, r < 3)

        pe_rows = slice(64, 96)
        with g.nc.Block() as block:
            @block.sync
            def _(sp):
                load_const(g, sp, swap[:, :], "swap1", tables_in)
                load_const(g, sp, cs[:, 0, :], "cos1", tables_in)
                load_const(g, sp, cs[:, 1, :], "sin1", tables_in)
                w.feed(sp, n0 + MLA_HEADS)

            @block.gpsimd
            def _(pool):
                st.begin(pool)

            @block.tensor
            def _(pe):
                def project(i, r):
                    n, b = n0 + r, r % 2
                    w.arrived(pe, n, i * 32)
                    wq, wkv = w.slot(n, 6, 96), w.slot(n, 2, P, 576)
                    for kk in range(6):
                        pe.matmul(g.ps[0:96, 0, :], wq[:, kk, :], cq[:, kk, :], start=(kk == 0), stop=(kk == 5))
                    for bank, toks in ((1, LAT), (2, CTX)):
                        for kk in range(2):
                            pe.matmul(g.ps[0:64, bank, 0:toks.stop - toks.start], wkv[:, kk, 0:64], ckv[:, kk, toks],
                                      start=(kk == 0), stop=(kk == 1))
                    for tile in range(TT):
                        for kk in range(2):
                            mm = pe.matmul(g.ps[:, 3, VH * tile:VH * tile + VH], ckv[:, kk, P * tile:P * tile + P],
                                           wkv[:, kk, 64:128], start=(kk == 0), stop=(kk == 1))
                    mm.then_inc(w.product_done, 1)

                def swap_q(i, r):
                    pe.wait_ge(q_copied, at(i, r, 1, 1))
                    pe.matmul(g.ps[64:128, 0, :], swap[pe_rows, :], q[r % 2][pe_rows, :], start=True, stop=True).then_inc(q_swapped, 1)

                def body(i, r, more):
                    b = r % 2
                    pe.wait_ge(q_roped, at(i, r, 1, 1))
                    pe.wait_ge(k_copied, at(i, r, 1, 1))
                    pe.wait_ge(kv_copied, at(i, r, 1, 1))
                    for qt in range(4):
                        if qt >= 2:
                            pe.wait_ge(max_done, at(i, r, 4, qt - 1))
                        for s in range(2):
                            mm = pe.matmul(g.ps[:, 4 + 2 * (qt % 2) + s, 0:HALF], q[b][0:96, P * qt:P * qt + P],
                                           k[b][0:96, HALF * s:HALF * s + HALF], start=True, stop=True)
                        mm.then_inc(scored, 1)
                    if more:
                        project(i, r + 1)
                    pe.wait_ge(max_done, at(i, r, 4, 4))
                    for qt in range(4):
                        mm = pe.matmul(g.ps[96:97, 4, P * qt:P * qt + P], neg_max[:, b, qt:qt + 1], g.ident, start=True, stop=True)
                    mm.then_inc(rows_made, 1)
                    pe.wait_ge(row_copied, at(i, r, 1, 1))
                    for kt in range(TT):
                        if kt >= 3:
                            pe.wait_ge(exp_done, at(i, r, TT, kt - 2))
                        pe.matmul(g.ps[:, 5 + kt % 3, :], k[b][0:97, P * kt:P * kt + P], q[b][0:97, :], start=True, stop=True).then_inc(keyed, 1)
                    if more:
                        swap_q(i, r + 1)
                    pe.wait_ge(exp_done, at(i, r, TT, TT))
                    for qt in range(4):
                        for kt in range(TT):
                            mm = pe.matmul(g.ps[:, 4, P * qt:P * qt + VH + 1], probs[:, kt, P * qt:P * qt + P], v[b][:, kt, :],
                                           start=(kt == 0), stop=(kt == TT - 1))
                    mm.then_inc(summed, 1)
                    pe.wait_ge(o_done, at(i, r, 1, 1))

                pe.wait_ge(tables_in, 48)
                pe.matmul(g.ps[64:128, 4, :], swap[pe_rows, :], kpe[pe_rows, LAT], start=True, stop=True).then_inc(kpe_swapped, 1)
                project(0, 0)
                swap_q(0, 0)
                pe.wait_ge(fixed_ready, 4)
                pe.wait_ge(kpe_roped, 2)
                all_heads(pe, body)

            @block.scalar
            def _(act):
                def take(i, r):
                    b = r % 2
                    act.wait_ge(w.product_done, at(i, r, 1, base + 1))
                    act.activation(q[b][0:96, :], g.ps[0:96, 0, :], ACT.Copy).then_inc(q_copied, 1)
                    act.activation(k[b][0:64, LAT], g.ps[0:64, 1, :], ACT.Copy).then_inc(k_copied, 1)

                def body(i, r, more):
                    b = r % 2
                    if more:
                        take(i, r + 1)
                    act.wait_ge(rows_made, at(i, r, 1, 1))
                    act.activation(q[b][96:97, :], g.ps[96:97, 4, :], ACT.Copy).then_inc(row_copied, 1)
                    for kt in range(TT):
                        act.wait_ge(keyed, at(i, r, TT, kt + 1))
                        act.activation(probs[:, kt, :], g.ps[:, 5 + kt % 3, :], ACT.Exp, scale=scale).then_inc(exp_done, 1)
                take(0, 0)
                all_heads(act, body)

            @block.vector
            def _(dve):
                step = Chain(dve, dve_step)

                def rope(x, swapped):
                    dve.tensor_tensor(t[pe_rows, 0, :], swapped, cs[pe_rows, 1, :], ALU.mult)
                    return dve.tensor_tensor(t[pe_rows, 1, :], x, cs[pe_rows, 0, :], ALU.mult)

                def take(i, r):
                    b = r % 2
                    dve.wait_ge(w.product_done, at(i, r, 1, base + 1))
                    dve.tensor_copy(k[b][0:64, CTX], g.ps[0:64, 2, 0:NC_])
                    dve.tensor_copy(v[b][:, :, 0:VH], g.ps[:, 3, 0:TT * VH].rearrange("p (t e) -> p t e", e=VH)).then_inc(kv_copied, 1)

                def rope_q(i, r, first=False):
                    b = r % 2
                    dve.wait_ge(q_swapped, at(i, r, 1, 1))
                    rope(q[b][pe_rows, :], g.ps[pe_rows, 0, :]).then_inc(dve_step, 1)
                    dve.wait_ge(dve_step, at(i, r, 2, 2 if first else 1))
                    dve.tensor_tensor(q[b][pe_rows, :], t[pe_rows, 0, :], t[pe_rows, 1, :], ALU.add).then_inc(q_roped, 1)

                def body(i, r, more):
                    b = r % 2
                    for qt in range(4):
                        dve.wait_ge(scored, at(i, r, 4, qt + 1))
                        pair = 4 + 2 * (qt % 2)
                        dve.tensor_reduce(neg_max[:, b, qt:qt + 1], g.ps[:, pair:pair + 2, 0:HALF], AX.XY, ALU.max, negate=True).then_inc(max_done, 1)
                    if more:
                        take(i, r + 1)
                        rope_q(i, r + 1)
                    dve.wait_ge(summed, at(i, r, 1, 1))
                    sums = g.ps[:, 4, :].rearrange("p (t e) -> p t e", e=P)
                    dve.reciprocal(denom[:, :].unsqueeze(2), sums[:, :, VH:VH + 1]).then_inc(dve_step, 1)
                    dve.wait_ge(dve_step, at(i, r, 2, 4 if more else 3))
                    dve.tensor_tensor(o_tok[:, :, bass.ds(at(i, r, VH, 0), VH)], sums[:, :, 0:VH],
                                      denom[:, :].unsqueeze(2).to_broadcast([P, 4, VH]), ALU.mult).then_inc(o_done, 1)

                for b in range(2):
                    dve.memset(k[b][96:97, :], 1.0).then_inc(fixed_ready, 1)
                    dve.memset(v[b][:, :, VH:VH + 1], 1.0).then_inc(fixed_ready, 1)
                dve.wait_ge(tables_in, 48)
                dve.wait_ge(kpe_swapped, 1)
                rope(kpe[pe_rows, LAT], g.ps[pe_rows, 4, :]).then_inc(dve_step, 1)
                dve.wait_ge(dve_step, 1)
                for b in range(2):
                    dve.tensor_copy(k[b][pe_rows, CTX], kpe[pe_rows, CTX])
                    dve.tensor_tensor(k[b][pe_rows, LAT], t[pe_rows, 0, :], t[pe_rows, 1, :], ALU.add).then_inc(kpe_roped, 1)
                take(0, 0)
                dve.wait_ge(kpe_roped, 2)
                rope_q(0, 0, True)
                all_heads(dve, body)


def stage_turn(g, o_tok, oT):
    with Stage(g, "turn") as st:
        turned, taken = st.sem("turned"), st.sem("taken")
        with g.nc.Block() as block:
            @block.gpsimd
            def _(pool):
                st.begin(pool)

            @block.tensor
            def _(pe):
                for m in range(KD):
                    for t in range(4):
                        mm = pe.transpose(g.ps[:, m, P * t:P * t + P], o_tok[:, t, P * m:P * m + P], g.ident)
                    mm.then_inc(turned, 1)

            @block.scalar
            def _(act):
                for m in range(0, KD, 2):
                    act.wait_ge(turned, m + 1)
                    act.activation(oT[:, m, LAT], g.ps[:, m, :], ACT.Copy).then_inc(taken, 1)

            @block.vector
            def _(dve):
                for m in range(1, KD, 2):
                    dve.wait_ge(turned, m + 1)
                    dve.tensor_copy(oT[:, m, LAT], g.ps[:, m, :]).then_inc(taken, 1)


def second_layer(g):
    stage_ada(g, "ada1", "b_ada1", 0)
    with ExitStack() as mem:
        def sb(name, shape):
            return mem.enter_context(g.nc.sbuf_tensor(name, [P] + shape, F32))
        cq, ckv, kpe, o_tok = sb("cq", [6, NL]), sb("ckv", [2, T]), sb("kpe", [T]), sb("o_tok", [4, D])
        with ExitStack() as split_mem:
            a_hi, a_lo = (split_mem.enter_context(g.nc.sbuf_tensor(f"a1_{n}", [P, KD, T], F32R)) for n in ("hi", "lo"))
            stage_norm(g, "norm1a", g.h, a_lo, KD, norm_parts(g, 0, True), upper=a_hi)
            stage_in1(g, a_lo, a_hi, cq, ckv, kpe)
        stage_norm(g, "norm1q", cq, cq, 6, [(slice(0, NL), lambda k: col(g, "q_norm", k, 1), None)])
        stage_norm(g, "norm1kv", ckv, ckv, 2, [(t, lambda k: col(g, "kv_norm", k, 1), None) for t in (LAT, CTX)])
        stage_heads(g, cq, ckv, kpe, o_tok)
        a = sb("a1", [KD, T])
        stage_turn(g, o_tok, a)
        stage_out(g, "out1", a, False)
    with ExitStack() as mem:
        a_hi, a_lo = (mem.enter_context(g.nc.sbuf_tensor(f"a1f_{n}", [P, KD, T], F32R)) for n in ("hi", "lo"))
        stage_norm(g, "norm1b", g.h, a_lo, KD, norm_parts(g, 3, False), upper=a_hi)
        stage_ffn(g, "ffn1", a_lo, a_hi, False)
    stage_norm(g, "norm1f", g.h, g.h, KD, [(LAT, lambda k: col(g, "final_norm", k, 1), None)])


GW, GR = GRID_W, NL // GRID_W
NR = 14
DECAY_FLOOR = float(np.exp(-0.5))


def stage_context2(g, A):
    with Stage(g, "context2") as st:
        context_in = st.sem("context_in")
        with g.nc.Block() as block:
            @block.gpsimd
            def _(pool):
                st.begin(pool)

            @block.sync
            def _(sp):
                sp.dma_start(g.h[:, :, CTX], A["ctx2T"].rearrange("(k p) t -> p k t", p=P)).then_inc(context_in, 16)
                sp.wait_ge(context_in, 16)


def stage_in2(g, a, raw, cv):
    n0 = g.first["in2"]
    groups = []
    for tile in range(26):
        who = "act" if tile % 2 else "dve"
        make = copy_act if tile % 2 else copy_dve
        if tile < NR:
            def dst(toks, tile=tile):
                return raw[:, tile, toks]
        else:
            def dst(toks, tile=tile):
                return cv[:, tile - NR, :]
        groups.append(feature_group(g, n0 + tile // 2, KD, P * (tile % 2), a, tile < NR, who, make(g, dst, tile < NR)))
    stage_project(g, "in2", groups, n0 + 13)


def stage_shift(g, raw, mix, cv, y):
    with Stage(g, "shift") as st, ExitStack() as mem:
        mods = mem.enter_context(g.nc.sbuf_tensor("shift_mods", [P, 6], F32))
        coef = mem.enter_context(g.nc.sbuf_tensor("shift_coef", [P, 7, NR], F32))
        tables_in, dve_step = st.sem("tables_in"), st.sem("dve_step")
        with g.nc.Block() as block:
            @block.gpsimd
            def _(pool):
                st.begin(pool)

            @block.sync
            def _(sp):
                load_const(g, sp, mods[:, 0:4], "mod4", tables_in)
                load_const(g, sp, mods[:, 4:6], "mod2", tables_in)

            @block.vector
            def _(dve):
                step = Chain(dve, dve_step)
                dve.wait_ge(tables_in, 32)
                for d in range(6):
                    step.done(dve.tensor_scalar(coef[:, d, :], col(g, "shift_mu"), mods[:, d:d + 1], None, ALU.mult))
                step.link(dve.tensor_scalar(coef[:, 6, :], col(g, "shift_mu"), -1.0, 1.0, ALU.mult, ALU.add))
                for m in range(NR):
                    step.link(dve.tensor_scalar(mix[:, m, :], raw[:, m, :], coef[:, 6, m:m + 1], None, ALU.mult))

                    def add(to, of, d):
                        return dve.scalar_tensor_tensor(to, of, coef[:, d, m:m + 1], to, ALU.mult, ALU.add)
                    x = raw[:, m, LAT].rearrange("p (r c) -> p r c", c=GW)
                    o = mix[:, m, LAT].rearrange("p (r c) -> p r c", c=GW)
                    xc, oc = raw[:, m, CTX], mix[:, m, CTX]
                    step.link(add(o[:, :, 1:GW], x[:, :, 0:GW - 1], 0))
                    step.done(add(oc[:, 1:NC_], xc[:, 0:NC_ - 1], 4))
                    step.link(add(o[:, :, 0:GW - 1], x[:, :, 1:GW], 1))
                    step.done(add(oc[:, 0:NC_ - 1], xc[:, 1:NC_], 5))
                    step.link(add(o[:, 1:GR, :], x[:, 0:GR - 1, :], 2))
                    step.link(add(o[:, 0:GR - 1, :], x[:, 1:GR, :], 3))
                for m in range(4):
                    b, u, out = cv[:, m, :], cv[:, 4 + m, :], y[:, 4 + m, LAT]
                    step.link(dve.tensor_tensor(u, u, cv[:, 8 + m, :], ALU.mult))
                    step.link(dve.tensor_scalar(out, u, col(g, "conv3", 4 + m, 1), None, ALU.mult))
                    step.link(dve.scalar_tensor_tensor(out[:, 1:NL], u[:, 0:NL - 1], col(g, "conv3", m, 1), out[:, 1:NL], ALU.mult, ALU.add))
                    step.link(dve.scalar_tensor_tensor(out[:, 0:NL - 1], u[:, 1:NL], col(g, "conv3", 8 + m, 1), out[:, 0:NL - 1], ALU.mult, ALU.add))
                    step.link(dve.tensor_tensor(out, out, b, ALU.mult))


def stage_keys(g, mix, nk, ka):
    with Stage(g, "keys") as st, ExitStack() as mem:
        blk = mem.enter_context(g.nc.sbuf_tensor("keys_blk", [P, P], F32))
        sq = mem.enter_context(g.nc.sbuf_tensor("keys_sq", [P, 2, T], F32))
        rs = mem.enter_context(g.nc.sbuf_tensor("keys_rs", [P, 2, T], F32))
        names = ("table_in", "kk_ready", "squared", "summed", "floored", "rooted", "act_step", "dve_step")
        table_in, kk_ready, squared, summed, floored, rooted, act_step, dve_step = (st.sem(n) for n in names)
        halves = ((0, LAT), (1, CTX))
        with g.nc.Block() as block:
            @block.gpsimd
            def _(pool):
                st.begin(pool)

            @block.sync
            def _(sp):
                load_const(g, sp, blk[:, :], "blk64", table_in)

            @block.tensor
            def _(pe):
                pe.wait_ge(table_in, 16)
                for m in range(4):
                    pe.wait_ge(squared, m + 1)
                    if m >= 2:
                        pe.wait_ge(floored, m - 1)
                    for b, toks in halves:
                        mm = pe.matmul(g.ps[:, 2 * (m % 2) + b, 0:toks.stop - toks.start], blk[:, :], sq[:, m % 2, toks], start=True, stop=True)
                    mm.then_inc(summed, 1)

            @block.scalar
            def _(act):
                step = Chain(act, act_step)
                for m in range(4):
                    act.wait_ge(kk_ready, m + 1)
                    if m >= 2:
                        act.wait_ge(summed, m - 1)
                    act.activation(sq[:, m % 2, :], nk[:, m, :], ACT.Square).then_inc(squared, 1)
                step.done(act.activation(mix[0:64, 12, :], mix[0:64, 12, :], ACT.Tanh))
                for m in range(4):
                    act.wait_ge(floored, m + 1)
                    step.link(act.activation(rs[:, m % 2, :], rs[:, m % 2, :], ACT.Ln, scale=2.0 ** 20))
                    act.activation(rs[:, m % 2, :], rs[:, m % 2, :], ACT.Exp, scale=-0.5, bias=g.basic[:, 2 * P + 5:2 * P + 6]).then_inc(rooted, 1)

            @block.vector
            def _(dve):
                step = Chain(dve, dve_step)
                for m in range(4):
                    dve.tensor_scalar(nk[:, m, :], mix[:, 4 + m, :], col(g, "k_k", m, 1), None, ALU.mult).then_inc(kk_ready, 1)
                for m in range(4):
                    step.link(dve.tensor_scalar(ka[:, m, :], mix[:, 4 + m, :], col(g, "k_a", m, 1), None, ALU.mult))
                    step.link(dve.tensor_tensor(mix[:, 4 + m, :], mix[:, 4 + m, :], ka[:, m, :], ALU.subtract))
                for m in range(4):
                    dve.wait_ge(summed, m + 1)
                    if m >= 2:
                        step.settle()
                    for b, toks in halves:
                        ins = dve.tensor_scalar(rs[:, m % 2, toks], g.ps[:, 2 * (m % 2) + b, 0:toks.stop - toks.start], 1e-24, None, ALU.max)
                    ins.then_inc(floored, 1)
                    dve.wait_ge(rooted, m + 1)
                    step.done(dve.scalar_tensor_tensor(nk[:, m, :], nk[:, m, :], -1.0, rs[:, m % 2, :], ALU.mult, ALU.mult))


def stage_recurrence(g, name, steps, fwd_at, bwd_at, mix, nk, ka, state, y):
    with Stage(g, name) as st, ExitStack() as mem:
        def sb(n, shape):
            return mem.enter_context(g.nc.sbuf_tensor(f"{name}_{n}", [P] + shape, F32))
        lora = sb("lora", [2, 512])
        pairs, levels, eye = sb("pairs", [2, P]), sb("levels", [6, 2, 64]), sb("eye", [64])
        restart = sb("restart", [2, 256])
        shape = [2, 4, 64]
        wa = sb("wa", [2, 64])
        wr = sb("wr", [2, 2, 4, 64])
        cum, up, down = sb("cum", shape), sb("up", shape), sb("down", shape)
        ar = sb("ar", [2, 4, 2, 64])
        bt, kt = sb("bt", shape), sb("kt", shape)
        lb, lk = sb("lb", [2, 4, 2, 64]), sb("lk", [2, 4, 2, 64])
        bktok, vtok = sb("bktok", [2, 2, 4, 64]), sb("vtok", shape)
        x, xt, ys = sb("x", shape), sb("xt", shape), sb("ys", shape)
        vs = ys
        lt = sb("lt", [2] + shape)
        u = lt[:, 0]
        names = ("tables_in", "wa_copied", "low_rank_done", "v_turned", "vtok_ready", "biased", "tanhed", "cum_ready", "exps_done",
                 "before_ready", "upx_done", "v_copied", "bt_ready", "kt_ready", "ar_ready", "products_done", "turned", "lb_ready",
                 "x_ready", "tokens_copied", "w_done", "w_copied", "u_done", "u_copied", "y_done", "ds_done", "dve_step")
        sem = {n: st.sem(n) for n in names}
        for l in range(1, 6):
            for n in ("masked", "y", "copied", "summed", "added"):
                sem[f"level{l}_{n}"] = st.sem(f"level{l}_{n}")

        def flat(t):
            return t.rearrange("p m c -> p (m c)")

        def heads():
            for p0 in (0, 64):
                for m in range(4):
                    yield m, slice(p0, p0 + 64)

        def bank(d, b, half=0):
            return g.ps[:, 4 * d + b, 256 * half:256 * half + 256].rearrange("p (m c) -> p m c", m=4)

        def once(i, d):
            return i * 2 + (d + 1)

        with g.nc.Block() as block:
            @block.sync
            def _(sp):
                sp.dma_start(lora[0:64, :, :], g.A["w_lora_up_2"][0].rearrange("d k n -> k d n")).then_inc(sem["tables_in"], 16)
                sp.dma_start(lora[64:128, :, :], g.A["a_lora_up_2"][0].rearrange("d k n -> k d n")).then_inc(sem["tables_in"], 16)
                load_const(g, sp, pairs[:, :, :].rearrange("p a b -> p (a b)"), "pairs", sem["tables_in"])
                load_const(g, sp, levels[:, :, :, :].rearrange("p a b c -> p (a b c)"), "levels", sem["tables_in"])
                load_const(g, sp, eye[:, :], "eye64", sem["tables_in"])
                load_const(g, sp, restart[:, 0, :], "restart", sem["tables_in"])
                load_const(g, sp, restart[:, 1, :], "restart_b", sem["tables_in"])

            @block.gpsimd
            def _(pool):
                st.begin(pool)
                pool.wait_ge(sem["tables_in"], 16 * 7)
                with pool.Fori(0, steps) as i:
                    for l in range(1, 6):
                        for d in range(2):
                            if l == 1:
                                pool.wait_ge(sem["lb_ready"], once(i, d))
                            if l >= 3:
                                pool.wait_ge(sem[f"level{l - 2}_y"], once(i, d))
                            pool.tensor_tensor(lt[:, l % 2, d], lb[:, d, :, 0, :], levels[:, l, d, :].unsqueeze(1).to_broadcast([P, 4, 64]),
                                               ALU.mult).then_inc(sem[f"level{l}_masked"], 1)

            @block.tensor
            def _(pe):
                pe.wait_ge(sem["tables_in"], 16 * 7)
                with pe.Fori(0, steps) as i:
                    def wait(*waits):
                        pe.wait_ge(sem["tables_in"], 16 * 7)
                        for n, count in waits:
                            pe.wait_ge(sem[n], count)
                    for d in range(2):
                        wait(("wa_copied", once(i, d)))
                        for m in range(4):
                            pe.matmul(bank(d, 0)[:, m, :], lora[0:64, d, P * m:P * m + P], wa[0:64, d, :], start=True, stop=True)
                            mm = pe.matmul(bank(d, 2)[:, m, :], lora[64:128, d, P * m:P * m + P], wa[64:128, d, :], start=True, stop=True)
                        mm.then_inc(sem["low_rank_done"], 1)
                        wait(("v_copied", once(i, d)))
                        for m, r in heads():
                            mm = pe.matmul(bank(d, 3)[r, m, :], vs[r, d, m, :], g.ident[r, r], start=True, stop=True)
                        mm.then_inc(sem["v_turned"], 1)
                    for d in range(2):
                        wait(*((n, once(i, d)) for n in ("bt_ready", "kt_ready", "ar_ready", "vtok_ready")))
                        for m, r in heads():
                            two = ar[r, d, m, :, :].rearrange("p s c -> p (s c)")
                            pe.matmul(g.ps[r, 4 * d + 1, P * m:P * m + P], bt[r, d, m, :], two, start=True, stop=True)
                            pe.matmul(bank(d, 3)[r, m, :], ar[r, d, m, 0, :], bt[r, d, m, :], start=True, stop=True)
                            mm = pe.matmul(g.ps[r, 4 * d + 2, P * m:P * m + P], kt[r, d, m, :], two, start=True, stop=True)
                        mm.then_inc(sem["products_done"], 1)
                        for m, r in heads():
                            pe.matmul(bank(d, 0)[r, m, :], bt[r, d, m, :], g.ident[r, r], start=True, stop=True)
                            mm = pe.matmul(bank(d, 0, 1)[r, m, :], kt[r, d, m, :], g.ident[r, r], start=True, stop=True)
                        mm.then_inc(sem["turned"], 1)
                    for l in range(1, 6):
                        for d in range(2):
                            wait((f"level{l}_masked", once(i, d)),
                                 ("x_ready", once(i, d)) if l == 1 else (f"level{l - 1}_added", once(i, d)))
                            for m, r in heads():
                                mm = pe.matmul(bank(d, 1)[r, m, :], lt[r, l % 2, d, m, :], x[r, d, m, :], start=True, stop=True)
                            mm.then_inc(sem[f"level{l}_y"], 1)
                        if l == 1:
                            for d in range(2):
                                wait(("tokens_copied", once(i, d)))
                                for m, r in heads():
                                    pe.matmul(bank(d, 0)[r, m, :], ar[r, d, m, 0, :], state[r, d, m, :], start=True, stop=False)
                                    mm = pe.matmul(bank(d, 0)[r, m, :], lk[r, d, m, 0, :], vtok[r, d, m, :], start=False, stop=True)
                                mm.then_inc(sem["w_done"], 1)
                        for d in range(2):
                            wait((f"level{l}_copied", once(i, d)))
                            for m, r in heads():
                                if l < 5:
                                    pe.matmul(bank(d, 2)[r, m, :], xt[r, d, m, :], ys[r, d, m, :], start=True, stop=True)
                                mm = pe.matmul(bank(d, 3)[r, m, :], ys[r, d, m, :], xt[r, d, m, :], start=True, stop=True)
                            mm.then_inc(sem[f"level{l}_summed"], 1)
                    for d in range(2):
                        wait(("w_copied", once(i, d)), ("level5_added", once(i, d)))
                        for m, r in heads():
                            mm = pe.matmul(bank(d, 1)[r, m, :], xt[r, d, m, :], x[r, d, m, :], start=True, stop=True)
                        mm.then_inc(sem["u_done"], 1)
                    for d in range(2):
                        wait(("u_copied", once(i, d)))
                        for m, r in heads():
                            pe.matmul(bank(d, 3)[r, m, :], bktok[r, d, 0, m, :], u[r, d, m, :], start=True, stop=False)
                            mm = pe.matmul(bank(d, 3)[r, m, :], bktok[r, d, 1, m, :], vtok[r, d, m, :], start=False, stop=True)
                        if y is not None:
                            for m, r in heads():
                                pe.matmul(bank(d, 2)[r, m, :], state[r, d, m, :], ar[r, d, m, 1, :], start=True, stop=False)
                                pe.matmul(bank(d, 2)[r, m, :], u[r, d, m, :], lb[r, d, m, 1, :], start=False, stop=False)
                                mm = pe.matmul(bank(d, 2)[r, m, :], vtok[r, d, m, :], lk[r, d, m, 1, :], start=False, stop=True)
                        mm.then_inc(sem["ds_done"], 1)

            @block.scalar
            def _(act):
                with act.Fori(0, steps) as i:
                    def wait(n, d):
                        act.wait_ge(sem[n], once(i, d))
                    at = [fwd_at(i), bwd_at(i)]
                    for d in range(2):
                        wait("wa_copied", d)
                        act.activation(vs[:, d], mix[:, 8:12, bass.ds(at[d], CHUNK)], ACT.Copy).then_inc(sem["v_copied"], 1)
                    for d in range(2):
                        wait("biased", d)
                        both = wr[:, d].rearrange("p s m c -> p (s m c)")
                        act.activation(both, both, ACT.Tanh, scale=0.5).then_inc(sem["tanhed"], 1)
                        wait("v_turned", d)
                        act.activation(flat(vtok[:, d]), flat(bank(d, 3)), ACT.Copy).then_inc(sem["vtok_ready"], 1)
                    for d in range(2):
                        wait("cum_ready", d)
                        act.activation(flat(down[:, d]), flat(cum[:, d]), ACT.Exp, scale=-1.0)
                        act.activation(flat(up[:, d]), flat(cum[:, d]), ACT.Exp).then_inc(sem["exps_done"], 1)
                        wait("before_ready", d)
                        act.activation(flat(wr[:, d, 0]), flat(wr[:, d, 0]), ACT.Exp).then_inc(sem["upx_done"], 1)
                    for d in range(2):
                        wait("turned", d)
                        act.activation(bktok[:, d].rearrange("p s m c -> p (s m c)"), g.ps[:, 4 * d, :], ACT.Copy).then_inc(sem["tokens_copied"], 1)
                    for l in range(1, 6):
                        for d in range(2):
                            act.wait_ge(sem[f"level{l}_y"], once(i, d))
                            if l > 1:
                                act.wait_ge(sem[f"level{l - 1}_summed"], once(i, d))
                            act.activation(flat(ys[:, d]), flat(bank(d, 1)), ACT.Copy).then_inc(sem[f"level{l}_copied"], 1)
                    for d in range(2):
                        wait("w_done", d)
                        act.wait_ge(sem["level5_y"], once(i, d))
                        act.activation(flat(x[:, d]), flat(bank(d, 0)), ACT.Copy).then_inc(sem["w_copied"], 1)
                    for d in range(2):
                        wait("u_done", d)
                        act.activation(flat(u[:, d]), flat(bank(d, 1)), ACT.Copy).then_inc(sem["u_copied"], 1)

            @block.vector
            def _(dve):
                PER = 12
                dve.wait_ge(sem["tables_in"], 16 * 7)
                if y is None:
                    dve.memset(state.rearrange("p d m c -> p (d m c)"), 0.0)
                else:
                    dve.memset(y[:, 0:4, LAT], 0.0)
                with dve.Fori(0, steps) as i:
                    n = [0]

                    def link(ins):
                        n[0] += 1
                        ins.then_inc(sem["dve_step"], 1)
                        dve.wait_ge(sem["dve_step"], i * PER + n[0])

                    def wait(s, d):
                        dve.wait_ge(sem[s], once(i, d))
                    at = [bass.ds(fwd_at(i), CHUNK), bass.ds(bwd_at(i), CHUNK)]
                    first = g.at["w0"][0]
                    bias = g.params[:, first:first + 16].rearrange("p (s d m) -> p s d m", s=2, d=2)
                    for d in range(2):
                        dve.tensor_copy(wa[:, d, :], mix[:, 12, at[d]]).then_inc(sem["wa_copied"], 1)
                    for d in range(2):
                        wait("low_rank_done", d)
                        dve.tensor_tensor(wr[:, d], g.ps[:, 4 * d:4 * d + 3:2, 0:256].rearrange("p s (m c) -> p s m c", m=4),
                                          bias[:, :, d, :].unsqueeze(3).to_broadcast([P, 2, 4, 64]), ALU.add).then_inc(sem["biased"], 1)
                    for d in range(2):
                        lw, rate = wr[:, d, 0], wr[:, d, 1]
                        wait("tanhed", d)
                        dve.tensor_scalar(flat(rate), flat(rate), 0.5, 0.5, ALU.mult, ALU.add)
                        link(dve.tensor_scalar(flat(lw), flat(lw), -0.5 * DECAY_FLOOR, -0.5 * DECAY_FLOOR, ALU.mult, ALU.add))
                        if d == 0:
                            scan = dve.tensor_tensor_scan(flat(cum[:, d]), restart[:, d, :], flat(lw), 0.0, ALU.mult, ALU.add)
                        else:
                            scan = dve.tensor_tensor_scan(flat(cum[:, d])[:, ::-1], restart[:, d, ::-1], flat(lw)[:, ::-1], 0.0, ALU.mult, ALU.add)
                        scan.then_inc(sem["cum_ready"], 1)
                        wait("cum_ready", d)
                        dve.tensor_tensor(flat(lw), flat(cum[:, d]), flat(lw), ALU.subtract).then_inc(sem["before_ready"], 1)
                        dve.tensor_tensor(bt[:, d], nk[:, :, at[d]], rate, ALU.mult)
                        link(dve.tensor_tensor(kt[:, d], ka[:, :, at[d]], rate, ALU.mult))
                        link(dve.tensor_tensor(kt[:, d], kt[:, d], mix[:, 4:8, at[d]], ALU.add))
                    for d in range(2):
                        wait("exps_done", d)
                        dve.scalar_tensor_tensor(flat(bt[:, d]), flat(bt[:, d]), -1.0, flat(down[:, d]), ALU.mult, ALU.mult).then_inc(sem["bt_ready"], 1)
                        dve.tensor_tensor(flat(kt[:, d]), flat(kt[:, d]), flat(down[:, d]), ALU.mult).then_inc(sem["kt_ready"], 1)
                        dve.tensor_tensor(ar[:, d, :, 1, :], mix[:, 0:4, at[d]], up[:, d], ALU.mult)
                        wait("upx_done", d)
                        dve.tensor_tensor(ar[:, d, :, 0, :], nk[:, :, at[d]], wr[:, d, 0], ALU.mult).then_inc(sem["ar_ready"], 1)
                    for d in range(2):
                        wait("products_done", d)
                        mask = pairs[:, d, :].unsqueeze(1).to_broadcast([P, 4, P])
                        both = eye[:, :].unsqueeze(1).to_broadcast([P, 4, 64])
                        dve.tensor_tensor(lb[:, d].rearrange("p m s c -> p m (s c)"), g.ps[:, 4 * d + 1, :].rearrange("p (m c) -> p m c", c=P), mask,
                                          ALU.mult).then_inc(sem["lb_ready"], 1)
                        wait("lb_ready", d)
                        dve.tensor_tensor(x[:, d], bank(d, 3), levels[:, 0, 1 - d, :].unsqueeze(1).to_broadcast([P, 4, 64]), ALU.mult)
                        link(dve.tensor_tensor(xt[:, d], lb[:, d, :, 0, :], levels[:, 0, d, :].unsqueeze(1).to_broadcast([P, 4, 64]), ALU.mult))
                        dve.tensor_tensor(x[:, d], x[:, d], both, ALU.add)
                        dve.tensor_tensor(xt[:, d], xt[:, d], both, ALU.add)
                        dve.tensor_tensor(lk[:, d].rearrange("p m s c -> p m (s c)"), g.ps[:, 4 * d + 2, :].rearrange("p (m c) -> p m c", c=P), mask,
                                          ALU.mult).then_inc(sem["x_ready"], 1)
                    for l in range(1, 6):
                        for d in range(2):
                            dve.wait_ge(sem[f"level{l}_summed"], once(i, d))
                            if l == 1:
                                wait("x_ready", d)
                            else:
                                dve.wait_ge(sem[f"level{l - 1}_added"], once(i, d))
                            if l < 5:
                                dve.tensor_tensor(flat(x[:, d]), flat(x[:, d]), flat(bank(d, 2)), ALU.add)
                            dve.tensor_tensor(flat(xt[:, d]), flat(xt[:, d]), flat(bank(d, 3)), ALU.add).then_inc(sem[f"level{l}_added"], 1)
                    for d in range(2):
                        wait("ds_done", d)
                        if y is not None:
                            out = y[:, 0:4, bass.ds(([fwd_at(i), bwd_at(i)])[d], CHUNK)]
                            dve.tensor_tensor(out, out, bank(d, 2), ALU.add)
                        link(dve.tensor_tensor(flat(state[:, d]), flat(state[:, d]), flat(bank(d, 3)), ALU.add))
                        last = (CHUNK - 1, 0)[d]
                        link(dve.tensor_tensor(state[:, d], state[:, d], up[:, d, :, last:last + 1].to_broadcast([P, 4, 64]), ALU.mult))
                    assert n[0] == PER, n


def stage_rwkv_out(g, mix, ka, y):
    with Stage(g, "rwkv_out") as st, ExitStack() as mem:
        def sb(n, shape):
            return mem.enter_context(g.nc.sbuf_tensor(f"rwkv_out_{n}", [P] + shape, F32))
        lora, gate_up, blk = sb("lora", [2, 512]), sb("gate_up", [512]), sb("blk", [P])
        half_a0 = sb("half_a0", [8])
        rate, rk, sq, rs, gate = (sb(n, [2, NL]) for n in ("rate", "rk", "sq", "rs", "gate"))
        names = ("tables_in", "half_ready", "gate_in", "rates_done", "tanhed", "rk_ready", "bonus_done", "gate_done", "mean_done",
                 "centred", "squared", "var_done", "rooted", "act_step", "dve_step", "gate_taken")
        (tables_in, half_ready, gate_in, rates_done, tanhed, rk_ready, bonus_done, gate_done, mean_done, centred, squared,
         var_done, rooted, act_step, dve_step, gate_taken) = (st.sem(n) for n in names)
        with g.nc.Block() as block:
            @block.gpsimd
            def _(pool):
                st.begin(pool)

            @block.sync
            def _(sp):
                sp.dma_start(lora[64:128, :, :], g.A["a_lora_up_2"][0].rearrange("d k n -> k d n")).then_inc(tables_in, 16)
                sp.dma_start(gate_up[:, :], g.A["g_lora_up_2"][0]).then_inc(tables_in, 16)
                load_const(g, sp, blk[:, :], "blk64", tables_in)

            @block.tensor
            def _(pe):
                pe.wait_ge(tables_in, 48)
                for m in range(4):
                    if m:
                        pe.wait_ge(tanhed, m)
                    for d in range(2):
                        mm = pe.matmul(g.ps[:, d, :], lora[64:128, d, P * m:P * m + P], mix[64:128, 12, LAT], start=True, stop=True)
                    mm.then_inc(rates_done, 1)
                    if m == 0:
                        pe.wait_ge(gate_in, 1)
                    if m:
                        pe.wait_ge(dve_step, 6 * m)
                        pe.wait_ge(gate_taken, m)
                    pe.matmul(g.ps[:, 3, :], gate_up[:, P * m:P * m + P], mix[:, 13, LAT], start=True, stop=True).then_inc(gate_done, 1)
                    pe.matmul(g.ps[:, 4, :], blk[:, :], y[:, m, LAT], start=True, stop=True).then_inc(mean_done, 1)
                    pe.wait_ge(rk_ready, m + 1)
                    pe.matmul(g.ps[:, 2, :], blk[:, :], rk[:, m % 2, :], start=True, stop=True).then_inc(bonus_done, 1)
                    pe.wait_ge(squared, m + 1)
                    pe.matmul(g.ps[:, 5, :], blk[:, :], sq[:, m % 2, :], start=True, stop=True).then_inc(var_done, 1)

            @block.scalar
            def _(act):
                step = Chain(act, act_step)
                act.activation(mix[:, 13, LAT], mix[:, 13, LAT], ACT.Tanh, scale=0.5).then_inc(act_step, 1)
                step.n = 1
                act.wait_ge(half_ready, 1)
                for m in range(4):
                    act.wait_ge(rates_done, m + 1)
                    if m:
                        act.wait_ge(rk_ready, m)
                    for d in range(2):
                        ins = act.activation(rate[:, d, :], g.ps[:, d, :], ACT.Tanh, scale=0.5, bias=half_a0[:, 4 * d + m:4 * d + m + 1])
                    ins.then_inc(tanhed, 1)
                    act.wait_ge(gate_done, m + 1)
                    act.activation(gate[:, m % 2, :], g.ps[:, 3, :], ACT.Copy).then_inc(gate_taken, 1)
                    act.wait_ge(centred, m + 1)
                    act.activation(sq[:, m % 2, :], y[:, m, LAT], ACT.Square).then_inc(squared, 1)
                    act.wait_ge(var_done, m + 1)
                    step.link(act.activation(rs[:, m % 2, :], g.ps[:, 5, :], ACT.Ln, bias=g.gn_eps, scale=1.0 / 64))
                    act.activation(rs[:, m % 2, :], rs[:, m % 2, :], ACT.Exp, scale=-0.5).then_inc(rooted, 1)

            @block.vector
            def _(dve):
                step = Chain(dve, dve_step)
                dve.tensor_scalar(half_a0[:, :], col(g, "a0"), 0.5, None, ALU.mult).then_inc(half_ready, 1)
                dve.wait_ge(act_step, 1)
                dve.tensor_scalar(mix[:, 13, LAT], mix[:, 13, LAT], 0.5, 0.5, ALU.mult, ALU.add).then_inc(gate_in, 1)
                for m in range(4):
                    dve.wait_ge(tanhed, m + 1)
                    s = rk[:, m % 2, :]
                    step.link(dve.scalar_tensor_tensor(s, rate[:, 0, :], 2.0, rate[:, 1, :], ALU.add, ALU.add))
                    step.link(dve.scalar_tensor_tensor(s, s, 0.5, ka[:, m, LAT], ALU.mult, ALU.mult))
                    step.link(dve.scalar_tensor_tensor(s, mix[:, 4 + m, LAT], 2.0, s, ALU.mult, ALU.add))
                    dve.scalar_tensor_tensor(s, s, col(g, "r_k", m, 1), mix[:, m, LAT], ALU.mult, ALU.mult).then_inc(rk_ready, 1)
                    dve.wait_ge(mean_done, m + 1)
                    dve.scalar_tensor_tensor(y[:, m, LAT], g.ps[:, 4, :], -1.0 / 64, y[:, m, LAT], ALU.mult, ALU.add).then_inc(centred, 1)
                    dve.wait_ge(bonus_done, m + 1)
                    step.done(dve.tensor_tensor(s, g.ps[:, 2, :], mix[:, 8 + m, LAT], ALU.mult))
                    dve.wait_ge(rooted, m + 1)
                    step.link(dve.scalar_tensor_tensor(y[:, m, LAT], y[:, m, LAT], col(g, "gn_g", m, 1), rs[:, m % 2, :], ALU.mult, ALU.mult))
                    dve.wait_ge(gate_taken, m + 1)
                    step.link(dve.scalar_tensor_tensor(y[:, m, LAT], y[:, m, LAT], col(g, "gn_b", m, 1), s, ALU.add, ALU.add))
                    dve.tensor_tensor(y[:, m, LAT], y[:, m, LAT], gate[:, m % 2, :], ALU.mult)


def stage_router(g, a, a_tok, aff, idx):
    with Stage(g, "router") as st, ExitStack() as mem:
        def sb(n, shape, parts=P):
            return mem.enter_context(g.nc.sbuf_tensor(f"router_{n}", [parts] + shape, F32))
        rw = sb("rw", [KD, EXPERTS])
        expd, small = sb("expd", [4, EXPERTS]), sb("small", [3, 4])
        affT, work, best = sb("affT", [NL], 16), sb("work", [2, NL], 16), sb("best", [8], 16)
        idxT, ones_row = sb("idxT", [NL], 16), sb("ones_row", [NL], 16)
        names = ("router_in", "logits_done", "max_ready", "exps_done", "aff_ready", "rows_done", "idx_ready", "idx_turned",
                 "turned", "taken_a", "taken_v", "dve_step", "act_step")
        (router_in, logits_done, max_ready, exps_done, aff_ready, rows_done, idx_ready, idx_turned, turned, taken_a, taken_v,
         dve_step, act_step) = (st.sem(n) for n in names)
        with g.nc.Block() as block:
            @block.gpsimd
            def _(pool):
                st.begin(pool)

            @block.sync
            def _(sp):
                sp.dma_start(rw[:, :, :], g.A["router_w_2"][0].rearrange("(k p) n -> p k n", p=P)).then_inc(router_in, 16)
                g.w.feed(sp, g.first["experts"])

            @block.tensor
            def _(pe):
                pe.wait_ge(router_in, 16)
                for t in range(4):
                    for k in range(KD):
                        mm = pe.matmul(g.ps[:, 0, EXPERTS * t:EXPERTS * t + EXPERTS], a[:, k, NC_ + P * t:NC_ + P * t + P], rw[:, k, :],
                                       start=(k == 0), stop=(k == KD - 1))
                mm.then_inc(logits_done, 1)
                for n in range(8):
                    t, half = n // 2, n % 2
                    if n >= 4:
                        pe.wait_ge(taken_a, n - 3)
                    for q in range(4):
                        mm = pe.transpose(g.ps[:, 2 + n % 4, P * q:P * q + P], a[:, 4 * half + q, NC_ + P * t:NC_ + P * t + P], g.ident)
                    mm.then_inc(turned, 1)
                pe.wait_ge(aff_ready, 1)
                for t in range(4):
                    mm = pe.transpose(g.ps[0:16, 1, P * t:P * t + P], aff[:, t, :], g.ident)
                mm.then_inc(rows_done, 1)
                pe.wait_ge(idx_ready, 1)
                for t in range(4):
                    mm = pe.transpose(g.ps[:, 6, 16 * t:16 * t + 16], idxT[:, P * t:P * t + P], g.ident[0:16, 0:16])
                mm.then_inc(idx_turned, 1)

            @block.scalar
            def _(act):
                act.wait_ge(max_ready, 1)
                for t in range(4):
                    ins = act.activation(expd[:, t, :], g.ps[:, 0, EXPERTS * t:EXPERTS * t + EXPERTS], ACT.Exp,
                                         bias=small[:, 0, t:t + 1], accum_out=small[:, 1, t:t + 1])
                ins.then_inc(exps_done, 1)
                for n in range(8):
                    act.wait_ge(turned, n + 1)
                    act.activation(a_tok[:, n // 2, 512 * (n % 2):512 * (n % 2) + 512], g.ps[:, 2 + n % 4, :], ACT.Copy).then_inc(taken_a, 1)

            @block.vector
            def _(dve):
                step = Chain(dve, dve_step)
                dve.memset(ones_row[:, :], 1.0)
                dve.wait_ge(logits_done, 1)
                logits = g.ps[:, 0, 0:4 * EXPERTS].rearrange("p (t e) -> p t e", e=EXPERTS)
                dve.tensor_reduce(small[:, 0, :], logits, AX.X, ALU.max, negate=True).then_inc(max_ready, 1)
                dve.wait_ge(exps_done, 1)
                step.link(dve.reciprocal(small[:, 2, :], small[:, 1, :]))
                dve.tensor_tensor(aff[:, :, :], expd[:, :, :], small[:, 2, :].unsqueeze(2).to_broadcast([P, 4, EXPERTS]), ALU.mult).then_inc(aff_ready, 1)
                dve.wait_ge(rows_done, 1)
                step.link(dve.tensor_copy(work[:, 0, :], g.ps[0:16, 1, :]))
                for n in range(CAP // 8):
                    step.link(dve.max(best[:, :], work[:, n % 2, :]))
                    step.link(dve.match_replace(work[:, (n + 1) % 2, :], best[:, :], work[:, n % 2, :], -1.0))
                chosen, count = work[:, 0, :], work[:, 1, :]
                step.link(dve.tensor_scalar(chosen, chosen, 0.0, None, ALU.is_lt))
                step.link(dve.tensor_tensor_scan(count, ones_row[:, :], chosen, 0.0, ALU.mult, ALU.add))
                step.link(dve.tensor_tensor(count, count, chosen, ALU.mult))
                dve.tensor_scalar(idxT[:, :], count, -1.0, None, ALU.add).then_inc(idx_ready, 1)
                dve.wait_ge(idx_turned, 1)
                dve.tensor_copy(idx[:, :, :], g.ps[:, 6, 0:64].rearrange("p (t e) -> p t e", e=EXPERTS))


def stage_experts(g, a_tok, aff, idx, made, pickT):
    w, n0 = g.w, g.first["experts"]
    base = w.before[n0]
    with Stage(g, "experts") as st, ExitStack() as mem:
        def sb(n, shape, dtype=F32, parts=P):
            return mem.enter_context(g.nc.sbuf_tensor(f"experts_{n}", [parts] + shape, dtype))
        iota = sb("iota", [CAP])
        pick = sb("pick", [4, 2, CAP])
        own = sb("own", [4, 2])
        val = sb("val", [2], parts=CAP)
        xs = sb("xs", [2, KD, P], F32R)
        hs = sb("hs", [D], parts=CAP)
        hT = sb("hT", [2, KD, CAP], F32R)
        PARTS = 4
        hi, lo = (sb(n, [PARTS, SLOT], F32R) for n in ("hi", "lo"))
        names = ("table_in", "pick_ready", "gathered", "xs_hi_ready", "xs_ready", "pick_turned", "pickT_ready", "valued",
                 "silu_ready", "hs_ready", "hs_turned", "hT_hi_ready", "hT_ready", "out_taken", "hi_made", "lo_made_v", "lo_made_p")
        (table_in, pick_ready, gathered, xs_hi_ready, xs_ready, pick_turned, pickT_ready, valued, silu_ready, hs_ready,
         hs_turned, hT_hi_ready, hT_ready, out_taken, hi_made, lo_made_v, lo_made_p) = (st.sem(n) for n in names)
        TURNS = EXPERTS // 2

        def at(i, r, per, more):
            return i * (2 * per) + (per * r + more)

        def turns(engine, body):
            with engine.Fori(0, TURNS - 1) as i:
                for r in range(2):
                    body(i, r, True)
            for r in range(2):
                body(TURNS - 1, r, False)

        def make_hi(act, i, e):
            n = n0 + e
            w.arrived(act, n, i * (16 * 24 // RING))
            act.wait_ge(w.product_done, i * 24 + (base + e - PARTS + 1))
            act.activation(hi[:, e % PARTS, :], w.ring[:, n % RING, :], ACT.Copy).then_inc(hi_made, 1)

        def make_lo(engine, i, e):
            engine.wait_ge(hi_made, i * 24 + (e + 1))
            engine.tensor_tensor(lo[:, e % PARTS, :], w.ring[:, (n0 + e) % RING, :], hi[:, e % PARTS, :].bitcast(F32),
                                 ALU.subtract).then_inc(lo_made_p if e % 4 == 3 else lo_made_v, 1)

        def await_split(pe, i, e):
            if e % 4 == 3:
                pe.wait_ge(lo_made_p, i * 6 + (e // 4 + 1))
            else:
                pe.wait_ge(lo_made_v, i * 18 + (e // 4 * 3 + e % 4 + 1))

        def weight(e, part):
            return (hi, lo)[part][:, e % PARTS, :].rearrange("p (k n) -> p k n", k=KD)

        with g.nc.Block() as block:
            @block.sync
            def _(sp):
                load_const(g, sp, iota[:, :], "iota64", table_in)
                for n in range(w.issued, len(w.entries)):
                    e = n - RING - n0
                    if e < 0:
                        sp.wait_ge(w.product_done, w.freed[n - RING])
                    elif e % 4 == 3:
                        sp.wait_ge(lo_made_p, e // 4 + 1)
                    else:
                        sp.wait_ge(lo_made_v, e // 4 * 3 + e % 4 + 1)
                    w.load(sp, n)

            @block.gpsimd
            def _(pool):
                st.begin(pool)

                def body(i, r, more):
                    for e in (3, 7, 11):
                        make_lo(pool, i, 12 * r + e)
                turns(pool, body)

            @block.tensor
            def _(pe):
                def gather(i):
                    pe.wait_ge(pick_ready, i * 1 + 1)
                    for k in range(KD):
                        for t in range(4):
                            mm = pe.matmul(g.ps[:, k // 4, P * (k % 4):P * (k % 4) + P], a_tok[:, t, P * k:P * k + P],
                                           pick[:, t, :, :].rearrange("p r c -> p (r c)"), start=(t == 0), stop=(t == 3))
                    mm.then_inc(gathered, 1)

                def product(i, r, e, out, source):
                    await_split(pe, i, 12 * r + e)
                    for k in range(KD):
                        for wt, sr in PRODUCTS:
                            mm = pe.matmul(out, source(sr, k), weight(12 * r + e, wt)[:, k, :],
                                           start=(k == 0 and wt + sr == 0), stop=(k == KD - 1 and wt == 1))
                    mm.then_inc(w.product_done, 1)

                def body(i, r, more):
                    if r == 0:
                        pe.wait_ge(xs_ready, i + 1)
                    for e in range(8):
                        bank, c = 2 + e // 2, e % 2
                        product(i, r, e, g.ps[0:CAP, bank, 256 * c:256 * c + 256],
                                lambda sr, k: xs[:, sr, k, 64 * r:64 * r + 64])
                    if r == 0:
                        for t in range(4):
                            pair = pick[:, t, :, :].rearrange("p r c -> p (r c)")
                            mm = pe.matmul(g.ps[:, 0, P * t:P * t + P], pair, g.ident, start=True, stop=True)
                        mm.then_inc(pick_turned, 1)
                        for q in range(2):
                            for t in range(4):
                                mm = pe.matmul(g.ps[0:CAP, 1, q:q + 1], pick[:, t, q, :], own[:, t, q:q + 1], start=(t == 0), stop=(t == 3))
                        mm.then_inc(valued, 1)
                    elif more:
                        pe.wait_ge(pickT_ready, i + 1)
                        gather(i + 1)
                    pe.wait_ge(hs_ready, at(i, r, 2, 2))
                    for k in range(KD):
                        mm = pe.matmul(g.ps[:, 2, CAP * k:CAP * k + CAP], hs[:, P * k:P * k + P], g.ident[0:CAP, 0:CAP], start=True, stop=True)
                    mm.then_inc(hs_turned, 1)
                    pe.wait_ge(hT_ready, at(i, r, 1, 1))
                    for c in range(4):
                        product(i, r, 8 + c, g.ps[0:CAP, 6 + c // 2, 256 * (c % 2):256 * (c % 2) + 256],
                                lambda sr, k: hT[:, sr, k, :])

                gather(0)
                turns(pe, body)

            @block.scalar
            def _(act):
                def take_xs(i):
                    act.wait_ge(gathered, i + 1)
                    for half in range(2):
                        ins = act.activation(xs[:, 0, 4 * half:4 * half + 4, :].rearrange("p k c -> p (k c)"),
                                             g.ps[:, half, :], ACT.Copy)
                    ins.then_inc(xs_hi_ready, 1)

                def silu(i, r, half):
                    act.wait_ge(w.product_done, at(i, r, 12, base + 4 * half + 2))
                    act.activation(hs[:, 512 * half:512 * half + 512], g.ps[0:CAP, 2 + 2 * half, :], ACT.Silu).then_inc(silu_ready, 1)

                def body(i, r, more):
                    b = slice(64 * r, 64 * r + 64)
                    make_hi(act, i, 12 * r + 3)
                    silu(i, r, 0)
                    for e in range(4, 8):
                        make_hi(act, i, 12 * r + e)
                    silu(i, r, 1)
                    for e in range(8, 12):
                        make_hi(act, i, 12 * r + e)
                    act.wait_ge(hs_turned, at(i, r, 1, 1))
                    act.activation(hT[:, 0, :, :].rearrange("p k c -> p (k c)"), g.ps[:, 2, :], ACT.Copy).then_inc(hT_hi_ready, 1)
                    if more and r:
                        take_xs(i + 1)
                    for e in (12, 13, 14) if more or r == 0 else ():
                        make_hi(act, i, 12 * r + e)
                    act.wait_ge(w.product_done, at(i, r, 12, base + 12))
                    act.wait_ge(pickT_ready, i + 1)
                    flat = made[:, :, :].rearrange("p e n -> p (e n)")
                    for c in range(2):
                        ins = act.activation(flat[b, bass.ds(i * D + 512 * c, 512)], g.ps[0:CAP, 6 + c, :], ACT.Copy, scale=val[:, r:r + 1])
                    ins.then_inc(out_taken, 1)

                take_xs(0)
                for e in (0, 1, 2):
                    make_hi(act, 0, e)
                turns(act, body)

            @block.vector
            def _(dve):
                dve.wait_ge(table_in, 16)

                def choose(i):
                    dve.tensor_copy(own[:, :, :], aff[:, :, bass.ds(i * 2, 2)])
                    fl = idx[:, :, :].rearrange("p t e -> p (t e)")
                    for t in range(4):
                        for r in range(2):
                            ins = dve.tensor_scalar(pick[:, t, r, :], iota[:, :], fl[:, bass.ds(i * 2 + (EXPERTS * t + r), 1)], None, ALU.is_equal)
                    ins.then_inc(pick_ready, 1)

                def take_xs(i):
                    dve.wait_ge(xs_hi_ready, i + 1)
                    for half in range(2):
                        part = xs[:, :, 4 * half:4 * half + 4, :]
                        ins = dve.tensor_tensor(part[:, 1].rearrange("p k c -> p (k c)"), g.ps[:, half, :],
                                                part[:, 0].rearrange("p k c -> p (k c)").bitcast(F32), ALU.subtract)
                    ins.then_inc(xs_ready, 1)

                def hidden(i, r, half):
                    dve.wait_ge(w.product_done, at(i, r, 12, base + 4 * half + 4))
                    dve.wait_ge(silu_ready, at(i, r, 2, half + 1))
                    own = hs[:, 512 * half:512 * half + 512]
                    dve.tensor_tensor(own, own, g.ps[0:CAP, 3 + 2 * half, :], ALU.mult).then_inc(hs_ready, 1)

                def body(i, r, more):
                    for e in (0, 1, 2, 4, 5, 6):
                        make_lo(dve, i, 12 * r + e)
                    hidden(i, r, 0)
                    make_lo(dve, i, 12 * r + 8)
                    hidden(i, r, 1)
                    make_lo(dve, i, 12 * r + 9)
                    make_lo(dve, i, 12 * r + 10)
                    dve.wait_ge(hT_hi_ready, at(i, r, 1, 1))
                    dve.tensor_tensor(hT[:, 1, :, :].rearrange("p k c -> p (k c)"), g.ps[:, 2, :],
                                      hT[:, 0, :, :].rearrange("p k c -> p (k c)").bitcast(F32), ALU.subtract).then_inc(hT_ready, 1)
                    if r == 0:
                        dve.wait_ge(pick_turned, i + 1)
                        pf = pickT[:, :, :].rearrange("p e n -> p (e n)")
                        dve.tensor_copy(pf[:, bass.ds(i * NL, NL)], g.ps[:, 0, :])
                        dve.wait_ge(valued, i + 1)
                        dve.tensor_copy(val[:, :], g.ps[0:CAP, 1, 0:2]).then_inc(pickT_ready, 1)
                    if more and r:
                        take_xs(i + 1)
                    if more and r == 0:
                        choose(i + 1)

                choose(0)
                take_xs(0)
                turns(dve, body)


def stage_scatter(g, made, pickT):
    with Stage(g, "scatter") as st:
        summed, added = st.sem("summed"), st.sem("added")
        pairs = EXPERTS // 2
        with g.nc.Block() as block:
            @block.gpsimd
            def _(pool):
                st.begin(pool)

            @block.tensor
            def _(pe):
                for m in range(KD):
                    for e in range(pairs):
                        mm = pe.matmul(g.ps[:, m, :], made[:, e, P * m:P * m + P], pickT[:, e, :], start=(e == 0), stop=(e == pairs - 1))
                    mm.then_inc(summed, 1)

            @block.vector
            def _(dve):
                for m in range(KD):
                    dve.wait_ge(summed, m + 1)
                    dve.scalar_tensor_tensor(g.h[:, m, LAT], g.ps[:, m, :], g.mod[:, 5 * KD + m, 0:1], g.h[:, m, LAT],
                                             ALU.mult, ALU.add).then_inc(added, 1)


def third_layer(g, A):
    stage_context2(g, A)
    stage_ada(g, "ada2", "b_ada2", 1, gains=("norm1_g", "norm2_g"))
    with ExitStack() as mem:
        def sb(name, shape):
            return mem.enter_context(g.nc.sbuf_tensor(name, [P] + shape, F32))
        a = sb("a2", [KD, T])
        mix = sb("mix", [NR, T])
        stage_norm(g, "norm2a", g.h, a, KD, norm_parts(g, 0, True))
        with ExitStack() as inner:
            raw = inner.enter_context(g.nc.sbuf_tensor("raw2", [P, NR, T], F32))
            cv = inner.enter_context(g.nc.sbuf_tensor("cv", [P, 12, NL], F32))
            stage_in2(g, a, raw, cv)
            stage_shift(g, raw, mix, cv, a)
        nk, ka, state = sb("nk", [4, T]), sb("ka", [4, T]), sb("state", [2, 4, 64])
        stage_keys(g, mix, nk, ka)
        nctx, nlat = NC_ // CHUNK, NL // CHUNK
        stage_recurrence(g, "ctx_rec", nctx, lambda i: i * CHUNK, lambda i: i * (-CHUNK) + (NC_ - CHUNK), mix, nk, ka, state, None)
        stage_recurrence(g, "lat_rec", nlat, lambda i: i * CHUNK + NC_, lambda i: i * (-CHUNK) + (T - CHUNK), mix, nk, ka, state, a)
        stage_rwkv_out(g, mix, ka, a)
        stage_out(g, "out2", a, False)
    with ExitStack() as mem:
        def sb(name, shape):
            return mem.enter_context(g.nc.sbuf_tensor(name, [P] + shape, F32))
        a_tok, aff, idx = sb("a_tok", [4, D]), sb("aff", [4, EXPERTS]), sb("idx", [4, EXPERTS])
        made, pickT = sb("made", [EXPERTS // 2, D]), sb("pickT", [EXPERTS // 2, NL])
        with ExitStack() as inner:
            a = inner.enter_context(g.nc.sbuf_tensor("a2f", [P, KD, T], F32))
            stage_norm(g, "norm2b", g.h, a, KD, norm_parts(g, 3, False))
            stage_router(g, a, a_tok, aff, idx)
        stage_experts(g, a_tok, aff, idx, made, pickT)
        stage_scatter(g, made, pickT)
    stage_norm(g, "norm2f", g.h, g.h, KD, [(LAT, lambda k: col(g, "final_g", k, 1), None)], store=A["out"])


def program(nc, A, at, cat):
    with ExitStack() as keep:
        g = Prog(nc)
        g.keep, g.A, g.at, g.cat = keep, A, at, cat
        vector_memory(g, A)
        g.first = plan_weights(g, A)
        stage_start(g, A)
        first_layer(g)
        second_layer(g)
        third_layer(g, A)


_WEIGHTS = ["w_ada", "w_ffn_gate", "w_ffn_up", "w_ffn_down", "ret_ssd_w_in", "ret_ssd_w_out", "mla_w_in",
            "mla_w_uq", "mla_w_ukv", "mla_w_out", "ada_w_2", "w_in_2", "w_lora_up_2", "a_lora_up_2",
            "g_lora_up_2", "w_out_2", "router_w_2", "exp_w_gate_2", "exp_w_up_2", "exp_w_down_2"]


def lay_out(inputs):
    x = {k: np.asarray(v) for k, v in inputs.items()}
    params, at = lay_params(x)
    consts, cat = constants()
    arrays = {k: np.ascontiguousarray(x[k]) for k in _WEIGHTS}
    arrays["params"], arrays["consts"] = params, consts
    for name, src in (("xT", "x"), ("ctxT", "ctx"), ("ctx2T", "ctx_2")):
        arrays[name] = np.ascontiguousarray(x[src][0].T)
    return arrays, at, cat


def kernel(**inputs):
    import concourse.bacc as bacc
    from concourse.bass_utils import run_bass_kernel_spmd

    arrays, at, cat = lay_out(inputs)
    nc = bacc.Bacc("TRN2", target_bir_lowering=False, num_devices=1)
    A = {k: nc.dram_tensor(f"in_{k}", v.shape, F32, kind="ExternalInput").ap() for k, v in arrays.items()}
    A["out"] = nc.dram_tensor("out", (D, NL), F32, kind="ExternalOutput").ap()
    program(nc, A, at, cat)
    r = run_bass_kernel_spmd(nc, [{f"in_{k}": v for k, v in arrays.items()}], core_ids=[0])
    return np.ascontiguousarray(np.asarray(r.results[0]["out"]).T)[None]
```
